# Optimizing a Trainium2 kernel written in Bass

```python
import jax, jax.numpy as jnp
from jax import lax
import numpy as np

D_MODEL = 1024
BATCH = 1
SEQ = 256
DEPTH = 2

HEAD_DIM = 64
N_BRANCH = 4
BRANCH_WIDTH = D_MODEL // N_BRANCH
N_META = 16
BLOCK = 128
N_FRONT_PAD = BLOCK - N_META
SB_HEADS = BRANCH_WIDTH // HEAD_DIM
GLA_HEADS = BRANCH_WIDTH // HEAD_DIM
GLA_DK = HEAD_DIM // 2
GLA_DV = HEAD_DIM
GLA_LOW_RANK = 16
GLA_GATE_NORMALIZER = 16.0
ML_HEADS = BRANCH_WIDTH // HEAD_DIM
ML_DH = HEAD_DIM
CONV_WIDTH = 4
RET_HEADS = BRANCH_WIDTH // HEAD_DIM
RET_DH = HEAD_DIM
D_FF = -(-8 * D_MODEL // (3 * 256)) * 256
ROPE_BASE = 10000.0
NORM_EPS = 1e-6

IN_SPLIT_SIZES = (
    BRANCH_WIDTH, BRANCH_WIDTH, BRANCH_WIDTH,
    GLA_HEADS * GLA_DK, GLA_HEADS * GLA_DK, GLA_HEADS * GLA_DV,
    GLA_HEADS * GLA_DV, GLA_LOW_RANK,
    2 * BRANCH_WIDTH, BRANCH_WIDTH, ML_HEADS, ML_HEADS, BRANCH_WIDTH,
    BRANCH_WIDTH, BRANCH_WIDTH, BRANCH_WIDTH, BRANCH_WIDTH,
    N_BRANCH * D_MODEL,
)
IN_WIDTH = sum(IN_SPLIT_SIZES)

kernel_name = "hybrid_sb_gla_mlstm_retnet_block"

F32 = jnp.float32

def _rmsnorm(x, g):
    xf = x.astype(F32)
    y = xf * lax.rsqrt(jnp.mean(xf * xf, axis=-1, keepdims=True) + NORM_EPS)
    return (y * g.astype(F32)).astype(x.dtype)

def _head_rmsnorm(y, g, n_heads):
    b, l, w = y.shape
    yh = y.reshape(b, l, n_heads, w // n_heads)
    yh = yh * lax.rsqrt(jnp.mean(yh * yh, axis=-1, keepdims=True) + NORM_EPS)
    return yh.reshape(b, l, w) * g.astype(F32)

def _to_chunks(t, n_heads):
    b, l, w = t.shape
    return t.reshape(b, l // BLOCK, BLOCK, n_heads, w // n_heads).transpose(0, 3, 1, 2, 4)

def _gate_chunks(t):
    b, l, h = t.shape
    return t.reshape(b, l // BLOCK, BLOCK, h).transpose(0, 3, 1, 2)

def _from_chunks(t):
    b, h, nc, c, d = t.shape
    return t.transpose(0, 2, 3, 1, 4).reshape(b, nc * c, h * d)

def _causal_tril():
    return jnp.tril(jnp.ones((BLOCK, BLOCK), dtype=bool))

def _scan_chunk_states(decay, local):
    decay = jnp.broadcast_to(decay, local.shape)

    def step(state, inp):
        d, u = inp
        return d * state + u, state

    _, prev = lax.scan(step, jnp.zeros_like(local[:, :, 0]),
                       (jnp.moveaxis(decay, 2, 0), jnp.moveaxis(local, 2, 0)))
    return jnp.moveaxis(prev, 0, 2)

def _causal_conv(x, w):
    ch = x.shape[-1]
    return lax.conv_general_dilated(x, w[:, None, :].astype(x.dtype), window_strides=(1,),
                                    padding=[(CONV_WIDTH - 1, 0)],
                                    dimension_numbers=('NWC', 'WIO', 'NWC'),
                                    feature_group_count=ch)

def _rotary(x, positions, n_heads):
    b, l, w = x.shape
    d = w // n_heads
    half = d // 2
    inv_freq = ROPE_BASE ** (-jnp.arange(half, dtype=F32) / half)
    ang = positions.astype(F32)[:, None] * inv_freq[None, :]
    cos, sin = jnp.cos(ang)[:, None, :], jnp.sin(ang)[:, None, :]
    xh = x.reshape(b, l, n_heads, d)
    x1, x2 = xh[..., :half], xh[..., half:]
    return jnp.concatenate([x1 * cos - x2 * sin, x1 * sin + x2 * cos], axis=-1).reshape(b, l, w)

def _stick_breaking(q, k, v, key_valid):
    b, l, w = q.shape
    nb = l // BLOCK
    qh = q.reshape(b, nb, BLOCK, SB_HEADS, HEAD_DIM).transpose(1, 0, 3, 2, 4)
    kh = k.reshape(b, l, SB_HEADS, HEAD_DIM).transpose(0, 2, 1, 3)
    vh = v.reshape(b, l, SB_HEADS, HEAD_DIM).transpose(0, 2, 1, 3)
    key_pos = jnp.arange(l)
    scale = HEAD_DIM ** -0.5

    def one_block(args):
        q_blk, blk = args
        q_pos = blk * BLOCK + jnp.arange(BLOCK)
        z = jnp.einsum('bhqd,bhkd->bhqk', q_blk, kh) * scale
        mask = (key_pos[None, :] < q_pos[:, None]) & key_valid[None, :]
        log_beta = jnp.where(mask, jax.nn.log_sigmoid(z), -jnp.inf)
        log_keep = jnp.where(mask, jax.nn.log_sigmoid(-z), 0.0)
        later = lax.cumsum(log_keep, axis=3, reverse=True) - log_keep
        a = jnp.exp(log_beta + later)
        return jnp.einsum('bhqk,bhkd->bhqd', a, vh)

    out = lax.map(one_block, (qh, jnp.arange(nb)))
    return out.transpose(1, 0, 3, 2, 4).reshape(b, l, w)

def _gla(q, k, v, r, code, w_gate_up, b_gate, norm_g):
    log_a = jax.nn.log_sigmoid(code @ w_gate_up.astype(F32) + b_gate.astype(F32)) / GLA_GATE_NORMALIZER
    qc = _to_chunks(q, GLA_HEADS) * GLA_DK ** -0.5
    kc = _to_chunks(k, GLA_HEADS)
    vc = _to_chunks(v, GLA_HEADS)
    cum = jnp.cumsum(_to_chunks(log_a, GLA_HEADS), axis=3)
    cum_last = cum[:, :, :, -1:, :]
    q_dec = qc * jnp.exp(cum)
    k_dec = kc * jnp.exp(-cum)
    scores = jnp.where(_causal_tril(), jnp.einsum('bhnqd,bhnkd->bhnqk', q_dec, k_dec), 0.0)
    intra = jnp.einsum('bhnqk,bhnke->bhnqe', scores, vc)
    local = jnp.einsum('bhnkd,bhnke->bhnde', kc * jnp.exp(cum_last - cum), vc)
    states = _scan_chunk_states(jnp.swapaxes(jnp.exp(cum_last), -1, -2), local)
    inter = jnp.einsum('bhnqd,bhnde->bhnqe', q_dec, states)
    o = _from_chunks(intra + inter)
    return _head_rmsnorm(o, norm_g, GLA_HEADS) * jax.nn.silu(r)

def _mlstm(qk, v, i_pre, f_pre, o_pre, conv_w, b_i, b_f, norm_g):
    qk = jax.nn.silu(_causal_conv(qk, conv_w))
    q, k = jnp.split(qk, 2, axis=-1)
    qc = _to_chunks(q, ML_HEADS)
    kc = _to_chunks(k, ML_HEADS) * ML_DH ** -0.5
    vc = _to_chunks(v, ML_HEADS)
    log_i = _gate_chunks(i_pre + b_i.astype(F32))
    log_f = jax.nn.log_sigmoid(_gate_chunks(f_pre + b_f.astype(F32)))
    cum_f = jnp.cumsum(log_f, axis=-1)
    cum_last = cum_f[..., -1]
    w_end = cum_last[..., None] - cum_f + log_i
    a_end = jnp.max(w_end, axis=-1)
    p_end = jnp.exp(w_end - a_end[..., None])
    c_loc = jnp.einsum('bhnk,bhnkd,bhnke->bhnde', p_end, kc, vc)
    n_loc = jnp.einsum('bhnk,bhnkd->bhnd', p_end, kc)

    def step(carry, inp):
        c_s, n_s, m_s = carry
        f_l, a_l, c_l, n_l = inp
        m_new = jnp.maximum(f_l + m_s, a_l)
        s_prev = jnp.exp(f_l + m_s - m_new)
        s_loc = jnp.exp(a_l - m_new)
        c_new = s_prev[..., None, None] * c_s + s_loc[..., None, None] * c_l
        n_new = s_prev[..., None] * n_s + s_loc[..., None] * n_l
        return (c_new, n_new, m_new), (c_s, n_s, m_s)

    b, h, nc, c, d = qc.shape
    init = (jnp.zeros((b, h, d, d), F32), jnp.zeros((b, h, d), F32), jnp.zeros((b, h), F32))
    xs = tuple(jnp.moveaxis(t, 2, 0) for t in (cum_last, a_end, c_loc, n_loc))
    _, (c_prev, n_prev, m_prev) = lax.scan(step, init, xs)
    c_prev, n_prev, m_prev = (jnp.moveaxis(t, 0, 2) for t in (c_prev, n_prev, m_prev))
    inter_log = cum_f + m_prev[..., None]
    intra_log = jnp.where(_causal_tril(),
                          cum_f[..., :, None] - cum_f[..., None, :] + log_i[..., None, :], -jnp.inf)
    m_t = jnp.maximum(inter_log, jnp.max(intra_log, axis=-1))
    w_intra = jnp.exp(intra_log - m_t[..., None])
    w_inter = jnp.exp(inter_log - m_t)
    s = jnp.einsum('bhnqd,bhnkd->bhnqk', qc, kc) * w_intra
    num = jnp.einsum('bhnqk,bhnke->bhnqe', s, vc) + w_inter[..., None] * jnp.einsum('bhnqd,bhnde->bhnqe', qc, c_prev)
    den = jnp.sum(s, axis=-1) + w_inter * jnp.einsum('bhnqd,bhnd->bhnq', qc, n_prev)
    h_cell = num / jnp.maximum(jnp.abs(den), jnp.exp(-m_t))[..., None]
    return jax.nn.sigmoid(o_pre) * _head_rmsnorm(_from_chunks(h_cell), norm_g, ML_HEADS)

def _retention(q, k, v, g, positions, norm_g):
    log_gamma = jnp.log1p(-jnp.exp2(-5.0 - jnp.arange(RET_HEADS, dtype=F32)))
    qc = _to_chunks(_rotary(q, positions, RET_HEADS), RET_HEADS)
    kc = _to_chunks(_rotary(k, positions, RET_HEADS), RET_HEADS) * RET_DH ** -0.5
    vc = _to_chunks(v, RET_HEADS)
    pos = jnp.arange(BLOCK, dtype=F32)
    diff = jnp.maximum(pos[:, None] - pos[None, :], 0.0)
    decay_intra = jnp.where(_causal_tril(), jnp.exp(log_gamma[:, None, None] * diff), 0.0)
    scores = jnp.einsum('bhnqd,bhnkd->bhnqk', qc, kc) * decay_intra[None, :, None]
    intra = jnp.einsum('bhnqk,bhnke->bhnqe', scores, vc)
    q_decay = jnp.exp(log_gamma[:, None] * (pos + 1.0))
    k_decay = jnp.exp(log_gamma[:, None] * (BLOCK - 1.0 - pos))
    local = jnp.einsum('bhnkd,bhnke->bhnde', kc * k_decay[None, :, None, :, None], vc)
    states = _scan_chunk_states(jnp.exp(log_gamma * BLOCK)[None, :, None, None, None], local)
    inter = jnp.einsum('bhnqd,bhnde->bhnqe', qc * q_decay[None, :, None, :, None], states)
    y = _from_chunks(intra + inter)
    return jax.nn.silu(g) * _head_rmsnorm(y, norm_g, RET_HEADS)

def _hybrid_layer(h, valid, positions, g_mix_pre, g_mix_post, g_ffn_pre, g_ffn_post, w_in,
                  gla_w_gate_up, gla_b_gate, gla_norm, ml_conv, ml_b_i, ml_b_f, ml_norm, ret_norm,
                  w_branch, b_merge, w_out, ffn_w_gate, ffn_w_up, ffn_w_down):
    b, l, _ = h.shape
    hn = _rmsnorm(h, g_mix_pre) * valid[None, :, None].astype(h.dtype)
    u = (hn @ w_in).astype(F32)
    split_points = [int(p) for p in np.cumsum(IN_SPLIT_SIZES)[:-1]]
    (sb_q, sb_k, sb_v, gla_q, gla_k, gla_v, gla_r, gla_code,
     ml_qk, ml_v, ml_i, ml_f, ml_o, ret_q, ret_k, ret_v, ret_g, merge_logits) = jnp.split(u, split_points, axis=-1)
    y_sb = _stick_breaking(sb_q, sb_k, sb_v, valid)
    y_gla = _gla(gla_q, gla_k, gla_v, gla_r, gla_code, gla_w_gate_up, gla_b_gate, gla_norm)
    y_ml = _mlstm(ml_qk, ml_v, ml_i, ml_f, ml_o, ml_conv, ml_b_i, ml_b_f, ml_norm)
    y_ret = _retention(ret_q, ret_k, ret_v, ret_g, positions, ret_norm)
    gates = jax.nn.sigmoid(merge_logits.reshape(b, l, N_BRANCH, D_MODEL) + b_merge.astype(F32))
    branches = (y_sb, y_gla, y_ml, y_ret)
    merged = gates[:, :, 0] * (branches[0] @ w_branch[0].astype(F32))
    for n in range(1, N_BRANCH):
        merged = merged + gates[:, :, n] * (branches[n] @ w_branch[n].astype(F32))
    mix_out = (merged @ w_out.astype(F32)).astype(h.dtype)
    h = h + _rmsnorm(mix_out, g_mix_post)
    f = _rmsnorm(h, g_ffn_pre)
    ffn_out = (jax.nn.silu(f @ ffn_w_gate) * (f @ ffn_w_up)) @ ffn_w_down
    return h + _rmsnorm(ffn_out.astype(h.dtype), g_ffn_post)

def setup_inputs(seed: int = 0) -> dict:
    key = jax.random.key(seed)
    ks = jax.random.split(key, 24)

    def nrm(k, shape, scale):
        return jax.random.normal(k, shape, F32) * scale

    def gain(k, shape):
        return 1.0 + 0.02 * jax.random.normal(k, shape, F32)

    return {
        'x': nrm(ks[0], (BATCH, SEQ, D_MODEL), 1.0),
        'meta_tokens': nrm(ks[1], (N_META, D_MODEL), 1.0),
        'norm_mix_pre': gain(ks[2], (DEPTH, D_MODEL)),
        'norm_mix_post': gain(ks[3], (DEPTH, D_MODEL)),
        'norm_ffn_pre': gain(ks[4], (DEPTH, D_MODEL)),
        'norm_ffn_post': gain(ks[5], (DEPTH, D_MODEL)),
        'w_in': nrm(ks[6], (DEPTH, D_MODEL, IN_WIDTH), D_MODEL ** -0.5),
        'gla_w_gate_up': nrm(ks[7], (DEPTH, GLA_LOW_RANK, GLA_HEADS * GLA_DK), GLA_LOW_RANK ** -0.5),
        'gla_b_gate': nrm(ks[8], (DEPTH, GLA_HEADS * GLA_DK), 0.1),
        'gla_norm': gain(ks[9], (DEPTH, GLA_HEADS * GLA_DV)),
        'ml_conv': nrm(ks[10], (DEPTH, CONV_WIDTH, 2 * BRANCH_WIDTH), CONV_WIDTH ** -0.5),
        'ml_b_i': nrm(ks[11], (DEPTH, ML_HEADS), 0.1),
        'ml_b_f': jnp.linspace(3.0, 6.0, ML_HEADS, dtype=F32)[None, :] + nrm(ks[12], (DEPTH, ML_HEADS), 0.1),
        'ml_norm': gain(ks[13], (DEPTH, BRANCH_WIDTH)),
        'ret_norm': gain(ks[14], (DEPTH, BRANCH_WIDTH)),
        'w_branch': nrm(ks[15], (DEPTH, N_BRANCH, BRANCH_WIDTH, D_MODEL), BRANCH_WIDTH ** -0.5),
        'b_merge': nrm(ks[16], (DEPTH, N_BRANCH, D_MODEL), 0.1),
        'w_out': nrm(ks[17], (DEPTH, D_MODEL, D_MODEL), D_MODEL ** -0.5),
        'ffn_w_gate': nrm(ks[18], (DEPTH, D_MODEL, D_FF), D_MODEL ** -0.5),
        'ffn_w_up': nrm(ks[19], (DEPTH, D_MODEL, D_FF), D_MODEL ** -0.5),
        'ffn_w_down': nrm(ks[20], (DEPTH, D_FF, D_MODEL), D_FF ** -0.5),
    }

def reference(x, meta_tokens, norm_mix_pre, norm_mix_post, norm_ffn_pre, norm_ffn_post, w_in,
              gla_w_gate_up, gla_b_gate, gla_norm, ml_conv, ml_b_i, ml_b_f, ml_norm, ret_norm,
              w_branch, b_merge, w_out, ffn_w_gate, ffn_w_up, ffn_w_down):
    b = x.shape[0]
    pad = jnp.zeros((b, N_FRONT_PAD, D_MODEL), x.dtype)
    meta = jnp.broadcast_to(meta_tokens.astype(x.dtype)[None], (b, N_META, D_MODEL))
    h = jnp.concatenate([pad, meta, x], axis=1)
    positions = jnp.arange(h.shape[1], dtype=jnp.int32) - N_FRONT_PAD
    valid = positions >= 0
    for layer in range(DEPTH):
        h = _hybrid_layer(h, valid, positions,
                          norm_mix_pre[layer], norm_mix_post[layer], norm_ffn_pre[layer], norm_ffn_post[layer],
                          w_in[layer], gla_w_gate_up[layer], gla_b_gate[layer], gla_norm[layer],
                          ml_conv[layer], ml_b_i[layer], ml_b_f[layer], ml_norm[layer], ret_norm[layer],
                          w_branch[layer], b_merge[layer], w_out[layer],
                          ffn_w_gate[layer], ffn_w_up[layer], ffn_w_down[layer])
    return h[:, BLOCK:, :]


_drawn_inputs = setup_inputs


def setup_inputs(seed=0):
    import zlib

    import numpy as np

    out = dict(_drawn_inputs(seed))
    spreads = {}
    factors = {'norm_ffn_post': 2.962,
     'gla_norm': 16.744,
     'ml_b_i': 64.0,
     'ml_norm': 18.404,
     'ret_norm': 18.164}
    for name, (base, spread) in spreads.items():
        noise = np.random.default_rng([zlib.crc32(name.encode()), seed]).standard_normal(out[name].shape)
        drawn = base * np.exp(spread * noise) if base else spread * noise
        out[name] = __import__('jax').numpy.asarray(drawn.astype(out[name].dtype))
    for name, factor in factors.items():
        out[name] = (out[name] * factor).astype(out[name].dtype)
    return out
```

```python
from contextlib import ExitStack

import numpy as np
import concourse.bass as bass
from concourse import mybir

F32 = mybir.dt.float32
F32R = mybir.dt.float32r
ALU = mybir.AluOpType
ACT = mybir.ActivationFunctionType
ds = bass.ds

P = 128
D = 1024
KT = D // P
DEPTH = 2
META = 16
SEQ = 256
T = META + SEQ
HEADS = 4
HD = 64
DFF = 2816
FT = DFF // P
EPS = 1e-6
GLA_NORMALIZER = 16.0
IN_WIDTH = 7704
NEG = -1e30
KB1, KB2 = META, META + P
SCW = 3 * P

C_SBQ, C_SBK, C_SBV = 0, 256, 512
C_GQ, C_GV, C_GR, C_CODE = 768, 1024, 1280, 1536
C_MQK, C_MV, C_MI, C_MF, C_MO = 1552, 2064, 2320, 2324, 2328
C_RQ, C_RK, C_RV, C_RG, C_MERGE = 2584, 2840, 3096, 3352, 3608

R_MIXPRE, R_MIXPOST, R_FFNPRE, R_FFNPOST, R_BGATE, R_GLAN, R_MLN, R_RETN, R_CONV, R_BMERGE = (
    0, 8, 16, 24, 32, 33, 35, 37, 39, 55)
NPAR = 87

MIX = [("small", None, "small"), ("mqk0", C_MQK, "two"), ("mqk1", C_MQK + 256, "two"), ("mv", C_MV, "v"),
       ("gqk", C_GQ, "two"), ("gv", C_GV, "v"), ("gr", C_GR, "two"), ("rq", C_RQ, "two"), ("rk", C_RK, "two"),
       ("rv", C_RV, "v"), ("rg", C_RG, "two"), ("sbq", C_SBQ, "two"), ("sbk", C_SBK, "two"),
       ("sbv", C_SBV, "v"), ("mo", C_MO, "two")]
TILES_OF = {"small": 1, "two": 2, "v": 3}
SB, GLA, ML, RET = range(4)
NORM_ORDER = (4, 5, 2, 3, 6, 7)
ML_SCALE = HD ** -0.5
V_OF = {"sbv": SB, "gv": GLA, "mv": ML, "rv": RET}
NLOGIT, NBRANCH, NOUT, NGU, NDOWN = 16, 4, 4, FT, 12
GROUPS = len(MIX) + NLOGIT + NBRANCH + NOUT + NGU + NDOWN
DOWN_K = (8, 8, 6)

CONSTS = [("ident", 128), ("mean", 128), ("negtri", 128), ("negones", 128), ("perm", 128), ("negtri0", 32),
          ("mask_lt", SCW), ("neg_lt", SCW), ("neg_le", SCW), ("mask_le", SCW),
          ("mask_lt0", T), ("neg_lt0", T), ("neg_le0", T), ("mask_le0", T),
          ("decay", 4 * SCW), ("decay0", T), ("cos", T), ("sin", T),
          ("headsum", 6 * 12), ("headbc", 6 * P), ("denind", 16), ("denind0", 4), ("negind", 4)]
CONST_W = sum(w for _, w in CONSTS)


def constants():
    c = {n: np.zeros((P, w), np.float64) for n, w in CONSTS}
    p = np.arange(P)
    c["ident"][:] = np.eye(P)
    c["mean"][:] = 1.0 / D
    c["negtri"][:] = -(p[:, None] >= p[None, :]).astype(float)
    c["negones"][:] = -1
    r, head = p % 32, p // 32
    for col in range(32):
        c["negtri0"][:, col] = -((r >= col) & (r < META)).astype(float)
    q = np.concatenate([np.arange(2 * P), np.arange(P)])[None, :]
    lt, le = p[:, None] < q, p[:, None] <= q
    q0 = np.arange(T)[None, :]
    real = (r < META)[:, None]
    lt0, le0 = (r[:, None] < q0) & real, (r[:, None] <= q0) & real
    c["mask_lt"][:], c["mask_le"][:], c["mask_lt0"][:], c["mask_le0"][:] = lt, le, lt0, le0
    c["neg_lt"][:], c["neg_le"][:] = np.where(lt, 0, NEG), np.where(le, 0, NEG)
    c["neg_lt0"][:], c["neg_le0"][:] = np.where(lt0, 0, NEG), np.where(le0, 0, NEG)
    log_gamma = np.log1p(-np.exp2(-5.0 - np.arange(HEADS)))
    for h in range(HEADS):
        c["decay"][:, h * SCW:(h + 1) * SCW] = np.where(le, np.exp(log_gamma[h] * (q - p[:, None])), 0) / 8
    c["decay0"][:] = np.where(le0, np.exp(log_gamma[head][:, None] * (q0 - r[:, None])), 0) / 8
    half = HD // 2
    freq = (10000.0 ** (-np.arange(half, dtype=np.float32) / half)).astype(np.float32)
    ang = (np.arange(T, dtype=np.float32)[None, :] * freq[:, None]).astype(np.float32).astype(np.float64)
    c["cos"][:] = np.tile(np.cos(ang), (4, 1))
    c["sin"][:] = np.tile(np.concatenate([-np.sin(ang), np.sin(ang)]), (2, 1))
    other = np.where(p % HD < half, p + half, p - half)
    c["perm"][other, p] = 1
    for pair in range(6):
        for i in range(P):
            j = 2 * pair + i // HD
            c["headsum"][i, pair * 12 + j] = 1.0 / HD
            c["headbc"][j, pair * P + i] = 1
    for h in range(HEADS):
        c["denind"][:, h * 4 + h] = 1
        c["denind0"][:, h] = head == h
        c["negind"][32 + h, h] = -1
    return np.concatenate([c[n] for n, _ in CONSTS], axis=1).astype(np.float32)


def plan_tiles():
    first, signal = [], []
    done = group = 0

    def free(n):
        nonlocal done
        for _ in range(n):
            done += 1
            signal.append(("tile", done))

    def grouped(n, groups=1):
        nonlocal group
        free(n - 1)
        group += groups
        signal.append(("group", group))

    free(2 + KT)
    for _ in range(DEPTH):
        f = {}

        def stage(name):
            f[name] = len(signal)

        stage("norm0"), free(1)
        for name, _, kind in MIX:
            stage(name), grouped(TILES_OF[kind])
        stage("gate"), free(1)
        stage("rot"), free(4)
        stage("logit"), [grouped(2) for _ in range(NLOGIT)]
        stage("headsum"), free(1)
        stage("headbc"), free(6)
        stage("branch"), [grouped(8) for _ in range(NBRANCH)]
        stage("out"), [grouped(2) for _ in range(NOUT)]
        stage("norm1"), free(1)
        stage("norm2"), free(1)
        stage("gu"), [grouped(2) for _ in range(NGU)]
        stage("down"), [grouped(2, len(DOWN_K)) for _ in range(KT // 2)]
        stage("norm3"), free(1)
        first.append(f)
    out_first = len(signal)
    free(4)
    assert group == GROUPS * DEPTH
    return first, signal, out_first


def build(nc, x, meta_tokens, norm_mix_pre, norm_mix_post, norm_ffn_pre, norm_ffn_post, w_in, gla_w_gate_up,
          gla_b_gate, gla_norm, ml_conv, ml_b_i, ml_b_f, ml_norm, ret_norm, w_branch, b_merge, w_out,
          ffn_w_gate, ffn_w_up, ffn_w_down, consts, out):
    TILE, SIGNAL, TILE_OUT = plan_tiles()
    with ExitStack() as ctx:
        def sb(name, shape, dt=F32):
            return ctx.enter_context(nc.sbuf_tensor(name, shape, dt))

        def sem(name):
            return ctx.enter_context(nc.semaphore(name))

        def per_layer(name):
            return [sem(f"{name}_l{i}") for i in range(DEPTH)]

        raw = [sb(f"raw{i}", [P, KT, 256]) for i in range(2)]
        hi = [sb(f"hi{i}", [P, KT, 256], F32R) for i in range(2)]
        lo = [sb(f"lo{i}", [P, KT, 256], F32R) for i in range(2)]
        hT = sb("hT", [P, KT, T])
        xh = sb("xh", [P, KT, T], F32R)
        xl = sb("xl", [P, KT, T], F32R)
        const = sb("const", [P, CONST_W])
        par = sb("par", [P, DEPTH, NPAR])
        ifbias = sb("ifbias", [P, DEPTH])
        wgate = sb("wgate", [16, DEPTH, P])
        glaref = sb("glaref", [P, 4])
        dm2 = sb("dm2", [12, T])
        ones = sb("ones", [P, T])
        gl = sb("gl", [36, T])
        gr_rows = sb("gr_rows", [36, HEADS, T])

        cut = {}
        at = 0
        for n, w in CONSTS:
            cut[n] = const[:, at:at + w]
            at += w

        def c3(name, n):
            return cut[name].rearrange("p (a b) -> p a b", a=n)

        def region(name, words):
            return ctx.enter_context(nc.sbuf_tensor(name, [P, words], F32))

        def room(shape):
            return (4 * int(np.prod(shape[1:])) + 31) // 32 * 32

        def tenants(start, spec):
            made = []
            for name, shape, dt in spec:
                made.append(nc.alloc_sbuf_tensor_at(name, shape, dt, offset=start))
                start += room(shape)
            return made, start

        a0 = nc.sbuf_base
        gate_region = region("gate_region", 4 * KT * T)
        a1 = nc.sbuf_base
        (gates,), _ = tenants(a0, [("gates", [P, 4 * KT, T], F32)])
        (xt, sq, sub, rstd), end = tenants(a0, [("xt", [P, 3, D], F32), ("sq", [P, KT, T], F32),
                                               ("sub", [P, KT, T], F32), ("rstd", [P, T], F32)])
        assert end <= a1
        mix_spec = [("sbq", [P, 2, T]), ("sbk", [P, 2, T]), ("rq", [P, 2, T]), ("rk", [P, 2, T]),
                    ("conv_in", [P, 4, T + 3]), ("mqk", [P, 4, T]), ("gq", [P, T]), ("gk", [P, T]),
                    ("gr", [P, 2, T]), ("mo", [P, 2, T]), ("rg", [P, 2, T]), ("v", [P, 2, 4, 256]), ("v0", [P, 4, HD]),
                    ("pt", [P, HEADS, SCW]), ("pt0", [P, T]), ("sa", [P, 2, SCW]), ("sb2", [P, 2, SCW]),
                    ("small", [P, T]), ("gwork", [P, T]), ("cum", [P, T]), ("gwork2", [P, T]),
                    ("rows", [P, 3, T]), ("osb", [P, 8, T])]
        gla_spec = [("qa", [P, SEQ]), ("qb", [P, P]), ("q0", [P, META]), ("kr0", [P, KB2]), ("kr1", [P, SEQ]), ("k00", [P, 32])]
        b0 = nc.sbuf_base
        words = sum(room(s) for _, s in mix_spec) // 4
        mix_region = region("mix_region", words)
        made, _ = tenants(b0, [(n, s, F32) for n, s in mix_spec])
        M = dict(zip([n for n, _ in mix_spec], made))
        conv_at = b0 + sum(room(s) for _, s in mix_spec[:4])
        made, end = tenants(conv_at, [(n, s, F32) for n, s in gla_spec])
        M.update(zip([n for n, _ in gla_spec], made))
        assert end <= conv_at + 4 * 4 * (T + 3)
        (yh,), e1 = tenants(b0, [("yh", [P, 8, T], F32R)])
        (yl,), _ = tenants(e1, [("yl", [P, 8, T], F32R)])
        (ah, al, silu_g, prod), end = tenants(b0, [("ah", [P, FT, T], F32R), ("al", [P, FT, T], F32R),
                                                   ("silu_g", [P, 2, T], F32), ("prod", [P, 2, T], F32)])
        assert end <= b0 + 4 * words
        (acc, term), end2 = tenants(e1 + 4 * 8 * T, [("acc", [P, 2, T], F32), ("term", [P, 2, T], F32)])
        assert end2 <= b0 + 4 * words
        (osq,), _ = tenants(b0, [("osq", [P, 6, T], F32)])
        (prows,), _ = tenants(b0, [("prows", [NPAR, DEPTH, P], F32)])
        (otok,), _ = tenants(b0, [("otok", [P, 2, D], F32)])

        def bank(name):
            return ctx.enter_context(nc.psum_tensor(name, [P, 512], F32))

        ring = [bank(f"ring{i}") for i in range(2)]
        sc = [bank(f"sc{i}") for i in range(2)]
        ex, k0, e0, ops = bank("ex"), bank("k0"), bank("e0"), bank("ops")

        raw_loaded = [sem(f"raw_loaded{i}") for i in range(2)]
        small_loaded = sem("small_loaded")
        hi_ready, lo_ready = sem("hi_ready"), sem("lo_ready")
        group_used, tile_done = sem("group_used"), sem("tile_done")
        bank_free = [sem(f"bank_free{i}") for i in range(2)]
        const_loaded, par_loaded, x_loaded, misc_set, bias_loaded = (
            sem(n) for n in ("const_loaded", "par_loaded", "x_loaded", "misc_set", "bias_loaded"))
        sq_ready = [[sem(f"sq_ready{n}_l{i}") for n in range(4)] for i in range(DEPTH)]
        out_rows, out_stored = sem("out_rows"), sem("out_stored")
        names = """var_ready std_ready rstd_ready xn_ready xh_ready xl_ready post_scaled h_ready pad_set
            rot_cos rot_done conv_step conv_done gla_soft gla_dve gla_exp gla_ops ml_soft ml_dve ml_em
            sc_ready sc_free ex_ready ex_free k0_ready k0_free e0_ready e0_free
            sb_soft sb_max sb_keep sb_keep0 sb_p sb_p0 ml_w o_ready o_free den_ready den_abs den_dve
            osq_ready hstd_ready hrstd_ready y_step yh_ready yl_ready merge_step mh_ready ml_ready
            ah_ready al_ready""".split()
        (var_ready, std_ready, rstd_ready, xn_ready, xh_ready, xl_ready, post_scaled, h_ready, pad_set,
         rot_cos, rot_done, conv_step, conv_done, gla_soft, gla_dve, gla_exp, gla_ops, ml_soft, ml_dve, ml_em,
         sc_ready, sc_free, ex_ready, ex_free, k0_ready, k0_free, e0_ready, e0_free,
         sb_soft, sb_max, sb_keep, sb_keep0, sb_p, sb_p0, ml_w, o_ready, o_free, den_ready, den_abs, den_dve,
         osq_ready, hstd_ready, hrstd_ready, y_step, yh_ready, yl_ready, merge_step, mh_ready, ml_ready,
         ah_ready, al_ready) = (per_layer(n) for n in names)

        G_MIX = [l * GROUPS for l in range(DEPTH)]
        G_LOGIT = [g + len(MIX) for g in G_MIX]
        G_BRANCH = [g + NLOGIT for g in G_LOGIT]
        G_OUT = [g + NBRANCH for g in G_BRANCH]
        G_GU = [g + NOUT for g in G_OUT]
        G_DOWN = [g + NGU for g in G_GU]
        G_END = GROUPS * DEPTH

        def group_k(g):
            l = g % GROUPS - (GROUPS - NDOWN)
            return DOWN_K[l % 3] if l >= 0 else KT

        def wait_tile(eng, t, i=0, step=0):
            kind, n = SIGNAL[t]
            per = SIGNAL[t + step][1] - n
            eng.wait_ge(tile_done if kind == "tile" else group_used, n + i * per)

        def wait_taken(eng, t, i=0, step=0):
            eng.wait_ge(bank_free[t % 2], t // 2 + 1 + i * (step // 2))

        def q_start(l):
            return META if l == DEPTH - 1 else 0

        head_rows = [slice(HD * (h % 2), HD * (h % 2) + HD) for h in range(HEADS)]
        quad = [slice(32 * h, 32 * h + 32) for h in range(HEADS)]
        quad_real = [slice(32 * h, 32 * h + META) for h in range(HEADS)]

        block = ctx.enter_context(nc.Block())

        @block.sync
        def _(sp):
            def load(g, src, i=0, step=0, nk=KT):
                if g >= 2:
                    sp.wait_ge(hi_ready, g - 1 + i * step)
                    sp.wait_ge(lo_ready, g - 1 + i * step)
                sp.dma_start(raw[g % 2][:, 0:nk, 0:src.shape[2]], src).then_inc(raw_loaded[g % 2], 16)

            def cols(w, c, n=256):
                return w.rearrange("(k p) n -> p k n", p=P)[:, :, c:c + n]

            for l in range(DEPTH):
                g = G_MIX[l]
                for name, c, kind in MIX:
                    if kind == "small":
                        load(g, cols(w_in[l], C_CODE, 32))
                        sp.dma_start(raw[g % 2][:, :, 32:64], cols(w_in[l], C_MI, 32)).then_inc(small_loaded, 16)
                        sp.dma_start(raw[g % 2][:, :, 64:256], cols(w_in[l], C_MF, 192)).then_inc(small_loaded, 16)
                    else:
                        load(g, cols(w_in[l], c))
                    g += 1
                wm = w_in[l].rearrange("(k p) n -> p k n", p=P)
                wb = w_branch[l].rearrange("n (k p) m -> p (n k) m", p=P)
                wo = w_out[l].rearrange("(k p) m -> p k m", p=P)
                wg = ffn_w_gate[l].rearrange("(k p) m -> p k m", p=P)
                wu = ffn_w_up[l].rearrange("(k p) m -> p k m", p=P)
                wd = ffn_w_down[l].rearrange("(k p) m -> p k m", p=P)
                with sp.Fori(0, NLOGIT // 2) as i:
                    for j in range(2):
                        load(G_LOGIT[l] + j, wm[:, :, ds(i * 512 + (C_MERGE + 256 * j), 256)], i, 2)
                with sp.Fori(0, NBRANCH // 2) as i:
                    for j in range(2):
                        load(G_BRANCH[l] + j, wb[:, :, ds(i * 512 + 256 * j, 256)], i, 2)
                with sp.Fori(0, NOUT // 2) as i:
                    for j in range(2):
                        load(G_OUT[l] + j, wo[:, :, ds(i * 512 + 256 * j, 256)], i, 2)
                with sp.Fori(0, NGU // 2) as i:
                    for j, w in enumerate((wg, wu)):
                        load(G_GU[l] + j, w[:, :, ds(i * 256, 256)], i, 2)
                with sp.Fori(0, 2) as i:
                    for j in range(6):
                        k = 8 * (j % 3)
                        nk = DOWN_K[j % 3]
                        load(G_DOWN[l] + j, wd[:, k:k + nk, ds(i * 512 + 256 * (j // 3), 256)], i, 6, nk)
            for b in range(2):
                sp.wait_ge(out_rows, 2 * b + 2)
                sp.dma_start(out[0, b * P:(b + 1) * P, :], otok[:, b, :]).then_inc(out_stored, 16)
            sp.wait_ge(out_stored, 32)

        @block.tensor
        def _(pe):
            mm = nc.tensor.matmul

            def open_tile(t, i=0, step=0):
                if t >= 2:
                    pe.wait_ge(bank_free[t % 2], t // 2 + i * (step // 2))
                return ring[t % 2]

            def close_tile(last, t):
                last.then_inc(tile_done if SIGNAL[t][0] == "tile" else group_used, 1)

            def use_group(g, i=0, step=0):
                pe.wait_ge(hi_ready, g + 1 + i * step)
                pe.wait_ge(lo_ready, g + 1 + i * step)
                return hi[g % 2], lo[g % 2]

            def product(dst, wh, wl, mh, ml, start, stop):
                mm(dst, wh, mh, start=start, stop=False)
                mm(dst, wh, ml, start=False, stop=False)
                return mm(dst, wl, mh, start=False, stop=stop)

            def features(t, wh, wl, c, mh, ml, q0, i=0, step=0):
                ps = open_tile(t, i, step)
                for k in range(KT):
                    last = product(ps[:, 0:T - q0], wh[:, k, c:c + P], wl[:, k, c:c + P], mh[:, k, q0:], ml[:, k, q0:],
                                   k == 0, k == KT - 1)
                close_tile(last, t)

            def mean_square(l, n, q0):
                t = TILE[l][f"norm{n}"]
                ps = open_tile(t)
                for k in range(KT):
                    pe.wait_ge(sq_ready[l][n], k + 1)
                    last = mm(ps[:, 0:T - q0], cut["mean"], sq[:, k, q0:], start=k == 0, stop=k == KT - 1)
                close_tile(last, t)

            def project(l):
                pe.wait_ge(xh_ready[l], KT)
                pe.wait_ge(xl_ready[l], KT)
                for n, (name, _, kind) in enumerate(MIX):
                    wh, wl = use_group(G_MIX[l] + n)
                    t = TILE[l][name]
                    if kind != "v":
                        for j in range(TILES_OF[kind]):
                            features(t + j, wh, wl, j * P, xh, xl, 0)
                        continue
                    for b, tok in enumerate((0, KB1, KB2)):
                        ps = open_tile(t + b)
                        for k in range(KT):
                            last = product(ps[:, 0:256], xh[:, k, tok:tok + P], xl[:, k, tok:tok + P], wh[:, k, :], wl[:, k, :],
                                           k == 0, k == KT - 1)
                        close_tile(last, t + b)

            def prepare(l):
                t = TILE[l]["gate"]
                wait_taken(pe, TILE[l]["small"])
                close_tile(mm(open_tile(t)[:, 0:T], wgate[:, l, :], M["small"][0:16, :], start=True, stop=True), t)
                for i, name in enumerate(("rq", "rq", "rk", "rk")):
                    t = TILE[l]["rot"] + i
                    wait_taken(pe, TILE[l][name] + i % 2)
                    close_tile(mm(open_tile(t)[:, 0:T], cut["perm"], M[name][:, i % 2, :], start=True, stop=True), t)

            def logits(l):
                q0, g, t = q_start(l), G_LOGIT[l], TILE[l]["logit"]
                with pe.Fori(0, NLOGIT // 2) as i:
                    for j in range(2):
                        wh, wl = use_group(g + j, i, 2)
                        for c in range(2):
                            features(t + 2 * j + c, wh, wl, c * P, xh, xl, q0, i, 4)

            def open_scores(l, mix, h):
                j = 4 * mix + h
                if j >= 2:
                    pe.wait_ge(sc_free[l], j - 1)
                return sc[j % 2]

            def open_scores0(l, mix):
                if mix:
                    pe.wait_ge(k0_free[l], mix)
                return k0

            def plain_scores(dst, dst0, qs, ks, h, both, last_start=True):
                i, rows = h // 2, head_rows[h]
                if dst is not None:
                    mm(dst[:, 0:256], ks[rows, i, KB1:KB2], qs[rows, i, KB1:], start=True, stop=both)
                    return mm(dst[:, 256:SCW], ks[rows, i, KB2:], qs[rows, i, KB2:], start=True, stop=both)
                return mm(dst0[quad[h], 0:T], ks[rows, i, 0:32], qs[rows, i, :], start=True, stop=both)

            def scores0(l, mix, qs, ks):
                d = open_scores0(l, mix)
                for h in range(HEADS):
                    last = plain_scores(None, d, qs, ks, h, True)
                last.then_inc(k0_ready[l], 1)

            def scores(l, mix, h, qs, ks):
                plain_scores(open_scores(l, mix, h), None, qs, ks, h, True).then_inc(sc_ready[l], 1)

            def sb_exponent(l, h):
                qs, ks, i, rows = M["sbq"], M["sbk"], h // 2, head_rows[h]
                keep = M["pt"]
                pe.wait_ge(sb_keep0[l], 1)
                pe.wait_ge(sb_keep[l], h + 1)
                mm(e0[quad[h], 0:T], ks[rows, i, 0:32], qs[rows, i, :], start=True, stop=False)
                mm(e0[quad[h], 0:T], cut["negtri0"][quad[h], :], M["pt0"][quad[h], :], start=False, stop=False)
                mm(e0[quad[h], KB1:T], cut["negones"][:, 0:32], keep[:, h, 0:256], start=False, stop=False)
                last0 = mm(e0[quad[h], KB2:T], cut["negones"][:, 0:32], keep[:, h, 256:SCW], start=False, stop=True)
                if h == HEADS - 1:
                    last0.then_inc(e0_ready[l], 1)
                if h:
                    pe.wait_ge(ex_free[l], h)
                mm(ex[:, 0:256], ks[rows, i, KB1:KB2], qs[rows, i, KB1:], start=True, stop=False)
                mm(ex[:, 0:256], cut["negtri"], keep[:, h, 0:256], start=False, stop=False)
                mm(ex[:, 128:256], cut["negones"], keep[:, h, 256:SCW], start=False, stop=True)
                mm(ex[:, 256:SCW], ks[rows, i, KB2:], qs[rows, i, KB2:], start=True, stop=False)
                mm(ex[:, 256:SCW], cut["negtri"], keep[:, h, 256:SCW], start=False, stop=True).then_inc(ex_ready[l], 1)

            def gla_scores0(l):
                d = open_scores0(l, GLA)
                pe.wait_ge(gla_ops[l], 6)
                for h in range(HEADS):
                    mm(d[quad[h], 0:META], M["k00"][quad[h], :], M["q0"][quad[h], :], start=True, stop=True)
                    last = mm(d[quad[h], META:T], M["kr0"][quad[h], 0:32], M["qa"][quad[h], :], start=True, stop=True)
                last.then_inc(k0_ready[l], 1)

            def gla_scores(l, h):
                d = open_scores(l, GLA, h)
                mm(d[:, 0:128], M["kr0"][quad[h], KB1:KB2], M["qa"][quad[h], 0:P], start=True, stop=True)
                mm(d[:, 128:256], M["kr1"][quad[h], 0:P], M["qb"][quad[h], :], start=True, stop=True)
                mm(d[:, 256:SCW], M["kr1"][quad[h], P:], M["qb"][quad[h], :], start=True, stop=True).then_inc(sc_ready[l], 1)

            def ml_exponent0(l):
                pe.wait_ge(ml_dve[l], 10)
                pe.wait_ge(e0_free[l], 1)
                for h in range(HEADS):
                    last = mm(e0[quad[h], 0:T], gl[:, 0:32], gr_rows[:, h, :], start=True, stop=True)
                last.then_inc(e0_ready[l], 1)

            def ml_exponent(l, h):
                pe.wait_ge(ex_free[l], HEADS + h)
                mm(ex[:, 0:256], gl[:, KB1:KB2], gr_rows[:, h, KB1:], start=True, stop=True)
                mm(ex[:, 256:SCW], gl[:, KB2:], gr_rows[:, h, KB2:], start=True, stop=True).then_inc(ex_ready[l], 1)

            def wait_p(l, mix, h):
                if mix == SB:
                    pe.wait_ge(sb_p0[l], 1)
                    pe.wait_ge(sb_p[l], h + 1)
                else:
                    pe.wait_ge(k0_free[l], mix + 1)
                    pe.wait_ge(sc_free[l], 4 * mix + h + 1)

            def ml_den(l):
                pe.wait_ge(e0_free[l], 2)
                den = c3("denind", 4)
                wait_p(l, ML, 0)
                mm(e0[0:4, 0:T], cut["denind0"], M["pt0"][:], start=True, stop=False)
                for h in range(HEADS):
                    wait_p(l, ML, h)
                    mm(e0[0:4, KB1:T], den[:, h, :], M["pt"][:, h, 0:256], start=False, stop=False)
                    last = mm(e0[0:4, KB2:T], den[:, h, :], M["pt"][:, h, 256:SCW], start=False, stop=h == 3)
                last.then_inc(den_ready[l], 1)

            def values(l, mix, pair):
                n = 2 * mix + pair
                if n:
                    pe.wait_ge(o_free[l], n)
                name = [k for k, m in V_OF.items() if m == mix][0]
                for b in range(3):
                    wait_taken(pe, TILE[l][name] + b)
                for h in (2 * pair, 2 * pair + 1):
                    wait_p(l, mix, h)
                    o = ops[head_rows[h], :]
                    c = slice(h * HD, h * HD + HD)
                    mm(o[:, 0:T], M["v0"][quad_real[h], mix, :], M["pt0"][quad_real[h], :], start=True, stop=False)
                    mm(o[:, KB1:T], M["v"][:, 0, mix, c], M["pt"][:, h, 0:256], start=False, stop=False)
                    last = mm(o[:, KB2:T], M["v"][:, 1, mix, c], M["pt"][:, h, 256:SCW], start=False, stop=True)
                last.then_inc(o_ready[l], 1)

            def mixers(l):
                for name in ("sbq", "sbk"):
                    for j in range(2):
                        wait_taken(pe, TILE[l][name] + j)
                scores0(l, SB, M["sbq"], M["sbk"])
                scores(l, SB, 0, M["sbq"], M["sbk"])
                scores(l, SB, 1, M["sbq"], M["sbk"])
                for h in range(HEADS):
                    sb_exponent(l, h)
                    if h + 2 < HEADS:
                        scores(l, SB, h + 2, M["sbq"], M["sbk"])
                gla_scores0(l)
                gla_scores(l, 0)
                gla_scores(l, 1)
                values(l, SB, 0)
                values(l, SB, 1)
                gla_scores(l, 2)
                gla_scores(l, 3)
                pe.wait_ge(conv_done[l], 4)
                mq, mk = M["mqk"][:, 0:2, :], M["mqk"][:, 2:4, :]
                ml_exponent0(l)
                scores0(l, ML, mq, mk)
                ml_exponent(l, 0)
                scores(l, ML, 0, mq, mk)
                ml_exponent(l, 1)
                values(l, GLA, 0)
                values(l, GLA, 1)
                scores(l, ML, 1, mq, mk)
                for h in (2, 3):
                    ml_exponent(l, h)
                    scores(l, ML, h, mq, mk)
                ml_den(l)
                values(l, ML, 0)
                values(l, ML, 1)
                pe.wait_ge(rot_done[l], 4)
                scores0(l, RET, M["rq"], M["rk"])
                for h in range(HEADS):
                    scores(l, RET, h, M["rq"], M["rk"])
                values(l, RET, 0)
                values(l, RET, 1)

            def head_norm(l):
                t = TILE[l]["headsum"]
                ps = open_tile(t)
                for p in range(6):
                    pe.wait_ge(osq_ready[l], p + 1)
                    last = mm(ps[0:12, 0:T], c3("headsum", 6)[:, p, :], osq[:, p, :], start=p == 0, stop=p == 5)
                close_tile(last, t)
                pe.wait_ge(hrstd_ready[l], 1)
                for p in range(6):
                    t = TILE[l]["headbc"] + p
                    close_tile(mm(open_tile(t)[:, 0:T], c3("headbc", 6)[0:12, p, :], M["rows"][0:12, 0, :], start=True, stop=True), t)

            def branch(l):
                q0, g, t = q_start(l), G_BRANCH[l], TILE[l]["branch"]
                pe.wait_ge(yh_ready[l], 8)
                pe.wait_ge(yl_ready[l], 8)
                with pe.Fori(0, NBRANCH // 2) as i:
                    for j in range(2):
                        wh, wl = use_group(g + j, i, 2)
                        for c in range(8):
                            m, n = c // 4, c % 4
                            tt = t + 8 * j + c
                            ps = open_tile(tt, i, 16)
                            for k in range(2):
                                last = product(ps[:, 0:T - q0], wh[:, 2 * n + k, m * P:m * P + P], wl[:, 2 * n + k, m * P:m * P + P],
                                               yh[:, 2 * n + k, q0:], yl[:, 2 * n + k, q0:], k == 0, k == 1)
                            close_tile(last, tt)

            def output(l):
                q0, g, t = q_start(l), G_OUT[l], TILE[l]["out"]
                pe.wait_ge(mh_ready[l], KT)
                pe.wait_ge(ml_ready[l], KT)
                with pe.Fori(0, NOUT // 2) as i:
                    for j in range(2):
                        wh, wl = use_group(g + j, i, 2)
                        for c in range(2):
                            features(t + 2 * j + c, wh, wl, c * P, xh, xl, q0, i, 4)

            def gate_up(l):
                q0, g, t = q_start(l), G_GU[l], TILE[l]["gu"]
                pe.wait_ge(xh_ready[l], 2 * KT)
                pe.wait_ge(xl_ready[l], 2 * KT)
                with pe.Fori(0, NGU // 2) as i:
                    for j in range(2):
                        wh, wl = use_group(g + j, i, 2)
                        for c in range(2):
                            features(t + 2 * j + c, wh, wl, c * P, xh, xl, q0, i, 4)

            def down(l):
                q0, g, t = q_start(l), G_DOWN[l], TILE[l]["down"]
                pe.wait_ge(ah_ready[l], FT)
                pe.wait_ge(al_ready[l], FT)
                with pe.Fori(0, 2) as i:
                    for j in range(6):
                        wh, wl = use_group(g + j, i, 6)
                        n = DOWN_K[j % 3]
                        for c in range(2):
                            tt = t + 2 * (j // 3) + c
                            ps = open_tile(tt, i, 4) if j % 3 == 0 else ring[tt % 2]
                            for k in range(n):
                                kk = 8 * (j % 3) + k
                                last = product(ps[:, 0:T - q0], wh[:, k, c * P:c * P + P], wl[:, k, c * P:c * P + P],
                                               ah[:, kk, q0:], al[:, kk, q0:], kk == 0, kk == FT - 1)
                            if j % 3 == 2:
                                close_tile(last, tt)
                            elif c == 1:
                                last.then_inc(group_used, 1)

            pe.wait_ge(const_loaded, 16)
            pe.wait_ge(par_loaded, 16 * 11 * DEPTH)
            for l in range(DEPTH):
                close_tile(nc.tensor.transpose(open_tile(l)[:, 0:NPAR], prows[:, l, :], cut["ident"][0:NPAR, 0:NPAR]), l)
            pe.wait_ge(x_loaded, 32)
            for k in range(KT):
                ps = open_tile(2 + k)
                f = slice(k * P, k * P + P)
                nc.tensor.transpose(ps[:, 0:META], xt[0:META, 0, f], cut["ident"][0:META, 0:META])
                nc.tensor.transpose(ps[:, KB1:KB2], xt[:, 1, f], cut["ident"])
                close_tile(nc.tensor.transpose(ps[:, KB2:T], xt[:, 2, f], cut["ident"]), 2 + k)
            for l in range(DEPTH):
                mean_square(l, 0, 0)
                project(l)
                prepare(l)
                logits(l)
                mixers(l)
                head_norm(l)
                branch(l)
                output(l)
                mean_square(l, 1, q_start(l))
                mean_square(l, 2, q_start(l))
                gate_up(l)
                down(l)
                mean_square(l, 3, q_start(l))
            for n, ps in enumerate((ring[0], ring[1], sc[0], sc[1])):
                b, half = n // 2, n % 2
                pe.wait_ge(h_ready[DEPTH - 1], 2 * KT)
                for c in range(4):
                    last = nc.tensor.transpose(ps[:, c * P:c * P + P], hT[:, 4 * half + c, META + b * P:META + b * P + P], cut["ident"])
                close_tile(last, TILE_OUT + n)

        @block.scalar
        def _(act):
            fn = nc.scalar.activation

            def round_group(g, i=0, step=0):
                if g >= G_END:
                    return
                n = group_k(g)
                act.wait_ge(raw_loaded[g % 2], 16 * (g // 2 + 1) + i * (8 * step))
                if g in G_MIX:
                    act.wait_ge(small_loaded, 32 * (G_MIX.index(g) + 1))
                if g >= 2:
                    act.wait_ge(group_used, g - 1 + i * step)
                fn(hi[g % 2][:, 0:n, :], raw[g % 2][:, 0:n, :], ACT.Copy).then_inc(hi_ready, 1)

            def taken(ins, t):
                ins.then_inc(bank_free[t % 2], 1)

            def squares(l, n, q0):
                for k in range(KT):
                    if n == 2:
                        act.wait_ge(h_ready[l], k + 1)
                    elif l:
                        act.wait_ge(h_ready[l - 1], KT + k + 1)
                    else:
                        wait_taken(act, 2 + k)
                    fn(sq[:, k, q0:], hT[:, k, q0:], ACT.Square).then_inc(sq_ready[l][n], 1)

            def std(l, n, q0):
                act.wait_ge(var_ready[l], n + 1)
                fn(rstd[:, q0:], rstd[:, q0:], ACT.Sqrt).then_inc(std_ready[l], 1)

            def round_x(l, n, q0):
                for k in range(KT):
                    act.wait_ge(xn_ready[l], n // 2 * KT + k + 1)
                    fn(xh[:, k, q0:], sq[:, k, q0:], ACT.Copy).then_inc(xh_ready[l], 1)

            def project(l):
                for n, (name, _, kind) in enumerate(MIX):
                    round_group(G_MIX[l] + n + 1)
                    if kind == "v":
                        continue
                    t = TILE[l][name]
                    for j in range(TILES_OF[kind]):
                        wait_tile(act, t + j)
                        ps = ring[(t + j) % 2][:, 0:T]
                        if name == "small":
                            ins = fn(M["small"][:], ps, ACT.Identity, bias=ifbias[:, l:l + 1])
                        elif name in ("mqk0", "mqk1"):
                            ins = fn(M["conv_in"][:, 2 * int(name[3]) + j, 3:], ps, ACT.Copy)
                        elif name == "gqk":
                            ins = fn((M["gq"], M["gk"])[j][:], ps, ACT.Copy, scale=(HD // 2) ** -0.5 if j == 0 else 1.0)
                        elif name in ("gr", "rg"):
                            ins = fn(M[name][:, j, :], ps, ACT.Silu)
                        elif name == "mo":
                            ins = fn(M["mo"][:, j, :], ps, ACT.Sigmoid)
                        elif name == "sbq":
                            ins = fn(M["sbq"][:, j, :], ps, ACT.Copy, scale=HD ** -0.5)
                        else:
                            ins = fn(M[name][:, j, :], ps, ACT.Copy)
                        taken(ins, t + j)

            def logits(l):
                q0, g, t = q_start(l), G_LOGIT[l], TILE[l]["logit"]
                with act.Fori(0, NLOGIT // 2) as i:
                    for j in range(2):
                        round_group(g + j + 1, i, 2)
                        for c in range(2):
                            n = 2 * j + c
                            wait_tile(act, t + n, i, 4)
                            taken(fn(gates[:, ds(i * 4 + n, 1), q0:], ring[(t + n) % 2][:, 0:T - q0], ACT.Sigmoid,
                                     bias=par[:, l, ds(i * 4 + (R_BMERGE + n), 1)]), t + n)

            def gla_prepare(l):
                t = TILE[l]["gate"]
                wait_tile(act, t)
                taken(fn(M["gwork"][:], ring[t % 2][:, 0:T], ACT.Identity, bias=par[:, l, R_BGATE:R_BGATE + 1]), t)

            def ml_conv_silu(l):
                for t in range(4):
                    act.wait_ge(conv_step[l], 12 + t + 1)
                    fn(M["mqk"][:, t, :], M["mqk"][:, t, :], ACT.Silu).then_inc(conv_done[l], 1)

            def softplus_part(dst, src, done, n, first_wait=None):
                if first_wait:
                    act.wait_ge(*first_wait)
                fn(dst, src, ACT.Abs).then_inc(done, 1)
                act.wait_ge(done, n + 1)
                fn(dst, dst, ACT.Exp, scale=-1.0).then_inc(done, 1)
                act.wait_ge(done, n + 2)
                fn(dst, dst, ACT.Ln, bias=1.0).then_inc(done, 1)

            def gates_prepare(l):
                softplus_part(M["gwork2"][:], M["gwork"][:], gla_soft[l], 0,
                              (bank_free[TILE[l]["gate"] % 2], TILE[l]["gate"] // 2 + 1))
                softplus_part(M["rows"][64:68, 0, :], M["small"][64:68, :], ml_soft[l], 0)
                act.wait_ge(gla_dve[l], 6)
                s = 1.0 / GLA_NORMALIZER
                cum, ref = M["cum"], glaref
                for dst, src, scale, bias in ((M["qa"], cum[:, KB1:], s, ref[:, 0:1]), (M["qb"], cum[:, KB2:], s, ref[:, 1:2]),
                                              (M["q0"], cum[:, 0:META], s, 0.0), (M["kr0"], cum[:, 0:KB2], -s, ref[:, 2:3]),
                                              (M["kr1"], cum[:, KB1:], -s, ref[:, 3:4]), (M["k00"], cum[:, 0:32], -s, 0.0)):
                    fn(dst[:], src, ACT.Exp, scale=scale, bias=bias).then_inc(gla_exp[l], 1)
                act.wait_ge(ml_dve[l], 11)
                fn(M["rows"][0:4, 1, :], M["rows"][32:36, 0, :], ACT.Exp, scale=-1.0).then_inc(ml_em[l], 1)

            def take_out(l, n):
                act.wait_ge(o_ready[l], n + 1)
                fn(M["osb"][:, n, :], ops[:, 0:T], ACT.Copy).then_inc(o_free[l], 1)

            def mixers(l):
                act.wait_ge(gla_dve[l], 6)
                softplus_part(M["gwork"][:], k0[:, 0:T], sb_soft[l], 0, (k0_ready[l], 1))
                for h in range(2):
                    softplus_part(M["sb2"][:, h, :], sc[h][:, 0:SCW], sb_soft[l], 3 * (h + 1), (sc_ready[l], h + 1))
                for h in range(HEADS):
                    act.wait_ge(ex_free[l], h + 1)
                    fn(M["pt"][:, h, :], M["sa"][:, h % 2, :], ACT.Exp).then_inc(sb_p[l], 1)
                    if h + 2 < HEADS:
                        softplus_part(M["sb2"][:, h % 2, :], sc[h % 2][:, 0:SCW], sb_soft[l], 3 * (h + 3), (sc_ready[l], h + 3))
                act.wait_ge(e0_free[l], 1)
                fn(M["pt0"][:], M["gwork2"][:], ACT.Exp).then_inc(sb_p0[l], 1)
                take_out(l, 0)
                take_out(l, 1)
                act.wait_ge(e0_free[l], 2)
                fn(M["gwork2"][:], M["gwork"][:], ACT.Exp).then_inc(ml_w[l], 1)
                for h in range(HEADS):
                    if h == 1:
                        take_out(l, 2)
                        take_out(l, 3)
                    act.wait_ge(ex_free[l], HEADS + h + 1)
                    if h >= 2:
                        act.wait_ge(sc_free[l], 4 * ML + h - 1)
                    fn(M["sb2"][:, h % 2, :], M["sa"][:, h % 2, :], ACT.Exp).then_inc(ml_w[l], 1)
                act.wait_ge(den_ready[l], 1)
                fn(M["rows"][0:4, 0, :], e0[0:4, 0:T], ACT.Abs).then_inc(den_abs[l], 1)
                for n in range(4, 8):
                    take_out(l, n)

            def head_norm(l):
                for p, n in enumerate(NORM_ORDER):
                    act.wait_ge(o_free[l], n + 1)
                    if p == 0:
                        act.wait_ge(o_free[l], 8)
                    fn(osq[:, p, :], M["osb"][:, n, :], ACT.Square).then_inc(osq_ready[l], 1)
                t = TILE[l]["headsum"]
                wait_taken(act, t)
                fn(M["rows"][0:12, 0, :], M["rows"][0:12, 0, :], ACT.Sqrt).then_inc(hstd_ready[l], 1)
                for i, n in enumerate((0, 1) + NORM_ORDER):
                    if i >= 2:
                        act.wait_ge(y_step[l], i - 1)
                    fn(yh[:, n, :], M["osb"][:, n, :], ACT.Copy).then_inc(yh_ready[l], 1)

            def branch(l):
                q0, g = q_start(l), G_BRANCH[l]
                with act.Fori(0, NBRANCH // 2) as i:
                    for j in range(2):
                        round_group(g + j + 1, i, 2)
                        for c in range(2):
                            m = 2 * j + c
                            act.wait_ge(merge_step[l], 3 * (m + 1) + i * 12)
                            fn(xh[:, ds(i * 4 + m, 1), q0:], acc[:, c, q0:], ACT.Copy).then_inc(mh_ready[l], 1)

            def take_sublayer(l, n, t, m, q0, i=0, step=0):
                wait_tile(act, t, i, step)
                k = ds(i * step + m, 1) if step else slice(m, m + 1)
                taken(fn(sub[:, k, q0:], ring[t % 2][:, 0:T - q0], ACT.Copy), t)
                wait_taken(act, t, i, step)
                fn(sq[:, k, q0:], sub[:, k, q0:], ACT.Square).then_inc(sq_ready[l][n], 1)

            def output(l):
                q0, g, t = q_start(l), G_OUT[l], TILE[l]["out"]
                with act.Fori(0, NOUT // 2) as i:
                    for j in range(2):
                        round_group(g + j + 1, i, 2)
                        for c in range(2):
                            take_sublayer(l, 1, t + 2 * j + c, 2 * j + c, q0, i, 4)

            def gate_up(l):
                q0, g, t = q_start(l), G_GU[l], TILE[l]["gu"]
                with act.Fori(0, NGU // 2) as i:
                    round_group(g + 1, i, 2)
                    for c in range(2):
                        wait_tile(act, t + c, i, 4)
                        act.wait_ge(bank_free[(t + c) % 2], (t + c) // 2 + i * 2)
                        taken(fn(silu_g[:, c, q0:], ring[(t + c) % 2][:, 0:T - q0], ACT.Silu), t + c)
                    round_group(g + 2, i, 2)
                    for c in range(2):
                        wait_taken(act, t + 2 + c, i, 4)
                        fn(ah[:, ds(i * 2 + c, 1), q0:], prod[:, c, q0:], ACT.Copy).then_inc(ah_ready[l], 1)

            def down(l):
                q0, g, t = q_start(l), G_DOWN[l], TILE[l]["down"]
                for j in range(NDOWN):
                    round_group(g + j + 1)
                    if j % 3 == 2:
                        for c in range(2):
                            m = 2 * (j // 3) + c
                            take_sublayer(l, 3, t + m, m, q0)

            act.dma_start(const[:], consts).then_inc(const_loaded, 16)
            act.dma_start(xt[0:META, 0, :], meta_tokens).then_inc(x_loaded, 16)
            act.dma_start(xt[:, 1:3, :], x[0].rearrange("(b p) n -> p b n", p=P)).then_inc(x_loaded, 16)
            for l in range(DEPTH):
                for r, src in ((R_MIXPRE, norm_mix_pre[l]), (R_MIXPOST, norm_mix_post[l]), (R_FFNPRE, norm_ffn_pre[l]),
                               (R_FFNPOST, norm_ffn_post[l]), (R_BGATE, gla_b_gate[l]), (R_GLAN, gla_norm[l]),
                               (R_MLN, ml_norm[l]), (R_RETN, ret_norm[l])):
                    n = src.shape[0] // P
                    act.dma_start(prows[r:r + n, l, :], src.rearrange("(a p) -> a p", p=P)).then_inc(par_loaded, 16)
                act.dma_start(prows[R_CONV:R_CONV + 16, l, :], ml_conv[l].rearrange("j (a p) -> (j a) p", p=P)).then_inc(par_loaded, 16)
                act.dma_start(prows[R_BMERGE:NPAR, l, :], b_merge[l].rearrange("n (a p) -> (n a) p", p=P)).then_inc(par_loaded, 16)
                act.dma_start(wgate[:, l, :], gla_w_gate_up[l]).then_inc(par_loaded, 16)
                act.wait_ge(misc_set, 1)
                act.dma_start(ifbias[32:36, l:l + 1], ml_b_i[l].rearrange("(p o) -> p o", o=1)).then_inc(bias_loaded, 16)
                act.dma_start(ifbias[64:68, l:l + 1], ml_b_f[l].rearrange("(p o) -> p o", o=1)).then_inc(bias_loaded, 16)
            act.wait_ge(bias_loaded, 32 * DEPTH)
            round_group(0)
            for l in range(DEPTH):
                q0 = q_start(l)
                squares(l, 0, 0)
                std(l, 0, 0)
                round_x(l, 0, 0)
                project(l)
                gla_prepare(l)
                logits(l)
                ml_conv_silu(l)
                gates_prepare(l)
                mixers(l)
                head_norm(l)
                branch(l)
                output(l)
                std(l, 1, q0)
                squares(l, 2, q0)
                std(l, 2, q0)
                round_x(l, 2, q0)
                gate_up(l)
                down(l)
                std(l, 3, q0)
            for n, ps in enumerate((ring[0], ring[1], sc[0], sc[1])):
                wait_tile(act, TILE_OUT + n)
                fn(otok[:, n // 2, 512 * (n % 2):512 * (n % 2) + 512], ps[:], ACT.Copy).then_inc(out_rows, 1)

        @block.vector
        def _(dve):
            tt, ts, stt = nc.vector.tensor_tensor, nc.vector.tensor_scalar, nc.vector.scalar_tensor_tensor
            scan = nc.vector.tensor_tensor_scan

            def rest_of_group(g, i=0, step=0):
                if g >= G_END:
                    return
                n = group_k(g)
                dve.wait_ge(hi_ready, g + 1 + i * step)
                tt(lo[g % 2][:, 0:n, :], raw[g % 2][:, 0:n, :], hi[g % 2][:, 0:n, :].bitcast(F32), ALU.subtract).then_inc(lo_ready, 1)

            def taken(ins, t):
                ins.then_inc(bank_free[t % 2], 1)

            def rstd_of(l, n, q0):
                t = TILE[l][f"norm{n}"]
                wait_tile(dve, t)
                ts(rstd[:, q0:], ring[t % 2][:, 0:T - q0], EPS, None, ALU.add).then_inc(var_ready[l], 1)
                dve.wait_ge(std_ready[l], n + 1)
                taken(nc.vector.reciprocal(rstd[:, q0:], rstd[:, q0:]), t)
                wait_taken(dve, t)

            def pre_norm(l, n, q0, row):
                rstd_of(l, n, q0)
                for k in range(KT + 1):
                    if k < KT:
                        stt(sq[:, k, q0:], hT[:, k, q0:], par[:, l, row + k:row + k + 1], rstd[:, q0:], ALU.mult, ALU.mult).then_inc(xn_ready[l], 1)
                    if k:
                        dve.wait_ge(xh_ready[l], n // 2 * KT + k)
                        tt(xl[:, k - 1, q0:], sq[:, k - 1, q0:], xh[:, k - 1, q0:].bitcast(F32), ALU.subtract).then_inc(xl_ready[l], 1)

            def post_norm(l, n, q0, row):
                rstd_of(l, n, q0)
                base = (n // 2) * KT
                for k in range(KT + 1):
                    if k < KT:
                        stt(sub[:, k, q0:], sub[:, k, q0:], par[:, l, row + k:row + k + 1], rstd[:, q0:], ALU.mult, ALU.mult).then_inc(post_scaled[l], 1)
                    if k:
                        dve.wait_ge(post_scaled[l], base + k)
                        tt(hT[:, k - 1, q0:], hT[:, k - 1, q0:], sub[:, k - 1, q0:], ALU.add).then_inc(h_ready[l], 1)

            def project(l):
                nc.vector.memset(M["conv_in"][:, :, 0:3], 0.0).then_inc(pad_set[l], 1)
                for n, (name, _, kind) in enumerate(MIX):
                    rest_of_group(G_MIX[l] + n + 1)
                    if kind != "v":
                        continue
                    t, mix = TILE[l][name], V_OF[name]
                    wait_tile(dve, t)
                    for h in range(HEADS):
                        ins = nc.vector.tensor_copy(M["v0"][quad_real[h], mix, :], ring[t % 2][0:META, h * HD:h * HD + HD])
                    taken(ins, t)
                    for b in range(2):
                        wait_tile(dve, t + 1 + b)
                        taken(nc.vector.tensor_copy(M["v"][:, b, mix, :], ring[(t + 1 + b) % 2][:, 0:256]), t + 1 + b)

            def logits(l):
                g = G_LOGIT[l]
                with dve.Fori(0, NLOGIT // 2) as i:
                    for j in range(2):
                        rest_of_group(g + j + 1, i, 2)

            def rotary(l):
                for i, name in enumerate(("rq", "rq", "rk", "rk")):
                    t = TILE[l]["rot"] + i
                    v = M[name][:, i % 2, :]
                    turned = M["sa"][:, i % 2, 0:T]
                    wait_tile(dve, t)
                    taken(tt(turned, ring[t % 2][:, 0:T], cut["sin"], ALU.mult), t)
                    tt(v, v, cut["cos"], ALU.mult).then_inc(rot_cos[l], 1)
                    wait_taken(dve, t)
                    dve.wait_ge(rot_cos[l], i + 1)
                    tt(v, v, turned, ALU.add).then_inc(rot_done[l], 1)

            def conv(l):
                for name in ("mqk0", "mqk1"):
                    for j in range(2):
                        wait_taken(dve, TILE[l][name] + j)
                dve.wait_ge(pad_set[l], 1)
                for j in range(4):
                    for t in range(4):
                        tap = par[:, l, R_CONV + 4 * j + t:R_CONV + 4 * j + t + 1]
                        src = M["conv_in"][:, t, j:j + T]
                        if j == 0:
                            ts(M["mqk"][:, t, :], src, tap, None, ALU.mult).then_inc(conv_step[l], 1)
                        else:
                            dve.wait_ge(conv_step[l], 4 * (j - 1) + t + 1)
                            stt(M["mqk"][:, t, :], src, tap, M["mqk"][:, t, :], ALU.mult, ALU.add).then_inc(conv_step[l], 1)

            def gates_prepare(l):
                dve.wait_ge(gla_soft[l], 3)
                stt(M["gwork"][:], M["gwork"][:], 0.0, M["gwork2"][:], ALU.min, ALU.subtract).then_inc(gla_dve[l], 1)
                dve.wait_ge(gla_dve[l], 1)
                scan(M["cum"][:], ones[:], M["gwork"][:], 0.0, ALU.mult, ALU.add).then_inc(gla_dve[l], 1)
                dve.wait_ge(gla_dve[l], 2)
                for c, (at_, s) in enumerate(((KB1 - 1, -1), (KB2 - 1, -1), (KB1 - 1, 1), (KB2 - 1, 1))):
                    ts(glaref[:, c:c + 1], M["cum"][:, at_:at_ + 1], s / GLA_NORMALIZER, None, ALU.mult).then_inc(gla_dve[l], 1)
                rows, small = M["rows"], M["small"]
                dve.wait_ge(ml_soft[l], 3)
                steps = (
                    lambda: stt(rows[64:68, 1, :], small[64:68, :], 0.0, rows[64:68, 0, :], ALU.min, ALU.subtract),
                    lambda: scan(rows[64:68, 2, :], ones[64:68, :], rows[64:68, 1, :], 0.0, ALU.mult, ALU.add),
                    lambda: nc.vector.tensor_copy(rows[32:36, 0, :], rows[64:68, 2, :]),
                    lambda: tt(rows[32:36, 1, :], small[32:36, :], rows[32:36, 0, :], ALU.subtract),
                    lambda: scan(rows[32:36, 2, :], rows[32:36, 1, :], rows[32:36, 1, :], 0.0, ALU.max, ALU.max),
                )
                for n, step in enumerate(steps):
                    step().then_inc(ml_dve[l], 1)
                    dve.wait_ge(ml_dve[l], n + 1)
                nc.vector.tensor_copy(gl[0:4, :], rows[32:36, 1, :]).then_inc(ml_dve[l], 1)
                for h in range(HEADS):
                    ts(gr_rows[32:36, h, :], rows[32:36, 2, :], cut["negind"][32:36, h:h + 1], None, ALU.mult).then_inc(ml_dve[l], 1)
                tt(rows[32:36, 0, :], rows[32:36, 0, :], rows[32:36, 2, :], ALU.add).then_inc(ml_dve[l], 1)
                for n, (dst, src, c) in enumerate(((M["qa"], M["gq"], KB1), (M["qb"], M["gq"], KB2), (M["q0"], M["gq"], 0),
                                                   (M["kr0"], M["gk"], 0), (M["kr1"], M["gk"], KB1), (M["k00"], M["gk"], 0))):
                    dve.wait_ge(gla_exp[l], n + 1)
                    tt(dst[:], dst[:], src[:, c:c + dst.shape[1]], ALU.mult).then_inc(gla_ops[l], 1)

            def wait_spent(l, mix, pair):
                dve.wait_ge(o_ready[l], 2 * (mix - 1) + pair + 1)

            def sb_keep_head(l, h):
                dve.wait_ge(sb_soft[l], 3 * (h + 2))
                stt(M["pt"][:, h, :], sc[h % 2][:, 0:SCW], 0.0, M["sb2"][:, h % 2, :], ALU.max, ALU.add).then_inc(sc_free[l], 1)
                dve.wait_ge(sc_free[l], h + 1)
                tt(M["pt"][:, h, :], M["pt"][:, h, :], cut["mask_lt"], ALU.mult).then_inc(sb_keep[l], 1)

            def mixers(l):
                pt, pt0, sa = M["pt"], M["pt0"], M["sa"]
                dve.wait_ge(sb_soft[l], 3)
                stt(pt0[:], k0[:, 0:T], 0.0, M["gwork"][:], ALU.max, ALU.add).then_inc(k0_free[l], 1)
                dve.wait_ge(k0_free[l], 1)
                tt(pt0[:], pt0[:], cut["mask_lt0"], ALU.mult).then_inc(sb_keep0[l], 1)
                sb_keep_head(l, 0)
                sb_keep_head(l, 1)
                for h in range(HEADS):
                    dve.wait_ge(ex_ready[l], h + 1)
                    if h >= 2:
                        dve.wait_ge(sb_p[l], h - 1)
                    stt(sa[:, h % 2, :], ex[:, 0:SCW], 0.0, cut["neg_lt"], ALU.min, ALU.add).then_inc(ex_free[l], 1)
                    if h + 2 < HEADS:
                        sb_keep_head(l, h + 2)
                dve.wait_ge(e0_ready[l], 1)
                stt(M["gwork2"][:], e0[:, 0:T], 0.0, cut["neg_lt0"], ALU.min, ALU.add).then_inc(e0_free[l], 1)
                dve.wait_ge(k0_ready[l], GLA + 1)
                wait_spent(l, GLA, 1)
                tt(pt0[:], k0[:, 0:T], cut["mask_le0"], ALU.mult).then_inc(k0_free[l], 1)
                for h in range(HEADS):
                    j = 4 * GLA + h
                    dve.wait_ge(sc_ready[l], j + 1)
                    tt(pt[:, h, :], sc[j % 2][:, 0:SCW], cut["mask_le"], ALU.mult).then_inc(sc_free[l], 1)
                dve.wait_ge(e0_ready[l], 2)
                dve.wait_ge(sb_p[l], 4)
                stt(M["gwork"][:], e0[:, 0:T], 0.0, cut["neg_le0"], ALU.min, ALU.add).then_inc(e0_free[l], 1)

                def ml_log(h):
                    dve.wait_ge(ex_ready[l], HEADS + h + 1)
                    if h >= 2:
                        dve.wait_ge(ml_w[l], h)
                    stt(sa[:, h % 2, :], ex[:, 0:SCW], 0.0, cut["neg_le"], ALU.min, ALU.add).then_inc(ex_free[l], 1)

                ml_log(0)
                dve.wait_ge(k0_ready[l], ML + 1)
                dve.wait_ge(ml_w[l], 1)
                wait_spent(l, ML, 1)
                stt(pt0[:], k0[:, 0:T], ML_SCALE, M["gwork2"][:], ALU.mult, ALU.mult).then_inc(k0_free[l], 1)
                for h in range(HEADS):
                    if h + 1 < HEADS:
                        ml_log(h + 1)
                    j = 4 * ML + h
                    dve.wait_ge(sc_ready[l], j + 1)
                    dve.wait_ge(ml_w[l], h + 2)
                    stt(pt[:, h, :], sc[j % 2][:, 0:SCW], ML_SCALE, M["sb2"][:, h % 2, :], ALU.mult, ALU.mult).then_inc(sc_free[l], 1)
                dve.wait_ge(den_abs[l], 1)
                tt(M["rows"][0:4, 2, :], M["rows"][0:4, 0, :], M["rows"][0:4, 1, :], ALU.max).then_inc(den_dve[l], 1)
                dve.wait_ge(den_dve[l], 1)
                tt(dm2[0:4, :], M["rows"][0:4, 2, :], M["rows"][0:4, 2, :], ALU.mult).then_inc(den_dve[l], 1)
                wait_spent(l, RET, 1)
                dve.wait_ge(k0_ready[l], RET + 1)
                tt(pt0[:], k0[:, 0:T], cut["decay0"], ALU.mult).then_inc(k0_free[l], 1)
                for h in range(HEADS):
                    j = 4 * RET + h
                    dve.wait_ge(sc_ready[l], j + 1)
                    tt(pt[:, h, :], sc[j % 2][:, 0:SCW], c3("decay", 4)[:, h, :], ALU.mult).then_inc(sc_free[l], 1)

            def head_norm(l):
                osb = M["osb"]
                t = TILE[l]["headsum"]
                wait_tile(dve, t)
                dve.wait_ge(den_dve[l], 2)
                taken(stt(M["rows"][0:12, 0, :], dm2[:], EPS, ring[t % 2][0:12, 0:T], ALU.mult, ALU.add), t)
                dve.wait_ge(hstd_ready[l], 1)
                nc.vector.reciprocal(M["rows"][0:12, 0, :], M["rows"][0:12, 0, :]).then_inc(hrstd_ready[l], 1)

                def remainder(i, n):
                    dve.wait_ge(yh_ready[l], i + 1)
                    tt(yl[:, n, :], osb[:, n, :], yh[:, n, :].bitcast(F32), ALU.subtract).then_inc(yl_ready[l], 1)

                remainder(0, 0)
                remainder(1, 1)
                for p, n in enumerate(NORM_ORDER):
                    t = TILE[l]["headbc"] + p
                    row, gate = {GLA: (R_GLAN, "gr"), ML: (R_MLN, "mo"), RET: (R_RETN, "rg")}[n // 2]
                    wait_tile(dve, t)
                    taken(stt(osb[:, n, :], osb[:, n, :], par[:, l, row + n % 2:row + n % 2 + 1], ring[t % 2][:, 0:T], ALU.mult, ALU.mult), t)
                    wait_taken(dve, t)
                    tt(osb[:, n, :], osb[:, n, :], M[gate][:, n % 2, :], ALU.mult).then_inc(y_step[l], 1)
                    if p:
                        remainder(p + 1, NORM_ORDER[p - 1])
                remainder(7, NORM_ORDER[5])

            def branch(l):
                q0, g, t0 = q_start(l), G_BRANCH[l], TILE[l]["branch"]
                with dve.Fori(0, NBRANCH // 2) as i:
                    for j in range(2):
                        rest_of_group(g + j + 1, i, 2)
                        for c in range(2):
                            m = 2 * j + c
                            for n in range(4):
                                t = t0 + 4 * m + n
                                ps, gate = ring[t % 2][:, 0:T - q0], gates[:, ds(i * 4 + (8 * n + m), 1), q0:]
                                wait_tile(dve, t, i, 16)
                                if n == 0:
                                    taken(tt(acc[:, c, q0:], ps, gate, ALU.mult), t)
                                    continue
                                taken(tt(term[:, n % 2, q0:], ps, gate, ALU.mult), t)
                                wait_taken(dve, t, i, 16)
                                if n == 1:
                                    wait_taken(dve, t - 1, i, 16)
                                else:
                                    dve.wait_ge(merge_step[l], 3 * m + n - 1 + i * 12)
                                tt(acc[:, c, q0:], acc[:, c, q0:], term[:, n % 2, q0:], ALU.add).then_inc(merge_step[l], 1)
                            dve.wait_ge(mh_ready[l], m + 1 + i * 4)
                            tt(xl[:, ds(i * 4 + m, 1), q0:], acc[:, c:c + 1, q0:], xh[:, ds(i * 4 + m, 1), q0:].bitcast(F32), ALU.subtract).then_inc(ml_ready[l], 1)

            def output(l):
                g = G_OUT[l]
                with dve.Fori(0, NOUT // 2) as i:
                    for j in range(2):
                        rest_of_group(g + j + 1, i, 2)

            def gate_up(l):
                q0, g, t = q_start(l), G_GU[l], TILE[l]["gu"]
                with dve.Fori(0, NGU // 2) as i:
                    rest_of_group(g + 1, i, 2)
                    rest_of_group(g + 2, i, 2)
                    for c in range(2):
                        wait_tile(dve, t + 2 + c, i, 4)
                        wait_taken(dve, t + c, i, 4)
                        taken(tt(prod[:, c, q0:], ring[(t + c) % 2][:, 0:T - q0], silu_g[:, c, q0:], ALU.mult), t + 2 + c)
                    for c in range(2):
                        dve.wait_ge(ah_ready[l], c + 1 + i * 2)
                        tt(al[:, ds(i * 2 + c, 1), q0:], prod[:, c:c + 1, q0:], ah[:, ds(i * 2 + c, 1), q0:].bitcast(F32), ALU.subtract).then_inc(al_ready[l], 1)

            def down(l):
                for j in range(NDOWN):
                    rest_of_group(G_DOWN[l] + j + 1)

            nc.vector.memset(ifbias[:], 0.0).then_inc(misc_set, 1)
            nc.vector.memset(ones[:], 1.0).then_inc(misc_set, 1)
            nc.vector.memset(dm2[:], 1.0).then_inc(misc_set, 1)
            nc.vector.memset(gl[:], 0.0).then_inc(misc_set, 1)
            nc.vector.memset(gr_rows[:], 0.0).then_inc(misc_set, 1)
            dve.wait_ge(misc_set, 5)
            nc.vector.memset(gl[32:36, :], 1.0).then_inc(misc_set, 1)
            dve.wait_ge(const_loaded, 16)
            for h in range(HEADS):
                ts(gr_rows[0:4, h, :], ones[0:4, :], cut["ident"][0:4, h:h + 1], None, ALU.mult).then_inc(misc_set, 1)
            for l in range(DEPTH):
                wait_tile(dve, l)
                taken(nc.vector.tensor_copy(par[:, l, :], ring[l][:, 0:NPAR]), l)
            for k in range(KT):
                wait_tile(dve, 2 + k)
                taken(nc.vector.tensor_copy(hT[:, k, :], ring[k % 2][:, 0:T]), 2 + k)
            wait_taken(dve, 2 + KT - 1)
            wait_taken(dve, 2 + KT - 2)
            rest_of_group(0)
            for l in range(DEPTH):
                q0 = q_start(l)
                pre_norm(l, 0, 0, R_MIXPRE)
                project(l)
                rotary(l)
                logits(l)
                conv(l)
                gates_prepare(l)
                mixers(l)
                head_norm(l)
                branch(l)
                output(l)
                post_norm(l, 1, q0, R_MIXPOST)
                pre_norm(l, 2, q0, R_FFNPRE)
                gate_up(l)
                down(l)
                post_norm(l, 3, q0, R_FFNPOST)


_INS = ["x", "meta_tokens", "norm_mix_pre", "norm_mix_post", "norm_ffn_pre", "norm_ffn_post", "w_in", "gla_w_gate_up",
        "gla_b_gate", "gla_norm", "ml_conv", "ml_b_i", "ml_b_f", "ml_norm", "ret_norm", "w_branch", "b_merge", "w_out",
        "ffn_w_gate", "ffn_w_up", "ffn_w_down"]


def kernel(**inputs):
    import concourse.bacc as bacc
    from concourse.bass_utils import run_bass_kernel_spmd

    nc = bacc.Bacc("TRN2", target_bir_lowering=False, num_devices=1)
    arrays = {f"in_{n}": np.ascontiguousarray(inputs[n]) for n in _INS}
    arrays["in_consts"] = constants()
    args = [nc.dram_tensor(n, a.shape, mybir.dt.from_np(a.dtype), kind="ExternalInput").ap() for n, a in arrays.items()]
    out = nc.dram_tensor("out", (1, SEQ, D), F32, kind="ExternalOutput").ap()
    build(nc, *args, out)
    r = run_bass_kernel_spmd(nc, [arrays], core_ids=[0])
    return r.results[0]["out"]
```

```python
from contextlib import ExitStack

import numpy as np
import concourse.bass as bass
from concourse import mybir

F32 = mybir.dt.float32
F32R = mybir.dt.float32r
ALU = mybir.AluOpType
ACT = mybir.ActivationFunctionType
ds = bass.ds

P = 128
D = 1024
KT = D // P
DEPTH = 2
META = 16
SEQ = 256
T = META + SEQ
HEADS = 4
HD = 64
DFF = 2816
FT = DFF // P
EPS = 1e-6
GLA_NORMALIZER = 16.0
IN_WIDTH = 7704
NEG = -1e30
KB1, KB2 = META, META + P
SCW = 3 * P

C_SBQ, C_SBK, C_SBV = 0, 256, 512
C_GQ, C_GV, C_GR, C_CODE = 768, 1024, 1280, 1536
C_MQK, C_MV, C_MI, C_MF, C_MO = 1552, 2064, 2320, 2324, 2328
C_RQ, C_RK, C_RV, C_RG, C_MERGE = 2584, 2840, 3096, 3352, 3608

R_MIXPRE, R_MIXPOST, R_FFNPRE, R_FFNPOST, R_BGATE, R_GLAN, R_MLN, R_RETN, R_CONV, R_BMERGE = (
    0, 8, 16, 24, 32, 33, 35, 37, 39, 55)
NPAR = 87

MIX = [("small", None, "small"), ("mqk0", C_MQK, "two"), ("mqk1", C_MQK + 256, "two"), ("gr", C_GR, "two"),
       ("rg", C_RG, "two"), ("gqk", C_GQ, "two"), ("rq", C_RQ, "two"), ("rk", C_RK, "two"), ("mv", C_MV, "v"),
       ("gv", C_GV, "v"), ("rv", C_RV, "v"), ("mo", C_MO, "two"), ("sbq", C_SBQ, "two"), ("sbk", C_SBK, "two"),
       ("sbv", C_SBV, "v")]
KIND = {name: kind for name, _, kind in MIX}
MIX_NO = {name: n for n, (name, _, _) in enumerate(MIX)}
TILES_OF = {"small": 1, "two": 2, "v": 3}
SB, GLA, ML, RET = range(4)
NORM_ORDER = (4, 5, 2, 3, 6, 7)
ML_SCALE = HD ** -0.5
V_OF = {"sbv": SB, "gv": GLA, "mv": ML, "rv": RET}
NLOGIT, NBRANCH, NOUT, NGU, NDOWN = 16, 4, 4, FT, 12
GROUPS = len(MIX) + NLOGIT + NBRANCH + NOUT + NGU + NDOWN
DOWN_K = (8, 8, 6)

CONSTS = [("ident", 128), ("mean", 128), ("eps", 1), ("negtri", 128), ("negones", 128), ("perm", 128), ("negtri0", 32),
          ("mask_lt", SCW), ("neg_lt", SCW), ("neg_le", SCW), ("mask_le", SCW),
          ("mask_lt0", T), ("neg_lt0", T), ("neg_le0", T), ("mask_le0", T),
          ("decay", 4 * SCW), ("decay0", T), ("cos", T), ("sin", T),
          ("headsum", 6 * 12), ("headbc", 6 * P), ("denind", 16), ("denind0", 4), ("negind", 4)]
CONST_FIRST = 257
CONST_W = sum(w for _, w in CONSTS)


def constants():
    c = {n: np.zeros((P, w), np.float64) for n, w in CONSTS}
    p = np.arange(P)
    c["ident"][:] = np.eye(P)
    c["mean"][:] = 1.0 / D
    c["negtri"][:] = -(p[:, None] >= p[None, :]).astype(float)
    c["negones"][:] = -1
    c["eps"][:] = EPS
    r, head = p % 32, p // 32
    for col in range(32):
        c["negtri0"][:, col] = -((r >= col) & (r < META)).astype(float)
    q = np.concatenate([np.arange(2 * P), np.arange(P)])[None, :]
    lt, le = p[:, None] < q, p[:, None] <= q
    q0 = np.arange(T)[None, :]
    real = (r < META)[:, None]
    lt0, le0 = (r[:, None] < q0) & real, (r[:, None] <= q0) & real
    c["mask_lt"][:], c["mask_le"][:], c["mask_lt0"][:], c["mask_le0"][:] = lt, le, lt0, le0
    c["neg_lt"][:], c["neg_le"][:] = np.where(lt, 0, NEG), np.where(le, 0, NEG)
    c["neg_lt0"][:], c["neg_le0"][:] = np.where(lt0, 0, NEG), np.where(le0, 0, NEG)
    log_gamma = np.log1p(-np.exp2(-5.0 - np.arange(HEADS)))
    for h in range(HEADS):
        c["decay"][:, h * SCW:(h + 1) * SCW] = np.where(le, np.exp(log_gamma[h] * (q - p[:, None])), 0) / 8
    c["decay0"][:] = np.where(le0, np.exp(log_gamma[head][:, None] * (q0 - r[:, None])), 0) / 8
    half = HD // 2
    freq = (10000.0 ** (-np.arange(half, dtype=np.float32) / half)).astype(np.float32)
    ang = (np.arange(T, dtype=np.float32)[None, :] * freq[:, None]).astype(np.float32).astype(np.float64)
    c["cos"][:] = np.tile(np.cos(ang), (4, 1))
    c["sin"][:] = np.tile(np.concatenate([-np.sin(ang), np.sin(ang)]), (2, 1))
    other = np.where(p % HD < half, p + half, p - half)
    c["perm"][other, p] = 1
    for pair in range(6):
        for i in range(P):
            j = 2 * pair + i // HD
            c["headsum"][i, pair * 12 + j] = 1.0 / HD
            c["headbc"][j, pair * P + i] = 1
    for h in range(HEADS):
        c["denind"][:, h * 4 + h] = 1
        c["denind0"][:, h] = head == h
        c["negind"][32 + h, h] = -1
    return np.concatenate([c[n] for n, _ in CONSTS], axis=1).astype(np.float32)


PROJECT = [("group", "small"), ("group", "mqk0"), ("gate",), ("group", "mqk1"), ("silu_tables",), ("group", "gr"), ("conv", 0), ("group", "rg"),
           ("conv", 1), ("group", "gqk"), ("conv", 2), ("group", "rq"), ("conv", 3), ("group", "rk"), ("conv_silu",),
           ("group", "mv"), ("rot", 0), ("rot", 1), ("group", "gv"), ("rot", 2), ("rot", 3), ("group", "rv"),
           ("group", "mo"), ("group", "sbq"), ("group", "sbk"), ("group", "sbv"), ("sb_scores0",), ("sb_scores", 0), ("sb_scores", 1)]
BEFORE = {
    0: [("exp_tables",), ("sb_soft0",), ("sb_keep0",), ("sb_soft", 0), ("sb_keep", 0)],
    1: [("sb_soft", 1), ("sb_mask", 0), ("sb_p", 0), ("sb_keep", 1)],
    2: [("sb_soft", 2), ("sb_mask", 1), ("sb_p", 1), ("sb_keep", 2)],
    3: [("sb_soft", 3), ("sb_mask", 2), ("sb_p", 2), ("sb_keep", 3)],
    4: [("gla_soft",), ("sb_mask", 3), ("sb_mask0",), ("sb_p", 3), ("sb_p0",)],
    5: [("gla_log",), ("gla_exp",), ("gla_decay",)],
    6: [("ml_soft",), ("take_out", 0)],
    7: [("take_out", 1), ("gla_p0",), ("gla_p", 0), ("gla_p", 1), ("ml_rows",)],
    8: [("gla_p", 2), ("gla_p", 3), ("ml_em",)],
    9: [("take_out", 2)],
    10: [("ml_mask0",), ("ml_mask", 0), ("ml_w0",), ("ml_w", 0), ("take_out", 3), ("ml_p0",), ("ml_p", 0)],
    11: [("ml_mask", 1), ("ml_w", 1), ("ml_p", 1)],
    12: [("ml_mask", 2), ("ml_w", 2), ("ml_p", 2)],
    13: [("ml_mask", 3), ("ml_w", 3), ("ml_p", 3)],
    14: [("den_abs",), ("den_square",)],
    15: [("take_out", 4)],
    16: [("take_out", 5), ("ret_p0",), ("ret_p", 0), ("ret_p", 1), ("head_square", 2), ("head_square", 3)],
    17: [("ret_p", 2), ("ret_p", 3), ("head_square", 0), ("head_square", 1)],
    18: [("take_out", 6)],
    19: [("take_out", 7), ("head_square", 4), ("head_square", 5)],
    20: [("head_var",), ("head_rstd",), ("sigmoid_tables",), ("y_plain",), ("mo_sigmoid",)],
    21: [("y_rest", 0)],
    22: [("y_rest", 1), ("gate_sigmoid", 0)],
    23: [("gate_sigmoid", 1)],
    24: [("y_rest", 2), ("gate_sigmoid", 2)],
    25: [("y_rest", 3)],
    26: [("y_rest", 4), ("gate_sigmoid", 3)],
    27: [("y_rest", 5)],
    28: [("gate_sigmoid", 4)],
}
BEHIND = {
    0: [("sb_exponent", 0), ("sb_scores", 2)],
    1: [("sb_exponent", 1), ("sb_scores", 3)],
    2: [("sb_exponent", 2)],
    3: [("sb_exponent", 3)],
    5: [("values", 0, 0), ("gla_scores0",)],
    6: [("values", 0, 1), ("gla_scores", 0), ("gla_scores", 1)],
    7: [("gla_scores", 2), ("gla_scores", 3)],
    8: [("values", 1, 0)],
    9: [("values", 1, 1), ("ml_exponent0",), ("ml_scores0",), ("ml_exponent", 0), ("ml_scores", 0)],
    10: [("ml_exponent", 1), ("ml_scores", 1)],
    11: [("ml_exponent", 2), ("ml_scores", 2)],
    12: [("ml_exponent", 3), ("ml_scores", 3)],
    13: [("ml_den",)],
    14: [("values", 2, 0)],
    15: [("values", 2, 1), ("ret_scores0",), ("ret_scores", 0), ("ret_scores", 1)],
    16: [("ret_scores", 2), ("ret_scores", 3)],
    17: [("values", 3, 0)],
    18: [("values", 3, 1)],
    19: [("headsum",)],
    20: [("headbc", 0)],
    21: [("headbc", 1)],
    23: [("headbc", 2)],
    24: [("headbc", 3)],
    25: [("headbc", 4)],
    26: [("headbc", 5)],
}
STEPS = PROJECT + [step for j in range(2 * NLOGIT) for step in BEFORE.get(j, []) + [("logit", j)] + BEHIND.get(j, [])]
SIGMOID_FROM = 20


ROUND_AHEAD = 4
REST_AHEAD = 3


def plan_tiles():
    first, signal = [], []
    done = halves = 0

    def free(n):
        nonlocal done
        for _ in range(n):
            done += 1
            signal.append(("tile", done, 1))

    def last_of(used, before=0):
        nonlocal halves
        halves += before + used
        signal.append(("half", halves, used))

    free(KT + DEPTH)
    for _ in range(DEPTH):
        f = {}

        def stage(name):
            f[name] = len(signal)

        stage("norm0"), free(1)
        for step in STEPS:
            stage(step)
            if step[0] == "group":
                kind = KIND[step[1]]
                if kind == "two":
                    last_of(1), last_of(1)
                else:
                    free(TILES_OF[kind] - 1)
                    last_of(2)
            elif step[0] == "logit":
                last_of(1)
            elif step[0] in ("gate", "rot", "headsum", "headbc"):
                free(1)
        halves += 2 * NBRANCH
        stage("out"), [last_of(1) for _ in range(KT)]
        stage("norm1"), free(1)
        stage("norm2"), free(1)
        stage("gu"), [last_of(1) for _ in range(2 * NGU)]
        stage("down")
        for _ in range(KT // 2):
            last_of(1, 2 * len(DOWN_K) - 2), last_of(1)
        stage("norm3"), free(1)
        first.append(f)
    out_first = len(signal)
    free(4)
    assert halves == 2 * GROUPS * DEPTH
    return first, signal, out_first


def build(nc, x, meta_tokens, norm_mix_pre, norm_mix_post, norm_ffn_pre, norm_ffn_post, w_in, gla_w_gate_up,
          gla_b_gate, gla_norm, ml_conv, ml_b_i, ml_b_f, ml_norm, ret_norm, w_branch, b_merge, w_out,
          ffn_w_gate, ffn_w_up, ffn_w_down, consts, out):
    TILE, SIGNAL, TILE_OUT = plan_tiles()
    with ExitStack() as ctx:
        def sb(name, shape, dt=F32):
            return ctx.enter_context(nc.sbuf_tensor(name, shape, dt))

        def sem(name):
            return ctx.enter_context(nc.semaphore(name))

        def per_layer(name):
            return [sem(f"{name}_l{i}") for i in range(DEPTH)]

        raw = [sb(f"raw{i}", [P, KT, 256]) for i in range(2)]
        hi = [sb(f"hi{i}", [P, KT, 256], F32R) for i in range(2)]
        lo = [sb(f"lo{i}", [P, KT, 256], F32R) for i in range(2)]
        hT = sb("hT", [P, KT, T])
        xh = sb("xh", [P, KT, T], F32R)
        xl = sb("xl", [P, KT, T], F32R)
        const = sb("const", [P, CONST_W])
        par = sb("par", [P, DEPTH, NPAR])
        ifbias = sb("ifbias", [P, DEPTH])
        wgate = sb("wgate", [16, DEPTH, P])
        glaref = sb("glaref", [P, 4])
        dm2 = sb("dm2", [12, T])
        ones = sb("ones", [P, T])
        gl = sb("gl", [36, T])
        gr_rows = sb("gr_rows", [36, HEADS, T])

        cut = {}
        at = 0
        for n, w in CONSTS:
            cut[n] = const[:, at:at + w]
            at += w

        def c3(name, n):
            return cut[name].rearrange("p (a b) -> p a b", a=n)

        def region(name, words):
            return ctx.enter_context(nc.sbuf_tensor(name, [P, words], F32))

        def room(shape):
            return (4 * int(np.prod(shape[1:])) + 31) // 32 * 32

        def tenants(start, spec):
            made = []
            for name, shape, dt in spec:
                made.append(nc.alloc_sbuf_tensor_at(name, shape, dt, offset=start))
                start += room(shape)
            return made, start

        a0 = nc.sbuf_base
        gate_region = region("gate_region", 4 * KT * T)
        a1 = nc.sbuf_base
        (gates,), _ = tenants(a0, [("gates", [P, 4 * KT, T], F32)])
        (xt, sq, sub, rstd), end = tenants(a0, [("xt", [P, 3, D], F32), ("sq", [P, KT, T], F32),
                                               ("sub", [P, KT, T], F32), ("rstd", [P, T], F32)])
        assert end <= a1
        mix_spec = [("sbq", [P, 2, T]), ("sbk", [P, 2, T]), ("rq", [P, 2, T]), ("rk", [P, 2, T]),
                    ("conv_in", [P, 4, T + 3]), ("mqk", [P, 4, T]), ("gq", [P, T]), ("gk", [P, T]),
                    ("gr", [P, 2, T]), ("mo", [P, 2, T]), ("rg", [P, 2, T]), ("v", [P, 2, 4, 256]), ("v0", [P, 4, HD]),
                    ("pt", [P, HEADS, SCW]), ("pt0", [P, T]), ("sa", [P, 2, SCW]), ("sb2", [P, 2, SCW]),
                    ("small", [P, T]), ("gwork", [P, T]), ("cum", [P, T]), ("gwork2", [P, T]),
                    ("rows", [P, 3, T]), ("osb", [P, 8, T])]
        gla_spec = [("qa", [P, SEQ]), ("qb", [P, P]), ("q0", [P, META]), ("kr0", [P, KB2]), ("kr1", [P, SEQ]), ("k00", [P, 32])]
        b0 = nc.sbuf_base
        words = sum(room(s) for _, s in mix_spec) // 4
        mix_region = region("mix_region", words)
        made, _ = tenants(b0, [(n, s, F32) for n, s in mix_spec])
        M = dict(zip([n for n, _ in mix_spec], made))
        conv_at = b0 + sum(room(s) for _, s in mix_spec[:4])
        made, end = tenants(conv_at, [(n, s, F32) for n, s in gla_spec])
        M.update(zip([n for n, _ in gla_spec], made))
        assert end <= conv_at + 4 * 4 * (T + 3)
        (yh,), e1 = tenants(b0, [("yh", [P, 8, T], F32R)])
        (yl,), _ = tenants(e1, [("yl", [P, 8, T], F32R)])
        (ah, al, silu_g, prod), end = tenants(b0, [("ah", [P, FT, T], F32R), ("al", [P, FT, T], F32R),
                                                   ("silu_g", [P, 2, T], F32), ("prod", [P, 2, T], F32)])
        assert end <= b0 + 4 * words
        (acc, half, term), end2 = tenants(e1 + 4 * 8 * T, [("acc", [P, 2, T], F32), ("half", [P, 2, T], F32),
                                                           ("term", [P, 2, 4, T], F32)])
        assert end2 <= b0 + 4 * words
        (osq,), _ = tenants(b0, [("osq", [P, 6, T], F32)])
        (prows,), _ = tenants(b0, [("prows", [NPAR, DEPTH, P], F32)])
        (otok,), _ = tenants(b0, [("otok", [P, 2, D], F32)])

        banks = ctx.enter_context(nc.psum_tensor("banks", [P, 8, 512], F32))
        ring = [banks[:, i, :] for i in range(2)]
        sc = [banks[:, 2 + i, :] for i in range(2)]
        ex, k0, e0, ops = (banks[:, 4 + i, :] for i in range(4))
        branch_banks = [banks[:, 4 * i:4 * i + 4, :] for i in range(2)]

        raw_loaded = [sem(f"raw_loaded{i}") for i in range(2)]
        small_loaded = sem("small_loaded")
        hi_ready, lo_ready = sem("hi_ready"), sem("lo_ready")
        half_used, tile_done = sem("half_used"), sem("tile_done")
        bank_free = [sem(f"bank_free{i}") for i in range(2)]
        first_loaded, const_loaded, par_loaded, meta_loaded, misc_set, bias_loaded = (
            sem(n) for n in ("first_loaded", "const_loaded", "par_loaded", "meta_loaded", "misc_set", "bias_loaded"))
        x_loaded = [sem(f"x_loaded{i}") for i in range(2)]
        sq_ready = [[sem(f"sq_ready{n}_l{i}") for n in range(4)] for i in range(DEPTH)]
        out_rows, out_stored = sem("out_rows"), sem("out_stored")
        names = """sq_summed silu_ready silu_scaled log_ready rstd_ready xn_ready xh_ready xl_ready post_scaled h_ready pad_set
            rot_cos rot_done conv_step conv_done gla_soft gla_dve gla_exp gla_ops ml_soft ml_dve ml_em
            sc_ready sc_free ex_ready ex_free k0_ready k0_free e0_ready e0_free
            sb_soft sb_max sb_keep sb_keep0 sb_p sb_p0 ml_w o_ready o_free den_ready den_abs den_dve
            osq_ready hlog_ready hrstd_ready mo_ready y_step yh_ready yl_ready gates_ready
            branch_free half_ready merge_step mh_ready ml_ready ah_ready al_ready""".split()
        (sq_summed, silu_ready, silu_scaled, log_ready, rstd_ready, xn_ready, xh_ready, xl_ready, post_scaled, h_ready, pad_set,
         rot_cos, rot_done, conv_step, conv_done, gla_soft, gla_dve, gla_exp, gla_ops, ml_soft, ml_dve, ml_em,
         sc_ready, sc_free, ex_ready, ex_free, k0_ready, k0_free, e0_ready, e0_free,
         sb_soft, sb_max, sb_keep, sb_keep0, sb_p, sb_p0, ml_w, o_ready, o_free, den_ready, den_abs, den_dve,
         osq_ready, hlog_ready, hrstd_ready, mo_ready, y_step, yh_ready, yl_ready, gates_ready,
         branch_free, half_ready, merge_step, mh_ready, ml_ready, ah_ready, al_ready) = (per_layer(n) for n in names)

        G_MIX = [l * GROUPS for l in range(DEPTH)]
        G_LOGIT = [g + len(MIX) for g in G_MIX]
        G_BRANCH = [g + NLOGIT for g in G_LOGIT]
        G_OUT = [g + NBRANCH for g in G_BRANCH]
        G_GU = [g + NOUT for g in G_OUT]
        G_DOWN = [g + NGU for g in G_GU]
        G_END = GROUPS * DEPTH

        def group_k(g):
            l = g % GROUPS - (GROUPS - NDOWN)
            return DOWN_K[l % 3] if l >= 0 else KT

        def wait_tile(eng, t, i=0, step=0):
            kind, n, _ = SIGNAL[t]
            per = SIGNAL[t + step][1] - n
            eng.wait_ge(tile_done if kind == "tile" else half_used, n + i * per)

        def wait_taken(eng, t, i=0, step=0):
            eng.wait_ge(bank_free[t % 2], t // 2 + 1 + i * (step // 2))

        def group_tile(l, name):
            return TILE[l][("group", name)]

        def run_steps(l, parts):
            for name, *which in STEPS:
                if name in parts:
                    parts[name](l, *which)

        def q_start(l):
            return META if l == DEPTH - 1 else 0

        head_rows = [slice(HD * (h % 2), HD * (h % 2) + HD) for h in range(HEADS)]
        quad = [slice(32 * h, 32 * h + 32) for h in range(HEADS)]
        quad_real = [slice(32 * h, 32 * h + META) for h in range(HEADS)]

        block = ctx.enter_context(nc.Block())

        @block.sync
        def _(sp):
            def load(g, src, i=0, step=0, nk=KT):
                if g >= 2:
                    sp.wait_ge(hi_ready, 2 * (g - 1) + i * (2 * step))
                    sp.wait_ge(lo_ready, 2 * (g - 1) + i * (2 * step))
                sp.dma_start(raw[g % 2][:, 0:nk, 0:src.shape[2]], src).then_inc(raw_loaded[g % 2], 16)

            def cols(w, c, n=256):
                return w.rearrange("(k p) n -> p k n", p=P)[:, :, c:c + n]

            sp.dma_start(xt[0:META, 0, :], meta_tokens).then_inc(meta_loaded, 16)
            for n in range(2):
                sp.dma_start(xt[:, 1:3, n * 512:n * 512 + 512],
                             x[0].rearrange("(b p) n -> p b n", p=P)[:, :, n * 512:n * 512 + 512]).then_inc(x_loaded[n], 16)
            for l in range(DEPTH):
                g = G_MIX[l]
                for name, c, kind in MIX:
                    if kind == "small":
                        load(g, cols(w_in[l], C_CODE, 32))
                        sp.dma_start(raw[g % 2][:, :, 32:64], cols(w_in[l], C_MI, 32)).then_inc(small_loaded, 16)
                        sp.dma_start(raw[g % 2][:, :, 64:256], cols(w_in[l], C_MF, 192)).then_inc(small_loaded, 16)
                    else:
                        load(g, cols(w_in[l], c))
                    g += 1
                wm = w_in[l].rearrange("(k p) n -> p k n", p=P)
                wb = w_branch[l].rearrange("n (k p) m -> p (n k) m", p=P)
                wo = w_out[l].rearrange("(k p) m -> p k m", p=P)
                wg = ffn_w_gate[l].rearrange("(k p) m -> p k m", p=P)
                wu = ffn_w_up[l].rearrange("(k p) m -> p k m", p=P)
                wd = ffn_w_down[l].rearrange("(k p) m -> p k m", p=P)
                with sp.Fori(0, NLOGIT // 2) as i:
                    for j in range(2):
                        load(G_LOGIT[l] + j, wm[:, :, ds(i * 512 + (C_MERGE + 256 * j), 256)], i, 2)
                with sp.Fori(0, NBRANCH // 2) as i:
                    for j in range(2):
                        load(G_BRANCH[l] + j, wb[:, :, ds(i * 512 + 256 * j, 256)], i, 2)
                with sp.Fori(0, NOUT // 2) as i:
                    for j in range(2):
                        load(G_OUT[l] + j, wo[:, :, ds(i * 512 + 256 * j, 256)], i, 2)
                with sp.Fori(0, NGU // 2) as i:
                    for j, w in enumerate((wg, wu)):
                        load(G_GU[l] + j, w[:, :, ds(i * 256, 256)], i, 2)
                with sp.Fori(0, 2) as i:
                    for j in range(6):
                        k = 8 * (j % 3)
                        nk = DOWN_K[j % 3]
                        load(G_DOWN[l] + j, wd[:, k:k + nk, ds(i * 512 + 256 * (j // 3), 256)], i, 6, nk)
            for n in range(4):
                half, b = n // 2, n % 2
                sp.wait_ge(out_rows, n + 1)
                sp.dma_start(out[0, b * P:(b + 1) * P, 512 * half:512 * half + 512],
                             otok[:, b, 512 * half:512 * half + 512]).then_inc(out_stored, 16)
            sp.wait_ge(out_stored, 64)

        @block.tensor
        def _(pe):
            mm = nc.tensor.matmul

            def open_tile(t, i=0, step=0):
                if t >= 2:
                    pe.wait_ge(bank_free[t % 2], t // 2 + i * (step // 2))
                return ring[t % 2]

            def close_tile(last, t):
                last.then_inc(tile_done if SIGNAL[t][0] == "tile" else half_used, SIGNAL[t][2])

            def use_half(g, c, i=0, step=0):
                pe.wait_ge(hi_ready, 2 * g + c + 1 + i * (2 * step))
                pe.wait_ge(lo_ready, 2 * g + c + 1 + i * (2 * step))
                return hi[g % 2], lo[g % 2]

            def product(dst, wh, wl, mh, ml, start, stop):
                mm(dst, wh, mh, start=start, stop=False)
                mm(dst, wh, ml, start=False, stop=False)
                return mm(dst, wl, mh, start=False, stop=stop)

            def features(t, g, c, mh, ml, q0, i=0, step=0, ready=None, mean=None):
                wh, wl = use_half(g, c, i, step)
                ps = open_tile(t, i, 2 * step)
                f = slice(c * P, c * P + P)
                for k in range(KT):
                    if ready:
                        pe.wait_ge(ready[0], ready[2] + k + 1)
                        pe.wait_ge(ready[1], ready[2] + k + 1)
                    last = product(ps[:, 0:T - q0], wh[:, k, f], wl[:, k, f], mh[:, k, q0:], ml[:, k, q0:],
                                   k == 0, k == KT - 1)
                    if mean:
                        mean(k)
                close_tile(last, t)

            def mean_square(l, n, q0):
                t = TILE[l][f"norm{n}"]
                ps = open_tile(t)

                def tile(k):
                    pe.wait_ge(sq_ready[l][n], k + 1)
                    last = mm(ps[:, 0:T - q0], cut["mean"], sq[:, k, q0:], start=k == 0, stop=k == KT - 1)
                    if k == KT - 1:
                        close_tile(last, t)

                if n == 2:
                    return tile
                if n == 0:
                    for k in range(KT):
                        tile(k)
                else:
                    pe.wait_ge(sq_summed[l], n // 2 * (KT - 2) + KT - 2)
                    tile(0)
                    tile(KT - 1)

            def group(l, name):
                g, t, kind = G_MIX[l] + MIX_NO[name], group_tile(l, name), KIND[name]
                if kind != "v":
                    for j in range(TILES_OF[kind]):
                        features(t + j, g, j, xh, xl, 0, ready=(xh_ready[l], xl_ready[l], 0) if name == "small" else None)
                    return
                use_half(g, 0)
                wh, wl = use_half(g, 1)
                for b, tok in enumerate((0, KB1, KB2)):
                    ps = open_tile(t + b)
                    for k in range(KT):
                        last = product(ps[:, 0:256], xh[:, k, tok:tok + P], xl[:, k, tok:tok + P], wh[:, k, :], wl[:, k, :],
                                       k == 0, k == KT - 1)
                    close_tile(last, t + b)

            def gate(l):
                t = TILE[l][("gate",)]
                wait_taken(pe, group_tile(l, "small"))
                close_tile(mm(open_tile(t)[:, 0:T], wgate[:, l, :], M["small"][0:16, :], start=True, stop=True), t)

            def rot(l, i):
                name, t = ("rq", "rk")[i // 2], TILE[l][("rot", i)]
                wait_taken(pe, group_tile(l, name) + i % 2)
                close_tile(mm(open_tile(t)[:, 0:T], cut["perm"], M[name][:, i % 2, :], start=True, stop=True), t)

            def logit(l, j):
                features(TILE[l][("logit", j)], G_LOGIT[l] + j // 2, j % 2, xh, xl, q_start(l))

            def open_scores(l, mix, h):
                j = 4 * mix + h
                if j >= 2:
                    pe.wait_ge(sc_free[l], j - 1)
                return sc[j % 2]

            def open_scores0(l, mix):
                if mix:
                    pe.wait_ge(k0_free[l], mix)
                return k0

            def plain_scores(dst, dst0, qs, ks, h, both, last_start=True):
                i, rows = h // 2, head_rows[h]
                if dst is not None:
                    mm(dst[:, 0:256], ks[rows, i, KB1:KB2], qs[rows, i, KB1:], start=True, stop=both)
                    return mm(dst[:, 256:SCW], ks[rows, i, KB2:], qs[rows, i, KB2:], start=True, stop=both)
                return mm(dst0[quad[h], 0:T], ks[rows, i, 0:32], qs[rows, i, :], start=True, stop=both)

            def scores0(l, mix, qs, ks):
                d = open_scores0(l, mix)
                for h in range(HEADS):
                    last = plain_scores(None, d, qs, ks, h, True)
                last.then_inc(k0_ready[l], 1)

            def scores(l, mix, h, qs, ks):
                plain_scores(open_scores(l, mix, h), None, qs, ks, h, True).then_inc(sc_ready[l], 1)

            def sb_exponent(l, h):
                qs, ks, i, rows = M["sbq"], M["sbk"], h // 2, head_rows[h]
                keep = M["pt"]
                pe.wait_ge(sb_keep0[l], 1)
                pe.wait_ge(sb_keep[l], h + 1)
                mm(e0[quad[h], 0:T], ks[rows, i, 0:32], qs[rows, i, :], start=True, stop=False)
                mm(e0[quad[h], 0:T], cut["negtri0"][quad[h], :], M["pt0"][quad[h], :], start=False, stop=False)
                mm(e0[quad[h], KB1:T], cut["negones"][:, 0:32], keep[:, h, 0:256], start=False, stop=False)
                last0 = mm(e0[quad[h], KB2:T], cut["negones"][:, 0:32], keep[:, h, 256:SCW], start=False, stop=True)
                if h == HEADS - 1:
                    last0.then_inc(e0_ready[l], 1)
                if h:
                    pe.wait_ge(ex_free[l], h)
                mm(ex[:, 0:256], ks[rows, i, KB1:KB2], qs[rows, i, KB1:], start=True, stop=False)
                mm(ex[:, 0:256], cut["negtri"], keep[:, h, 0:256], start=False, stop=False)
                mm(ex[:, 128:256], cut["negones"], keep[:, h, 256:SCW], start=False, stop=True)
                mm(ex[:, 256:SCW], ks[rows, i, KB2:], qs[rows, i, KB2:], start=True, stop=False)
                mm(ex[:, 256:SCW], cut["negtri"], keep[:, h, 256:SCW], start=False, stop=True).then_inc(ex_ready[l], 1)

            def gla_scores0(l):
                d = open_scores0(l, GLA)
                pe.wait_ge(gla_ops[l], 6)
                for h in range(HEADS):
                    mm(d[quad[h], 0:META], M["k00"][quad[h], :], M["q0"][quad[h], :], start=True, stop=True)
                    last = mm(d[quad[h], META:T], M["kr0"][quad[h], 0:32], M["qa"][quad[h], :], start=True, stop=True)
                last.then_inc(k0_ready[l], 1)

            def gla_scores(l, h):
                d = open_scores(l, GLA, h)
                mm(d[:, 0:128], M["kr0"][quad[h], KB1:KB2], M["qa"][quad[h], 0:P], start=True, stop=True)
                mm(d[:, 128:256], M["kr1"][quad[h], 0:P], M["qb"][quad[h], :], start=True, stop=True)
                mm(d[:, 256:SCW], M["kr1"][quad[h], P:], M["qb"][quad[h], :], start=True, stop=True).then_inc(sc_ready[l], 1)

            def ml_exponent0(l):
                pe.wait_ge(ml_dve[l], 10)
                pe.wait_ge(e0_free[l], 1)
                for h in range(HEADS):
                    last = mm(e0[quad[h], 0:T], gl[:, 0:32], gr_rows[:, h, :], start=True, stop=True)
                last.then_inc(e0_ready[l], 1)

            def ml_exponent(l, h):
                pe.wait_ge(ex_free[l], HEADS + h)
                mm(ex[:, 0:256], gl[:, KB1:KB2], gr_rows[:, h, KB1:], start=True, stop=True)
                mm(ex[:, 256:SCW], gl[:, KB2:], gr_rows[:, h, KB2:], start=True, stop=True).then_inc(ex_ready[l], 1)

            def wait_p(l, mix, h):
                if mix == SB:
                    pe.wait_ge(sb_p0[l], 1)
                    pe.wait_ge(sb_p[l], h + 1)
                else:
                    pe.wait_ge(k0_free[l], mix + 1)
                    pe.wait_ge(sc_free[l], 4 * mix + h + 1)

            def ml_den(l):
                pe.wait_ge(e0_free[l], 2)
                den = c3("denind", 4)
                wait_p(l, ML, 0)
                mm(e0[0:4, 0:T], cut["denind0"], M["pt0"][:], start=True, stop=False)
                for h in range(HEADS):
                    wait_p(l, ML, h)
                    mm(e0[0:4, KB1:T], den[:, h, :], M["pt"][:, h, 0:256], start=False, stop=False)
                    last = mm(e0[0:4, KB2:T], den[:, h, :], M["pt"][:, h, 256:SCW], start=False, stop=h == 3)
                last.then_inc(den_ready[l], 1)

            def values(l, mix, pair):
                n = 2 * mix + pair
                if n:
                    pe.wait_ge(o_free[l], n)
                name = [k for k, m in V_OF.items() if m == mix][0]
                for b in range(3):
                    wait_taken(pe, group_tile(l, name) + b)
                for h in (2 * pair, 2 * pair + 1):
                    wait_p(l, mix, h)
                    o = ops[head_rows[h], :]
                    c = slice(h * HD, h * HD + HD)
                    mm(o[:, 0:T], M["v0"][quad_real[h], mix, :], M["pt0"][quad_real[h], :], start=True, stop=False)
                    mm(o[:, KB1:T], M["v"][:, 0, mix, c], M["pt"][:, h, 0:256], start=False, stop=False)
                    last = mm(o[:, KB2:T], M["v"][:, 1, mix, c], M["pt"][:, h, 256:SCW], start=False, stop=True)
                last.then_inc(o_ready[l], 1)

            mq, mk = M["mqk"][:, 0:2, :], M["mqk"][:, 2:4, :]

            def sb_scores0(l):
                for name in ("sbq", "sbk"):
                    for j in range(2):
                        wait_taken(pe, group_tile(l, name) + j)
                scores0(l, SB, M["sbq"], M["sbk"])

            def ml_scores0(l):
                pe.wait_ge(conv_done[l], 4)
                scores0(l, ML, mq, mk)

            def ret_scores0(l):
                pe.wait_ge(rot_done[l], 4)
                scores0(l, RET, M["rq"], M["rk"])

            def headsum(l):
                t = TILE[l][("headsum",)]
                ps = open_tile(t)
                for p in range(6):
                    pe.wait_ge(osq_ready[l], 6)
                    last = mm(ps[0:12, 0:T], c3("headsum", 6)[:, p, :], osq[:, p, :], start=p == 0, stop=p == 5)
                close_tile(last, t)

            def headbc(l, p):
                t = TILE[l][("headbc", p)]
                pe.wait_ge(hrstd_ready[l], 1)
                close_tile(mm(open_tile(t)[:, 0:T], c3("headbc", 6)[0:12, p, :], M["rows"][0:12, 0, :], start=True, stop=True), t)

            parts = {
                "group": group, "gate": gate, "rot": rot, "logit": logit, "headsum": headsum, "headbc": headbc,
                "sb_scores0": sb_scores0, "sb_scores": lambda l, h: scores(l, SB, h, M["sbq"], M["sbk"]),
                "sb_exponent": sb_exponent, "gla_scores0": gla_scores0, "gla_scores": gla_scores,
                "ml_exponent0": ml_exponent0, "ml_exponent": ml_exponent, "ml_scores0": ml_scores0,
                "ml_scores": lambda l, h: scores(l, ML, h, mq, mk), "ml_den": ml_den,
                "ret_scores0": ret_scores0, "ret_scores": lambda l, h: scores(l, RET, h, M["rq"], M["rk"]),
                "values": values,
            }

            def branch(l):
                q0 = q_start(l)
                for b in range(2):
                    wait_taken(pe, TILE[l][("logit", 2 * NLOGIT - 1)] - b)
                pe.wait_ge(yh_ready[l], 8)
                pe.wait_ge(yl_ready[l], 8)
                for m in range(KT):
                    wh, wl = use_half(G_BRANCH[l] + m // 2, m % 2)
                    if m >= 2:
                        pe.wait_ge(branch_free[l], m - 1)
                    c = m % 2 * P
                    for n in range(4):
                        for k in range(2):
                            last = product(branch_banks[m % 2][:, n, 0:T - q0], wh[:, 2 * n + k, c:c + P], wl[:, 2 * n + k, c:c + P],
                                           yh[:, 2 * n + k, q0:], yl[:, 2 * n + k, q0:], k == 0, k == 1)
                    last.then_inc(half_used, 1)

            def output(l):
                q0, g, t = q_start(l), G_OUT[l], TILE[l]["out"]
                pe.wait_ge(branch_free[l], KT - 1)
                with pe.Fori(0, NOUT // 2) as i:
                    for j in range(2):
                        for c in range(2):
                            features(t + 2 * j + c, g + j, c, xh, xl, q0, i, 2, (mh_ready[l], ml_ready[l], 0) if j + c == 0 else None)

            def gate_up(l):
                q0, g, t = q_start(l), G_GU[l], TILE[l]["gu"]
                mean = mean_square(l, 2, q0)
                for j in range(2):
                    for c in range(2):
                        first = (j, c) == (0, 0)
                        features(t + 2 * j + c, g + j, c, xh, xl, q0, ready=(xh_ready[l], xl_ready[l], KT) if first else None, mean=mean if first else None)
                with pe.Fori(0, NGU // 2 - 1) as i:
                    for j in range(2, 4):
                        for c in range(2):
                            features(t + 2 * j + c, g + j, c, xh, xl, q0, i, 2)

            def down(l):
                q0, g, t = q_start(l), G_DOWN[l], TILE[l]["down"]
                with pe.Fori(0, 2) as i:
                    for j in range(6):
                        n = DOWN_K[j % 3]
                        for c in range(2):
                            wh, wl = use_half(g + j, c, i, 6)
                            tt = t + 2 * (j // 3) + c
                            ps = open_tile(tt, i, 4) if j % 3 == 0 else ring[tt % 2]
                            if j < 3 and c == 0:
                                pe.wait_ge(ah_ready[l], 8 * j + n)
                                pe.wait_ge(al_ready[l], 8 * j + n)
                            for k in range(n):
                                kk = 8 * (j % 3) + k
                                last = product(ps[:, 0:T - q0], wh[:, k, c * P:c * P + P], wl[:, k, c * P:c * P + P],
                                               ah[:, kk, q0:], al[:, kk, q0:], kk == 0, kk == FT - 1)
                            if j % 3 == 2:
                                close_tile(last, tt)
                            else:
                                last.then_inc(half_used, 1)

            pe.wait_ge(first_loaded, 16)
            pe.wait_ge(meta_loaded, 16)
            for k in range(KT):
                pe.wait_ge(x_loaded[k // 4], 16)
                ps = open_tile(k)
                f = slice(k * P, k * P + P)
                nc.tensor.transpose(ps[:, 0:META], xt[0:META, 0, f], cut["ident"][0:META, 0:META])
                nc.tensor.transpose(ps[:, KB1:KB2], xt[:, 1, f], cut["ident"])
                close_tile(nc.tensor.transpose(ps[:, KB2:T], xt[:, 2, f], cut["ident"]), k)
            pe.wait_ge(par_loaded, 16 * 11)
            for l in range(DEPTH):
                t = KT + l
                close_tile(nc.tensor.transpose(open_tile(t)[:, 0:NPAR], prows[:, l, :], cut["ident"][0:NPAR, 0:NPAR]), t)
            for l in range(DEPTH):
                mean_square(l, 0, 0)
                if l == 0:
                    pe.wait_ge(const_loaded, 16)
                run_steps(l, parts)
                branch(l)
                output(l)
                mean_square(l, 1, q_start(l))
                gate_up(l)
                down(l)
                mean_square(l, 3, q_start(l))
            for n, ps in enumerate((sc[0], sc[1], ex, k0)):
                half, b = n // 2, n % 2
                for c in range(4):
                    pe.wait_ge(h_ready[DEPTH - 1], KT + 4 * half + c + 1)
                    last = nc.tensor.transpose(ps[:, c * P:c * P + P], hT[:, 4 * half + c, META + b * P:META + b * P + P], cut["ident"])
                close_tile(last, TILE_OUT + n)

        @block.scalar
        def _(act):
            fn = nc.scalar.activation

            def round_half(n, i=0, step=0):
                if n >= 2 * G_END:
                    return
                g, c, k = n // 2, n % 2 * P, group_k(n // 2)
                act.wait_ge(raw_loaded[g % 2], 16 * (g // 2 + 1) + i * (4 * step))
                if g in G_MIX:
                    act.wait_ge(small_loaded, 32 * (G_MIX.index(g) + 1))
                if n >= 4:
                    act.wait_ge(half_used, n - 3 + i * step)
                fn(hi[g % 2][:, 0:k, c:c + P], raw[g % 2][:, 0:k, c:c + P], ACT.Copy).then_inc(hi_ready, 1)

            def taken(ins, t):
                ins.then_inc(bank_free[t % 2], 1)

            def square_h(l, n, k, q0):
                if n == 2:
                    act.wait_ge(h_ready[l], k + 1)
                elif l:
                    act.wait_ge(h_ready[l - 1], KT + k + 1)
                else:
                    wait_taken(act, k)
                fn(sq[:, k, q0:], hT[:, k, q0:], ACT.Square).then_inc(sq_ready[l][n], 1)

            def root(l, n, q0):
                t = TILE[l][f"norm{n}"]
                wait_tile(act, t)
                taken(fn(rstd[:, q0:], ring[t % 2][:, 0:T - q0], ACT.Ln, bias=cut["eps"]), t)
                wait_taken(act, t)
                fn(rstd[:, q0:], rstd[:, q0:], ACT.Exp, scale=-0.5).then_inc(rstd_ready[l], 1)

            def round_x(l):
                for k in range(KT):
                    act.wait_ge(xn_ready[l], k + 1)
                    fn(xh[:, k, :], sq[:, k, :], ACT.Copy).then_inc(xh_ready[l], 1)

            def round_ffn_x(l, q0):
                for k in range(KT):
                    act.wait_ge(h_ready[l], k + 1)
                    fn(xh[:, k, q0:], hT[:, k, q0:], ACT.Copy, scale=par[:, l, R_FFNPRE + k:R_FFNPRE + k + 1]).then_inc(xh_ready[l], 1)
                    square_h(l, 2, k, q0)

            def group(l, name):
                kind, t = KIND[name], group_tile(l, name)
                half = 2 * (G_MIX[l] + MIX_NO[name]) + ROUND_AHEAD
                if kind == "v":
                    round_half(half)
                    round_half(half + 1)
                    return
                for j in range(TILES_OF[kind]):
                    wait_tile(act, t + j)
                    ps = ring[(t + j) % 2][:, 0:T]
                    if name == "small":
                        ins = fn(M["small"][:], ps, ACT.Identity, bias=ifbias[:, l:l + 1])
                    elif name in ("mqk0", "mqk1"):
                        ins = fn(M["conv_in"][:, 2 * int(name[3]) + j, 3:], ps, ACT.Copy)
                    elif name == "gqk":
                        ins = fn((M["gq"], M["gk"])[j][:], ps, ACT.Copy, scale=(HD // 2) ** -0.5 if j == 0 else 1.0)
                    elif name in ("gr", "rg"):
                        ins = fn(M[name][:, j, :], ps, ACT.Silu)
                    elif name == "sbq":
                        ins = fn(M["sbq"][:, j, :], ps, ACT.Copy, scale=HD ** -0.5)
                    else:
                        ins = fn(M[name][:, j, :], ps, ACT.Copy)
                    taken(ins, t + j)
                    round_half(half + j)
                if kind == "small":
                    round_half(half + 1)

            def logit(l, j):
                q0, t = q_start(l), TILE[l][("logit", j)]
                wait_tile(act, t)
                taken(fn(gates[:, j, q0:], ring[t % 2][:, 0:T - q0], ACT.Sigmoid if j >= SIGMOID_FROM else ACT.Identity,
                         bias=par[:, l, R_BMERGE + j:R_BMERGE + j + 1]), t)
                round_half(2 * G_LOGIT[l] + j + ROUND_AHEAD)

            def mo_sigmoid(l):
                for j in range(2):
                    wait_taken(act, group_tile(l, "mo") + j)
                fn(M["mo"][:], M["mo"][:], ACT.Sigmoid).then_inc(mo_ready[l], 1)

            def gate_sigmoid(l, n):
                for j in (4 * n + 2, 4 * n + 3):
                    wait_taken(act, TILE[l][("logit", j)])
                v = gates[:, 4 * n:4 * n + 4, q_start(l):]
                fn(v, v, ACT.Sigmoid).then_inc(gates_ready[l], 1)

            def gate(l):
                t = TILE[l][("gate",)]
                wait_tile(act, t)
                taken(fn(M["gwork"][:], ring[t % 2][:, 0:T], ACT.Identity, bias=par[:, l, R_BGATE:R_BGATE + 1]), t)

            def conv_silu(l):
                for t in range(4):
                    act.wait_ge(conv_step[l], 12 + t + 1)
                    fn(M["mqk"][:, t, :], M["mqk"][:, t, :], ACT.Silu).then_inc(conv_done[l], 1)

            def softplus_part(dst, src, done, n, first_wait=None):
                if first_wait:
                    act.wait_ge(*first_wait)
                fn(dst, src, ACT.Abs).then_inc(done, 1)
                act.wait_ge(done, n + 1)
                fn(dst, dst, ACT.Exp, scale=-1.0).then_inc(done, 1)
                act.wait_ge(done, n + 2)
                fn(dst, dst, ACT.Ln, bias=1.0).then_inc(done, 1)

            def gla_soft_(l):
                softplus_part(M["gwork2"][:], M["gwork"][:], gla_soft[l], 0,
                              (bank_free[TILE[l][("gate",)] % 2], TILE[l][("gate",)] // 2 + 1))

            def ml_soft_(l):
                t = group_tile(l, "small")
                softplus_part(M["rows"][64:68, 0, :], M["small"][64:68, :], ml_soft[l], 0, (bank_free[t % 2], t // 2 + 1))

            def gla_exp_(l):
                act.wait_ge(gla_dve[l], 6)
                s = 1.0 / GLA_NORMALIZER
                cum, ref = M["cum"], glaref
                for dst, src, scale, bias in ((M["qa"], cum[:, KB1:], s, ref[:, 0:1]), (M["qb"], cum[:, KB2:], s, ref[:, 1:2]),
                                              (M["q0"], cum[:, 0:META], s, 0.0), (M["kr0"], cum[:, 0:KB2], -s, ref[:, 2:3]),
                                              (M["kr1"], cum[:, KB1:], -s, ref[:, 3:4]), (M["k00"], cum[:, 0:32], -s, 0.0)):
                    fn(dst[:], src, ACT.Exp, scale=scale, bias=bias).then_inc(gla_exp[l], 1)

            def ml_em_(l):
                act.wait_ge(ml_dve[l], 11)
                fn(M["rows"][0:4, 1, :], M["rows"][32:36, 0, :], ACT.Exp, scale=-1.0).then_inc(ml_em[l], 1)

            def take_out(l, n):
                act.wait_ge(o_ready[l], n + 1)
                fn(M["osb"][:, n, :], ops[:, 0:T], ACT.Copy).then_inc(o_free[l], 1)

            def sb_soft0(l):
                softplus_part(M["cum"][:], k0[:, 0:T], sb_soft[l], 0, (k0_ready[l], 1))

            def sb_soft_(l, h):
                softplus_part(M["sb2"][:, h % 2, :], sc[h % 2][:, 0:SCW], sb_soft[l], 3 * (h + 1), (sc_ready[l], h + 1))

            def sb_p_(l, h):
                act.wait_ge(ex_free[l], h + 1)
                fn(M["pt"][:, h, :], M["sa"][:, h % 2, :], ACT.Exp).then_inc(sb_p[l], 1)

            def sb_p0_(l):
                act.wait_ge(e0_free[l], 1)
                fn(M["pt0"][:], M["cum"][:], ACT.Exp).then_inc(sb_p0[l], 1)

            def ml_w0(l):
                act.wait_ge(e0_free[l], 2)
                fn(M["gwork2"][:], M["gwork"][:], ACT.Exp).then_inc(ml_w[l], 1)

            def ml_w_(l, h):
                act.wait_ge(ex_free[l], HEADS + h + 1)
                if h >= 2:
                    act.wait_ge(sc_free[l], 4 * ML + h - 1)
                fn(M["sb2"][:, h % 2, :], M["sa"][:, h % 2, :], ACT.Exp).then_inc(ml_w[l], 1)

            def den_abs_(l):
                act.wait_ge(den_ready[l], 1)
                act.wait_ge(ml_em[l], 1)
                fn(M["rows"][0:4, 0, :], e0[0:4, 0:T], ACT.Abs).then_inc(den_abs[l], 1)

            def head_square(l, p):
                n = NORM_ORDER[p]
                act.wait_ge(o_free[l], n + 1)
                fn(osq[:, p, :], M["osb"][:, n, :], ACT.Square).then_inc(osq_ready[l], 1)

            def head_rstd(l):
                r = M["rows"][0:12, 0, :]
                wait_taken(act, TILE[l][("headsum",)])
                fn(r, r, ACT.Ln).then_inc(hlog_ready[l], 1)
                act.wait_ge(hlog_ready[l], 1)
                fn(r, r, ACT.Exp, scale=-0.5).then_inc(hrstd_ready[l], 1)

            def round_y(l, n):
                fn(yh[:, n, :], M["osb"][:, n, :], ACT.Copy).then_inc(yh_ready[l], 1)

            def y_plain(l):
                for n in range(2):
                    act.wait_ge(o_free[l], n + 1)
                    round_y(l, n)

            def y_rest(l, p):
                act.wait_ge(y_step[l], p + 1)
                round_y(l, NORM_ORDER[p])

            def tables(name):
                return lambda l: nc.scalar.preload_act_table_set(name)

            parts = {
                "group": group, "logit": logit, "gate_sigmoid": gate_sigmoid, "gate": gate, "conv_silu": conv_silu,
                "gla_soft": gla_soft_, "ml_soft": ml_soft_, "gla_exp": gla_exp_, "ml_em": ml_em_, "take_out": take_out,
                "sb_soft0": sb_soft0, "sb_soft": sb_soft_, "sb_p": sb_p_, "sb_p0": sb_p0_, "ml_w0": ml_w0, "ml_w": ml_w_,
                "den_abs": den_abs_, "head_square": head_square, "head_rstd": head_rstd, "mo_sigmoid": mo_sigmoid, "y_plain": y_plain, "y_rest": y_rest,
                "exp_tables": tables("natural_log_exp_and_others"), "silu_tables": tables("silu_and_others"),
                "sigmoid_tables": tables("sigmoid_and_others"),
            }

            def branch(l):
                q0 = q_start(l)

                def round_merged(m):
                    act.wait_ge(merge_step[l], m + 1)
                    fn(xh[:, m, q0:], acc[:, m % 2, q0:], ACT.Copy).then_inc(mh_ready[l], 1)

                for m in range(KT):
                    round_half(2 * G_BRANCH[l] + m + ROUND_AHEAD)
                    if m:
                        round_merged(m - 1)
                round_merged(KT - 1)

            def take_sublayer(l, n, t, m, q0, i=0, step=0):
                wait_tile(act, t, i, step)
                k = ds(i * step + m, 1) if step else slice(m, m + 1)
                ps = ring[t % 2][:, 0:T - q0]
                fn(sq[:, k, q0:], ps, ACT.Square).then_inc(sq_ready[l][n], 1)
                taken(fn(sub[:, k, q0:], ps, ACT.Copy), t)

            def output(l):
                q0, t = q_start(l), TILE[l]["out"]
                with act.Fori(0, KT // 4) as i:
                    for m in range(4):
                        take_sublayer(l, 1, t + m, m, q0, i, 4)
                        round_half(2 * G_OUT[l] + m + ROUND_AHEAD, i, 4)

            def gate_up(l):
                q0, n, t = q_start(l), 2 * G_GU[l] + ROUND_AHEAD, TILE[l]["gu"]
                with act.Fori(0, NGU // 2) as i:
                    for c in range(2):
                        wait_taken(act, t + c, i, 4)
                        v = silu_g[:, c, q0:]
                        fn(v, v, ACT.Silu).then_inc(silu_ready[l], 1)
                        round_half(n + c, i, 4)
                    for c in range(2):
                        wait_taken(act, t + 2 + c, i, 4)
                        fn(ah[:, ds(i * 2 + c, 1), q0:], prod[:, c, q0:], ACT.Copy).then_inc(ah_ready[l], 1)
                        round_half(n + 2 + c, i, 4)

            def down(l):
                q0, g, t = q_start(l), G_DOWN[l], TILE[l]["down"]
                for j in range(NDOWN):
                    for c in range(2):
                        if j % 3 == 2:
                            m = 2 * (j // 3) + c
                            take_sublayer(l, 3, t + m, m, q0)
                        round_half(2 * (g + j) + c + ROUND_AHEAD)

            act.dma_start(const[:, 0:CONST_FIRST], consts[:, 0:CONST_FIRST]).then_inc(first_loaded, 16)
            for r, src in ((R_MIXPRE, norm_mix_pre), (R_MIXPOST, norm_mix_post), (R_FFNPRE, norm_ffn_pre),
                           (R_FFNPOST, norm_ffn_post), (R_BGATE, gla_b_gate), (R_GLAN, gla_norm),
                           (R_MLN, ml_norm), (R_RETN, ret_norm)):
                n = src.shape[1] // P
                act.dma_start(prows[r:r + n, :, :], src.rearrange("l (a p) -> a l p", p=P)).then_inc(par_loaded, 16)
            act.dma_start(prows[R_CONV:R_CONV + 16, :, :], ml_conv.rearrange("l j (a p) -> (j a) l p", p=P)).then_inc(par_loaded, 16)
            act.dma_start(prows[R_BMERGE:NPAR, :, :], b_merge.rearrange("l n (a p) -> (n a) l p", p=P)).then_inc(par_loaded, 16)
            act.dma_start(wgate[:], gla_w_gate_up.rearrange("l r m -> r l m")).then_inc(par_loaded, 16)
            act.wait_ge(misc_set, 1)
            act.dma_start(ifbias[32:36, :], ml_b_i.rearrange("l h -> h l"), allow_slow_non_contiguous=True).then_inc(bias_loaded, 16)
            act.dma_start(ifbias[64:68, :], ml_b_f.rearrange("l h -> h l"), allow_slow_non_contiguous=True).then_inc(bias_loaded, 16)
            act.wait_ge(first_loaded, 16)
            exp_tables = tables("natural_log_exp_and_others")
            for l in range(DEPTH):
                q0 = q_start(l)
                if l == 0:
                    exp_tables(l)
                for k in range(KT):
                    square_h(l, 0, k, 0)
                if l == 0:
                    round_half(0)
                    act.dma_start(const[:, CONST_FIRST:], consts[:, CONST_FIRST:]).then_inc(const_loaded, 16)
                root(l, 0, 0)
                round_x(l)
                if l == 0:
                    for n in range(1, ROUND_AHEAD):
                        round_half(n)
                    act.wait_ge(bias_loaded, 32)
                run_steps(l, parts)
                branch(l)
                exp_tables(l)
                output(l)
                root(l, 1, q0)
                round_ffn_x(l, q0)
                root(l, 2, q0)
                tables("silu_and_others")(l)
                gate_up(l)
                exp_tables(l)
                down(l)
                root(l, 3, q0)
            for n, ps in enumerate((sc[0], sc[1], ex, k0)):
                half, b = n // 2, n % 2
                wait_tile(act, TILE_OUT + n)
                fn(otok[:, b, 512 * half:512 * half + 512], ps, ACT.Copy).then_inc(out_rows, 1)

        @block.vector
        def _(dve):
            tt, ts, stt = nc.vector.tensor_tensor, nc.vector.tensor_scalar, nc.vector.scalar_tensor_tensor
            scan = nc.vector.tensor_tensor_scan

            def rest_of_half(n, i=0, step=0):
                if n >= 2 * G_END:
                    return
                g, c, k = n // 2, n % 2 * P, group_k(n // 2)
                dve.wait_ge(hi_ready, n + 1 + i * step)
                tt(lo[g % 2][:, 0:k, c:c + P], raw[g % 2][:, 0:k, c:c + P], hi[g % 2][:, 0:k, c:c + P].bitcast(F32), ALU.subtract).then_inc(lo_ready, 1)

            def taken(ins, t):
                ins.then_inc(bank_free[t % 2], 1)

            def pre_norm(l):
                dve.wait_ge(rstd_ready[l], 1)
                for k in range(KT):
                    stt(sq[:, k, :], hT[:, k, :], par[:, l, R_MIXPRE + k:R_MIXPRE + k + 1], rstd[:], ALU.mult, ALU.mult).then_inc(xn_ready[l], 1)

            def post_norm(l, n, q0, row, behind=None):
                dve.wait_ge(rstd_ready[l], n + 1)
                for k in range(KT):
                    stt(sub[:, k, q0:], sub[:, k, q0:], par[:, l, row + k:row + k + 1], rstd[:, q0:], ALU.mult, ALU.mult).then_inc(post_scaled[l], 1)
                    if behind and k >= 3:
                        behind(k - 3)
                if behind:
                    for k in range(KT - 3, KT):
                        behind(k)

            def rest_of_ffn_x(l, q0):
                def tile(k):
                    dve.wait_ge(xh_ready[l], KT + k + 1)
                    stt(xl[:, k, q0:], hT[:, k, q0:], par[:, l, R_FFNPRE + k:R_FFNPRE + k + 1], xh[:, k, q0:].bitcast(F32),
                        ALU.mult, ALU.subtract).then_inc(xl_ready[l], 1)
                return tile

            def group(l, name):
                g, t, kind = G_MIX[l] + MIX_NO[name], group_tile(l, name), KIND[name]
                if name == "small":
                    nc.vector.memset(M["conv_in"][:, :, 0:3], 0.0).then_inc(pad_set[l], 1)
                rest_of_half(2 * g + REST_AHEAD)
                if kind != "v":
                    rest_of_half(2 * g + REST_AHEAD + 1)
                    return
                mix = V_OF[name]
                wait_tile(dve, t)
                for h in range(HEADS):
                    ins = nc.vector.tensor_copy(M["v0"][quad_real[h], mix, :], ring[t % 2][0:META, h * HD:h * HD + HD])
                taken(ins, t)
                for b in range(2):
                    wait_tile(dve, t + 1 + b)
                    taken(nc.vector.tensor_copy(M["v"][:, b, mix, :], ring[(t + 1 + b) % 2][:, 0:256]), t + 1 + b)
                rest_of_half(2 * g + REST_AHEAD + 1)

            def logit(l, j):
                rest_of_half(2 * G_LOGIT[l] + j + REST_AHEAD)

            def rot(l, i):
                name, t = ("rq", "rk")[i // 2], TILE[l][("rot", i)]
                v = M[name][:, i % 2, :]
                turned = M["sa"][:, i % 2, 0:T]
                wait_tile(dve, t)
                taken(tt(turned, ring[t % 2][:, 0:T], cut["sin"], ALU.mult), t)
                tt(v, v, cut["cos"], ALU.mult).then_inc(rot_cos[l], 1)
                wait_taken(dve, t)
                dve.wait_ge(rot_cos[l], i + 1)
                tt(v, v, turned, ALU.add).then_inc(rot_done[l], 1)

            def conv(l, j):
                if j == 0:
                    for name in ("mqk0", "mqk1"):
                        for c in range(2):
                            wait_taken(dve, group_tile(l, name) + c)
                    dve.wait_ge(pad_set[l], 1)
                for t in range(4):
                    tap = par[:, l, R_CONV + 4 * j + t:R_CONV + 4 * j + t + 1]
                    src = M["conv_in"][:, t, j:j + T]
                    if j == 0:
                        ts(M["mqk"][:, t, :], src, tap, None, ALU.mult).then_inc(conv_step[l], 1)
                    else:
                        dve.wait_ge(conv_step[l], 4 * (j - 1) + t + 1)
                        stt(M["mqk"][:, t, :], src, tap, M["mqk"][:, t, :], ALU.mult, ALU.add).then_inc(conv_step[l], 1)

            def gla_log(l):
                dve.wait_ge(gla_soft[l], 3)
                stt(M["gwork"][:], M["gwork"][:], 0.0, M["gwork2"][:], ALU.min, ALU.subtract).then_inc(gla_dve[l], 1)
                dve.wait_ge(gla_dve[l], 1)
                dve.wait_ge(sb_p0[l], 1)
                scan(M["cum"][:], ones[:], M["gwork"][:], 0.0, ALU.mult, ALU.add).then_inc(gla_dve[l], 1)
                dve.wait_ge(gla_dve[l], 2)
                for c, (at_, s) in enumerate(((KB1 - 1, -1), (KB2 - 1, -1), (KB1 - 1, 1), (KB2 - 1, 1))):
                    ts(glaref[:, c:c + 1], M["cum"][:, at_:at_ + 1], s / GLA_NORMALIZER, None, ALU.mult).then_inc(gla_dve[l], 1)

            def ml_rows(l):
                rows, small = M["rows"], M["small"]
                dve.wait_ge(ml_soft[l], 3)
                stt(rows[64:68, 1, :], small[64:68, :], 0.0, rows[64:68, 0, :], ALU.min, ALU.subtract).then_inc(ml_dve[l], 1)
                dve.wait_ge(ml_dve[l], 1)
                scan(rows[64:68, 2, :], ones[64:68, :], rows[64:68, 1, :], 0.0, ALU.mult, ALU.add).then_inc(ml_dve[l], 1)
                dve.wait_ge(ml_dve[l], 2)
                nc.vector.tensor_copy(rows[32:36, 0, :], rows[64:68, 2, :]).then_inc(ml_dve[l], 1)
                dve.wait_ge(ml_dve[l], 3)
                tt(rows[32:36, 1, :], small[32:36, :], rows[32:36, 0, :], ALU.subtract).then_inc(ml_dve[l], 1)
                dve.wait_ge(ml_dve[l], 4)
                scan(rows[32:36, 2, :], rows[32:36, 1, :], rows[32:36, 1, :], 0.0, ALU.max, ALU.max).then_inc(ml_dve[l], 1)
                dve.wait_ge(ml_dve[l], 5)
                nc.vector.tensor_copy(gl[0:4, :], rows[32:36, 1, :]).then_inc(ml_dve[l], 1)
                for h in range(HEADS):
                    ts(gr_rows[32:36, h, :], rows[32:36, 2, :], cut["negind"][32:36, h:h + 1], None, ALU.mult).then_inc(ml_dve[l], 1)
                tt(rows[32:36, 0, :], rows[32:36, 0, :], rows[32:36, 2, :], ALU.add).then_inc(ml_dve[l], 1)

            def gla_decay(l):
                for n, (dst, src, c) in enumerate(((M["qa"], M["gq"], KB1), (M["qb"], M["gq"], KB2), (M["q0"], M["gq"], 0),
                                                   (M["kr0"], M["gk"], 0), (M["kr1"], M["gk"], KB1), (M["k00"], M["gk"], 0))):
                    dve.wait_ge(gla_exp[l], n + 1)
                    tt(dst[:], dst[:], src[:, c:c + dst.shape[1]], ALU.mult).then_inc(gla_ops[l], 1)

            def wait_spent(l, mix, pair):
                dve.wait_ge(o_ready[l], 2 * (mix - 1) + pair + 1)

            def sb_keep_head(l, h):
                dve.wait_ge(sb_soft[l], 3 * (h + 2))
                stt(M["pt"][:, h, :], sc[h % 2][:, 0:SCW], 0.0, M["sb2"][:, h % 2, :], ALU.max, ALU.add).then_inc(sc_free[l], 1)
                dve.wait_ge(sc_free[l], h + 1)
                tt(M["pt"][:, h, :], M["pt"][:, h, :], cut["mask_lt"], ALU.mult).then_inc(sb_keep[l], 1)

            pt, pt0, sa = M["pt"], M["pt0"], M["sa"]

            def sb_keep0_(l):
                dve.wait_ge(sb_soft[l], 3)
                stt(pt0[:], k0[:, 0:T], 0.0, M["cum"][:], ALU.max, ALU.add).then_inc(k0_free[l], 1)
                dve.wait_ge(k0_free[l], 1)
                tt(pt0[:], pt0[:], cut["mask_lt0"], ALU.mult).then_inc(sb_keep0[l], 1)

            def sb_mask(l, h):
                dve.wait_ge(ex_ready[l], h + 1)
                if h >= 2:
                    dve.wait_ge(sb_p[l], h - 1)
                stt(sa[:, h % 2, :], ex[:, 0:SCW], 0.0, cut["neg_lt"], ALU.min, ALU.add).then_inc(ex_free[l], 1)

            def sb_mask0(l):
                dve.wait_ge(e0_ready[l], 1)
                stt(M["cum"][:], e0[:, 0:T], 0.0, cut["neg_lt0"], ALU.min, ALU.add).then_inc(e0_free[l], 1)

            def gla_p0(l):
                dve.wait_ge(k0_ready[l], GLA + 1)
                wait_spent(l, GLA, 1)
                tt(pt0[:], k0[:, 0:T], cut["mask_le0"], ALU.mult).then_inc(k0_free[l], 1)

            def gla_p(l, h):
                j = 4 * GLA + h
                dve.wait_ge(sc_ready[l], j + 1)
                wait_spent(l, GLA, h // 2)
                tt(pt[:, h, :], sc[j % 2][:, 0:SCW], cut["mask_le"], ALU.mult).then_inc(sc_free[l], 1)

            def ml_mask0(l):
                dve.wait_ge(e0_ready[l], 2)
                stt(M["gwork"][:], e0[:, 0:T], 0.0, cut["neg_le0"], ALU.min, ALU.add).then_inc(e0_free[l], 1)

            def ml_mask(l, h):
                dve.wait_ge(ex_ready[l], HEADS + h + 1)
                dve.wait_ge(sb_p[l], 4)
                if h >= 2:
                    dve.wait_ge(ml_w[l], h)
                stt(sa[:, h % 2, :], ex[:, 0:SCW], 0.0, cut["neg_le"], ALU.min, ALU.add).then_inc(ex_free[l], 1)

            def ml_p0(l):
                dve.wait_ge(k0_ready[l], ML + 1)
                dve.wait_ge(ml_w[l], 1)
                wait_spent(l, ML, 1)
                stt(pt0[:], k0[:, 0:T], ML_SCALE, M["gwork2"][:], ALU.mult, ALU.mult).then_inc(k0_free[l], 1)

            def ml_p(l, h):
                j = 4 * ML + h
                dve.wait_ge(sc_ready[l], j + 1)
                dve.wait_ge(ml_w[l], h + 2)
                wait_spent(l, ML, h // 2)
                stt(pt[:, h, :], sc[j % 2][:, 0:SCW], ML_SCALE, M["sb2"][:, h % 2, :], ALU.mult, ALU.mult).then_inc(sc_free[l], 1)

            def den_square(l):
                dve.wait_ge(den_abs[l], 1)
                tt(M["rows"][0:4, 2, :], M["rows"][0:4, 0, :], M["rows"][0:4, 1, :], ALU.max).then_inc(den_dve[l], 1)
                dve.wait_ge(den_dve[l], 1)
                tt(dm2[0:4, :], M["rows"][0:4, 2, :], M["rows"][0:4, 2, :], ALU.mult).then_inc(den_dve[l], 1)

            def ret_p0(l):
                wait_spent(l, RET, 1)
                dve.wait_ge(k0_ready[l], RET + 1)
                tt(pt0[:], k0[:, 0:T], cut["decay0"], ALU.mult).then_inc(k0_free[l], 1)

            def ret_p(l, h):
                j = 4 * RET + h
                dve.wait_ge(sc_ready[l], j + 1)
                wait_spent(l, RET, h // 2)
                tt(pt[:, h, :], sc[j % 2][:, 0:SCW], c3("decay", 4)[:, h, :], ALU.mult).then_inc(sc_free[l], 1)

            def head_var(l):
                t = TILE[l][("headsum",)]
                wait_tile(dve, t)
                dve.wait_ge(den_dve[l], 2)
                taken(stt(M["rows"][0:12, 0, :], dm2[:], EPS, ring[t % 2][0:12, 0:T], ALU.mult, ALU.add), t)

            def rest_of_y(l, i, n):
                dve.wait_ge(yh_ready[l], i + 1)
                tt(yl[:, n, :], M["osb"][:, n, :], yh[:, n, :].bitcast(F32), ALU.subtract).then_inc(yl_ready[l], 1)

            def y_plain(l):
                rest_of_y(l, 0, 0)
                rest_of_y(l, 1, 1)

            def y_rest(l, p):
                osb, n, t = M["osb"], NORM_ORDER[p], TILE[l][("headbc", p)]
                row, gate = {GLA: (R_GLAN, "gr"), ML: (R_MLN, "mo"), RET: (R_RETN, "rg")}[n // 2]
                wait_tile(dve, t)
                taken(stt(osb[:, n, :], osb[:, n, :], par[:, l, row + n % 2:row + n % 2 + 1], ring[t % 2][:, 0:T], ALU.mult, ALU.mult), t)
                wait_taken(dve, t)
                if gate == "mo":
                    dve.wait_ge(mo_ready[l], 1)
                tt(osb[:, n, :], osb[:, n, :], M[gate][:, n % 2, :], ALU.mult).then_inc(y_step[l], 1)
                rest_of_y(l, p + 2, n)

            parts = {
                "group": group, "logit": logit, "rot": rot, "conv": conv, "gla_log": gla_log, "gla_decay": gla_decay,
                "ml_rows": ml_rows, "sb_keep0": sb_keep0_, "sb_keep": sb_keep_head, "sb_mask": sb_mask, "sb_mask0": sb_mask0,
                "gla_p0": gla_p0, "gla_p": gla_p, "ml_mask0": ml_mask0, "ml_mask": ml_mask, "ml_p0": ml_p0, "ml_p": ml_p,
                "den_square": den_square, "ret_p0": ret_p0, "ret_p": ret_p, "head_var": head_var,
                "y_plain": y_plain, "y_rest": y_rest,
            }

            def branch(l):
                q0 = q_start(l)
                dve.wait_ge(gates_ready[l], SIGMOID_FROM // 4)
                for b in range(2):
                    wait_taken(dve, TILE[l][("logit", 2 * NLOGIT - 1 - b)])

                def rest_of_merged(m):
                    dve.wait_ge(mh_ready[l], m + 1)
                    tt(xl[:, m, q0:], acc[:, m % 2, q0:], xh[:, m, q0:].bitcast(F32), ALU.subtract).then_inc(ml_ready[l], 1)

                by_branch = gates[:].rearrange("p (n m) t -> p n m t", n=4)
                for m in range(KT):
                    dve.wait_ge(half_used, 2 * G_BRANCH[l] + m + 1)
                    if m >= 2:
                        dve.wait_ge(merge_step[l], m - 1)
                    tt(term[:, m % 2, :, q0:], branch_banks[m % 2][:, :, 0:T - q0], by_branch[:, :, m, q0:], ALU.mult).then_inc(branch_free[l], 1)
                    rest_of_half(2 * G_BRANCH[l] + m + REST_AHEAD)
                    if m:
                        rest_of_merged(m - 1)
                rest_of_merged(KT - 1)

            def output(l):
                with dve.Fori(0, KT // 4) as i:
                    for m in range(4):
                        rest_of_half(2 * G_OUT[l] + m + REST_AHEAD, i, 4)

            def gate_up(l):
                q0, n, t = q_start(l), 2 * G_GU[l] + REST_AHEAD, TILE[l]["gu"]
                dve.wait_ge(rstd_ready[l], 3)
                with dve.Fori(0, NGU // 2) as i:
                    for c in range(2):
                        wait_tile(dve, t + c, i, 4)
                        dve.wait_ge(bank_free[(t + c) % 2], (t + c) // 2 + i * 2)
                        taken(tt(silu_g[:, c, q0:], ring[(t + c) % 2][:, 0:T - q0], rstd[:, q0:], ALU.mult), t + c)
                        rest_of_half(n + c, i, 4)
                    for c in range(2):
                        wait_tile(dve, t + 2 + c, i, 4)
                        dve.wait_ge(silu_scaled[l], c + 1 + i * 2)
                        taken(tt(prod[:, c, q0:], ring[(t + c) % 2][:, 0:T - q0], silu_g[:, c, q0:], ALU.mult), t + 2 + c)
                        rest_of_half(n + 2 + c, i, 4)
                        dve.wait_ge(ah_ready[l], c + 1 + i * 2)
                        tt(al[:, ds(i * 2 + c, 1), q0:], prod[:, c:c + 1, q0:], ah[:, ds(i * 2 + c, 1), q0:].bitcast(F32), ALU.subtract).then_inc(al_ready[l], 1)

            def down(l):
                for j in range(2 * NDOWN):
                    rest_of_half(2 * G_DOWN[l] + j + REST_AHEAD)

            nc.vector.memset(ifbias[:], 0.0).then_inc(misc_set, 1)
            nc.vector.memset(ones[:], 1.0).then_inc(misc_set, 1)
            nc.vector.memset(dm2[:], 1.0).then_inc(misc_set, 1)
            nc.vector.memset(gl[:], 0.0).then_inc(misc_set, 1)
            nc.vector.memset(gr_rows[:], 0.0).then_inc(misc_set, 1)
            dve.wait_ge(misc_set, 5)
            nc.vector.memset(gl[32:36, :], 1.0).then_inc(misc_set, 1)
            dve.wait_ge(first_loaded, 16)
            for h in range(HEADS):
                ts(gr_rows[0:4, h, :], ones[0:4, :], cut["ident"][0:4, h:h + 1], None, ALU.mult).then_inc(misc_set, 1)
            for k in range(KT):
                wait_tile(dve, k)
                taken(nc.vector.tensor_copy(hT[:, k, :], ring[k % 2][:, 0:T]), k)
            for l in range(DEPTH):
                t = KT + l
                wait_tile(dve, t)
                taken(nc.vector.tensor_copy(par[:, l, :], ring[t % 2][:, 0:NPAR]), t)
            for l in range(DEPTH):
                wait_taken(dve, KT + l)
            rest_of_half(0)
            for l in range(DEPTH):
                q0 = q_start(l)
                pre_norm(l)
                if l == 0:
                    for n in range(1, REST_AHEAD):
                        rest_of_half(n)
                    dve.wait_ge(const_loaded, 16)
                run_steps(l, parts)
                branch(l)
                output(l)
                post_norm(l, 1, q0, R_MIXPOST, rest_of_ffn_x(l, q0))
                gate_up(l)
                down(l)
                post_norm(l, 3, q0, R_FFNPOST)

        @block.gpsimd
        def _(pool):
            tt = nc.gpsimd.tensor_tensor

            def rest_of_x(l):
                for k in range(KT):
                    pool.wait_ge(xh_ready[l], k + 1)
                    tt(xl[:, k, :], sq[:, k, :], xh[:, k, :].bitcast(F32), ALU.subtract).then_inc(xl_ready[l], 1)

            def sum_squares(l, n, q0):
                for k in range(1, KT - 1):
                    pool.wait_ge(sq_ready[l][n], k + 1)
                    if k > 1:
                        pool.wait_ge(sq_summed[l], n // 2 * (KT - 2) + k - 1)
                    elif n == 3:
                        pool.wait_ge(sq_summed[l], KT - 2)
                    tt(sq[:, 0, q0:], sq[:, 0, q0:], sq[:, k, q0:], ALU.add).then_inc(sq_summed[l], 1)

            def scale_silu(l, q0):
                with pool.Fori(0, NGU // 2) as i:
                    for c in range(2):
                        pool.wait_ge(silu_ready[l], c + 1 + i * 2)
                        v = silu_g[:, c, q0:]
                        tt(v, v, rstd[:, q0:], ALU.mult).then_inc(silu_scaled[l], 1)

            def merge(l):
                q0 = q_start(l)
                for m in range(KT):
                    pool.wait_ge(branch_free[l], m + 1)
                    if m:
                        pool.wait_ge(merge_step[l], m)
                    tt(half[:, :, q0:], term[:, m % 2, 0:2, q0:], term[:, m % 2, 2:4, q0:], ALU.add).then_inc(half_ready[l], 1)
                    pool.wait_ge(half_ready[l], m + 1)
                    if m >= 2:
                        pool.wait_ge(ml_ready[l], m - 1)
                    tt(acc[:, m % 2, q0:], half[:, 0, q0:], half[:, 1, q0:], ALU.add).then_inc(merge_step[l], 1)

            def add_sublayer(l, n, q0):
                for k in range(KT):
                    pool.wait_ge(post_scaled[l], n // 2 * KT + k + 1)
                    tt(hT[:, k, q0:], hT[:, k, q0:], sub[:, k, q0:], ALU.add).then_inc(h_ready[l], 1)

            for l in range(DEPTH):
                q0 = q_start(l)
                rest_of_x(l)
                merge(l)
                sum_squares(l, 1, q0)
                add_sublayer(l, 1, q0)
                scale_silu(l, q0)
                sum_squares(l, 3, q0)
                add_sublayer(l, 3, q0)


_INS = ["x", "meta_tokens", "norm_mix_pre", "norm_mix_post", "norm_ffn_pre", "norm_ffn_post", "w_in", "gla_w_gate_up",
        "gla_b_gate", "gla_norm", "ml_conv", "ml_b_i", "ml_b_f", "ml_norm", "ret_norm", "w_branch", "b_merge", "w_out",
        "ffn_w_gate", "ffn_w_up", "ffn_w_down"]


def kernel(**inputs):
    import concourse.bacc as bacc
    from concourse.bass_utils import run_bass_kernel_spmd

    nc = bacc.Bacc("TRN2", target_bir_lowering=False, num_devices=1)
    arrays = {f"in_{n}": np.ascontiguousarray(inputs[n]) for n in _INS}
    arrays["in_consts"] = constants()
    args = [nc.dram_tensor(n, a.shape, mybir.dt.from_np(a.dtype), kind="ExternalInput").ap() for n, a in arrays.items()]
    out = nc.dram_tensor("out", (1, SEQ, D), F32, kind="ExternalOutput").ap()
    build(nc, *args, out)
    r = run_bass_kernel_spmd(nc, [arrays], core_ids=[0])
    return r.results[0]["out"]
```

```python
from contextlib import ExitStack

import numpy as np
import concourse.bass as bass
from concourse import mybir

F32 = mybir.dt.float32
F32R = mybir.dt.float32r
ALU = mybir.AluOpType
ACT = mybir.ActivationFunctionType
ds = bass.ds

P = 128
D = 1024
KT = D // P
DEPTH = 2
META = 16
SEQ = 256
T = META + SEQ
HEADS = 4
HD = 64
DFF = 2816
FT = DFF // P
EPS = 1e-6
GLA_NORMALIZER = 16.0
NEG = -1e30
KB1, KB2 = META, META + P
SCW = 3 * P

C_SBQ, C_SBK, C_SBV = 0, 256, 512
C_GQ, C_GV, C_GR, C_CODE = 768, 1024, 1280, 1536
C_MQK, C_MV, C_MI, C_MF, C_MO = 1552, 2064, 2320, 2324, 2328
C_RQ, C_RK, C_RV, C_RG, C_MERGE = 2584, 2840, 3096, 3352, 3608

R_MIXPRE, R_MIXPOST, R_FFNPRE, R_FFNPOST, R_BGATE, R_GLAN, R_MLN, R_RETN, R_CONV, R_BMERGE = (
    0, 8, 16, 24, 32, 33, 35, 37, 39, 55)
NPAR = 87

MIX = [("small", None, "small"), ("mqk0", C_MQK, "two"), ("mqk1", C_MQK + 256, "two"), ("gr", C_GR, "two"),
       ("rg", C_RG, "two"), ("gqk", C_GQ, "two"), ("rq", C_RQ, "two"), ("rk", C_RK, "two"), ("mv", C_MV, "v"),
       ("gv", C_GV, "v"), ("rv", C_RV, "v"), ("sbq", C_SBQ, "two"), ("sbk", C_SBK, "two"), ("mo", C_MO, "two"),
       ("sbv", C_SBV, "v")]
KIND = {name: kind for name, _, kind in MIX}
MIX_NO = {name: n for n, (name, _, _) in enumerate(MIX)}
TILES_OF = {"small": 1, "two": 2, "v": 3}
SB, GLA, ML, RET = range(4)
NORM_ORDER = (4, 5, 2, 3, 6, 7)
ML_SCALE = HD ** -0.5
V_OF = {"sbv": SB, "gv": GLA, "mv": ML, "rv": RET}
NLOGIT, NBRANCH, NOUT, NGU, NDOWN = 16, 4, 4, FT, 12
GROUPS = len(MIX) + NLOGIT + NBRANCH + NOUT + NGU + NDOWN
DOWN_K = (8, 8, 6)

CONSTS = [("ident", 128), ("mean", 128), ("eps", 1), ("negtri", 128), ("negones", 128), ("perm", 128), ("negtri0", 32),
          ("mask_lt", SCW), ("neg_lt", SCW), ("neg_le", SCW), ("mask_le", SCW),
          ("mask_lt0", T), ("neg_lt0", T), ("neg_le0", T), ("mask_le0", T),
          ("decay", 4 * SCW), ("decay0", T), ("cos", T), ("sin", T),
          ("headsum", 6 * 12), ("headbc", 6 * P), ("denind", 16), ("denind0", 4), ("negind", 4)]
CONST_FIRST = 257
CONST_W = sum(w for _, w in CONSTS)


def constants():
    c = {n: np.zeros((P, w), np.float64) for n, w in CONSTS}
    p = np.arange(P)
    c["ident"][:] = np.eye(P)
    c["mean"][:] = 1.0 / D
    c["negtri"][:] = -(p[:, None] >= p[None, :]).astype(float)
    c["negones"][:] = -1
    c["eps"][:] = EPS
    r, head = p % 32, p // 32
    for col in range(32):
        c["negtri0"][:, col] = -((r >= col) & (r < META)).astype(float)
    q = np.concatenate([np.arange(2 * P), np.arange(P)])[None, :]
    lt, le = p[:, None] < q, p[:, None] <= q
    q0 = np.arange(T)[None, :]
    real = (r < META)[:, None]
    lt0, le0 = (r[:, None] < q0) & real, (r[:, None] <= q0) & real
    c["mask_lt"][:], c["mask_le"][:], c["mask_lt0"][:], c["mask_le0"][:] = lt, le, lt0, le0
    c["neg_lt"][:], c["neg_le"][:] = np.where(lt, 0, NEG), np.where(le, 0, NEG)
    c["neg_lt0"][:], c["neg_le0"][:] = np.where(lt0, 0, NEG), np.where(le0, 0, NEG)
    log_gamma = np.log1p(-np.exp2(-5.0 - np.arange(HEADS)))
    for h in range(HEADS):
        c["decay"][:, h * SCW:(h + 1) * SCW] = np.where(le, np.exp(log_gamma[h] * (q - p[:, None])), 0) / 8
    c["decay0"][:] = np.where(le0, np.exp(log_gamma[head][:, None] * (q0 - r[:, None])), 0) / 8
    half = HD // 2
    freq = (10000.0 ** (-np.arange(half, dtype=np.float32) / half)).astype(np.float32)
    ang = (np.arange(T, dtype=np.float32)[None, :] * freq[:, None]).astype(np.float32).astype(np.float64)
    c["cos"][:] = np.tile(np.cos(ang), (4, 1))
    c["sin"][:] = np.tile(np.concatenate([-np.sin(ang), np.sin(ang)]), (2, 1))
    other = np.where(p % HD < half, p + half, p - half)
    c["perm"][other, p] = 1
    for pair in range(6):
        for i in range(P):
            j = 2 * pair + i // HD
            c["headsum"][i, pair * 12 + j] = 1.0 / HD
            c["headbc"][j, pair * P + i] = 1
    for h in range(HEADS):
        c["denind"][:, h * 4 + h] = 1
        c["denind0"][:, h] = head == h
        c["negind"][32 + h, h] = -1
    return np.concatenate([c[n] for n, _ in CONSTS], axis=1).astype(np.float32)


PROJECT = [("group", "small"), ("group", "mqk0"), ("gate",), ("group", "mqk1"), ("load_tables", 0), ("silu_tables",),
           ("group", "gr"), ("load_tables", 1), ("conv", 0), ("group", "rg"), ("load_tables", 2), ("conv", 1), ("group", "gqk"),
           ("conv", 2), ("group", "rq"), ("conv", 3), ("group", "rk"), ("conv_silu",),
           ("group", "mv"), ("rot", 0), ("rot", 1), ("rest", "mv"),
           ("group", "gv"), ("rot", 2), ("rot", 3), ("rest", "gv"),
           ("group", "rv"), ("rest", "rv"), ("group", "sbq"), ("group", "sbk"), ("exp_tables",),
           ("sb_scores0",), ("sb_scores", 0), ("sb_scores", 1), ("sb_soft0",), ("sb_keep0",), ("sb_soft", 0), ("sb_keep", 0),
           ("group", "mo"), ("sb_exponent", 0), ("sb_scores", 2), ("sb_soft", 1), ("sb_mask", 0), ("sb_p", 0), ("sb_keep", 1),
           ("group", "sbv"), ("rest", "sbv"), ("sb_exponent", 1), ("sb_scores", 3)]
BEFORE = {
    0: [("sb_soft", 2), ("sb_mask", 1), ("sb_p", 1), ("sb_keep", 2)],
    1: [("sb_soft", 3), ("sb_mask", 2), ("sb_p", 2), ("sb_keep", 3)],
    2: [("gla_soft",), ("sb_mask", 3), ("sb_mask0",), ("sb_p", 3), ("sb_p0",)],
    3: [("gla_log",), ("gla_exp",), ("gla_decay",)],
    4: [("ml_soft",), ("take_out", 0)],
    5: [("take_out", 1), ("gla_p0",), ("gla_p", 0), ("gla_p", 1), ("ml_rows",)],
    6: [("gla_p", 2), ("gla_p", 3), ("ml_em",)],
    7: [("take_out", 2)],
    8: [("ml_mask0",), ("ml_mask", 0), ("ml_w0",), ("ml_w", 0), ("take_out", 3), ("ml_p0",), ("ml_p", 0)],
    9: [("ml_mask", 1), ("ml_w", 1), ("ml_p", 1)],
    10: [("ml_mask", 2), ("ml_w", 2), ("ml_p", 2)],
    11: [("ml_mask", 3), ("ml_w", 3), ("ml_p", 3)],
    12: [("den_abs",), ("den_square",)],
    13: [("take_out", 4)],
    14: [("take_out", 5), ("ret_p0",), ("ret_p", 0), ("ret_p", 1), ("head_square", 2), ("head_square", 3)],
    15: [("ret_p", 2), ("ret_p", 3), ("head_square", 0), ("head_square", 1)],
    16: [("take_out", 6)],
    17: [("take_out", 7), ("head_square", 4), ("head_square", 5)],
    18: [("head_var",), ("head_rstd",), ("sigmoid_tables",)],
    19: [("y_plain",), ("mo_sigmoid",)],
    20: [("y_rest", 0), ("gate_sigmoid", 0)],
    21: [("y_rest", 1)],
    22: [("y_rest", 2), ("gate_sigmoid", 1)],
    23: [("y_rest", 3)],
    24: [("y_rest", 4), ("gate_sigmoid", 2)],
    25: [("y_rest", 5)],
    26: [("gate_sigmoid", 3)],
    28: [("gate_sigmoid", 4)],
}
BEHIND = {
    0: [("sb_exponent", 2)],
    1: [("sb_exponent", 3)],
    3: [("values", 0, 0), ("gla_scores0",)],
    4: [("values", 0, 1), ("gla_scores", 0), ("gla_scores", 1)],
    5: [("gla_scores", 2), ("gla_scores", 3)],
    6: [("values", 1, 0)],
    7: [("values", 1, 1), ("ml_exponent0",), ("ml_scores0",), ("ml_exponent", 0), ("ml_scores", 0)],
    8: [("ml_exponent", 1), ("ml_scores", 1)],
    9: [("ml_exponent", 2), ("ml_scores", 2)],
    10: [("ml_exponent", 3), ("ml_scores", 3)],
    11: [("ml_den",)],
    12: [("values", 2, 0)],
    13: [("values", 2, 1), ("ret_scores0",), ("ret_scores", 0), ("ret_scores", 1)],
    14: [("ret_scores", 2), ("ret_scores", 3)],
    15: [("values", 3, 0)],
    16: [("values", 3, 1)],
    17: [("headsum",)],
    19: [("headbc", 0)],
    20: [("headbc", 1)],
    21: [("headbc", 2)],
    22: [("headbc", 3)],
    23: [("headbc", 4)],
    24: [("headbc", 5)],
}
STEPS = PROJECT + [step for j in range(2 * NLOGIT) for step in BEFORE.get(j, []) + [("logit", j)] + BEHIND.get(j, [])]
SIGMOID_FROM = 20


ROUND_AHEAD = 4
REST_AHEAD = 3
WARM_START, WARM_PRE, WARM_POST = 4, 6, 8
RSTD_COUNT = (1, 2, 4, 5)
X_POOL = 4
H_POOL = 5


def plan_tiles():
    first, signal = [], []
    done = halves = 0

    def free(n):
        nonlocal done
        for _ in range(n):
            done += 1
            signal.append(("tile", done, 1))

    def last_of(used, before=0):
        nonlocal halves
        halves += before + used
        signal.append(("half", halves, used))

    free(KT + DEPTH)
    for _ in range(DEPTH):
        f = {}

        def stage(name):
            f[name] = len(signal)

        stage("norm0"), free(1)
        for step in STEPS:
            stage(step)
            if step[0] == "group":
                kind = KIND[step[1]]
                if kind == "two":
                    last_of(1), last_of(1)
                else:
                    free(TILES_OF[kind] - 1)
                    last_of(2)
            elif step[0] == "logit":
                last_of(1)
            elif step[0] in ("gate", "headsum"):
                free(1)
        halves += 2 * NBRANCH
        stage("out"), [last_of(1) for _ in range(KT)]
        stage("norm1"), free(1)
        stage("gu"), [last_of(1) for _ in range(2 * NGU)]
        stage("down")
        for _ in range(KT // 2):
            last_of(1, 2 * len(DOWN_K) - 2), last_of(1)
        stage("norm3"), free(1)
        first.append(f)
    out_first = len(signal)
    free(4)
    assert halves == 2 * GROUPS * DEPTH
    return first, signal, out_first


def build(nc, x, meta_tokens, norm_mix_pre, norm_mix_post, norm_ffn_pre, norm_ffn_post, w_in, gla_w_gate_up,
          gla_b_gate, gla_norm, ml_conv, ml_b_i, ml_b_f, ml_norm, ret_norm, w_branch, b_merge, w_out,
          ffn_w_gate, ffn_w_up, ffn_w_down, consts, out):
    TILE, SIGNAL, TILE_OUT = plan_tiles()
    with ExitStack() as ctx:
        def sb(name, shape, dt=F32):
            return ctx.enter_context(nc.sbuf_tensor(name, shape, dt))

        def sem(name):
            return ctx.enter_context(nc.semaphore(name))

        def per_layer(name):
            return [sem(f"{name}_l{i}") for i in range(DEPTH)]

        raw = [sb(f"raw{i}", [P, KT, 256]) for i in range(2)]
        hi = [sb(f"hi{i}", [P, KT, 256], F32R) for i in range(2)]
        lo = [sb(f"lo{i}", [P, KT, 256], F32R) for i in range(2)]
        hT = sb("hT", [P, KT, T])
        xh = sb("xh", [P, KT, T], F32R)
        xl = sb("xl", [P, KT, T], F32R)
        const = sb("const", [P, CONST_W])
        par = sb("par", [P, DEPTH, NPAR])
        ifbias = sb("ifbias", [P, DEPTH])
        wgate = sb("wgate", [16, DEPTH, P])
        glaref = sb("glaref", [P, 4])
        dm2 = sb("dm2", [12, T])
        ones = sb("ones", [P, T])
        gl = sb("gl", [36, T])
        gr_rows = sb("gr_rows", [36, HEADS, T])

        cut = {}
        at = 0
        for n, w in CONSTS:
            cut[n] = const[:, at:at + w]
            at += w

        def c3(name, n):
            return cut[name].rearrange("p (a b) -> p a b", a=n)

        def region(name, words):
            return ctx.enter_context(nc.sbuf_tensor(name, [P, words], F32))

        def room(shape):
            return (4 * int(np.prod(shape[1:])) + 31) // 32 * 32

        def tenants(start, spec):
            made = []
            for name, shape, dt in spec:
                made.append(nc.alloc_sbuf_tensor_at(name, shape, dt, offset=start))
                start += room(shape)
            return made, start

        a0 = nc.sbuf_base
        gate_region = region("gate_region", 4 * KT * T)
        a1 = nc.sbuf_base
        (gates,), _ = tenants(a0, [("gates", [P, 4 * KT, T], F32)])
        (xt, sq, sub, rstd), end = tenants(a0, [("xt", [P, 3, D], F32), ("sq", [P, KT, T], F32),
                                               ("sub", [P, KT, T], F32), ("rstd", [P, T], F32)])
        assert end <= a1
        mix_spec = [("sbq", [P, 2, T]), ("sbk", [P, 2, T]), ("rq", [P, 2, T]), ("rk", [P, 2, T]),
                    ("conv_in", [P, 4, T + 3]), ("mqk", [P, 4, T]), ("gq", [P, T]), ("gk", [P, T]),
                    ("gr", [P, 2, T]), ("mo", [P, 2, T]), ("rg", [P, 2, T]), ("v", [P, 2, 4, 256]), ("v0", [P, 4, HD]),
                    ("pt", [P, HEADS, SCW]), ("pt0", [P, T]), ("sa", [P, 2, SCW]), ("sb2", [P, 2, SCW]),
                    ("small", [P, T]), ("gwork", [P, T]), ("cum", [P, T]), ("gwork2", [P, T]),
                    ("rows", [P, 3, T]), ("osb", [P, 8, T])]
        gla_spec = [("qa", [P, SEQ]), ("qb", [P, P]), ("q0", [P, META]), ("kr0", [P, KB2]), ("kr1", [P, SEQ]), ("k00", [P, 32])]
        b0 = nc.sbuf_base
        words = sum(room(s) for _, s in mix_spec) // 4
        mix_region = region("mix_region", words)
        made, _ = tenants(b0, [(n, s, F32) for n, s in mix_spec])
        M = dict(zip([n for n, _ in mix_spec], made))
        conv_at = b0 + sum(room(s) for _, s in mix_spec[:4])
        made, end = tenants(conv_at, [(n, s, F32) for n, s in gla_spec])
        M.update(zip([n for n, _ in gla_spec], made))
        assert end <= conv_at + 4 * 4 * (T + 3)
        (yh,), e1 = tenants(b0, [("yh", [P, 8, T], F32R)])
        (yl,), _ = tenants(e1, [("yl", [P, 8, T], F32R)])
        (ah, al, silu_g, prod), end = tenants(b0, [("ah", [P, FT, T], F32R), ("al", [P, FT, T], F32R),
                                                   ("silu_g", [P, 2, T], F32), ("prod", [P, 2, T], F32)])
        assert end <= b0 + 4 * words
        (acc, half, term), end2 = tenants(e1 + 4 * 8 * T, [("acc", [P, 2, T], F32), ("half", [P, 2, T], F32),
                                                           ("term", [P, 2, 4, T], F32)])
        assert end2 <= b0 + 4 * words
        (osq,), _ = tenants(b0, [("osq", [P, 6, T], F32)])
        (prows,), _ = tenants(b0, [("prows", [NPAR, DEPTH, P], F32)])
        (otok,), _ = tenants(b0, [("otok", [P, 2, D], F32)])

        banks = ctx.enter_context(nc.psum_tensor("banks", [P, 8, 512], F32))
        ring = [banks[:, i, :] for i in range(2)]
        sc = [banks[:, 2 + i, :] for i in range(2)]
        ex, k0, e0, ops = (banks[:, 4 + i, :] for i in range(4))
        mean2_bank = e0
        rot_banks = [ex, e0]
        spread_banks = sc
        branch_banks = [banks[:, 4 * i:4 * i + 4, :] for i in range(2)]

        raw_loaded = [sem(f"raw_loaded{i}") for i in range(2)]
        small_loaded = sem("small_loaded")
        hi_ready, lo_ready = sem("hi_ready"), sem("lo_ready")
        half_used, tile_done = sem("half_used"), sem("tile_done")
        bank_free = [sem(f"bank_free{i}") for i in range(2)]
        first_loaded, const_loaded, par_loaded, par_late, meta_loaded, misc_set, bias_loaded = (
            sem(n) for n in ("first_loaded", "const_loaded", "par_loaded", "par_late", "meta_loaded", "misc_set", "bias_loaded"))
        x_loaded = [sem(f"x_loaded{i}") for i in range(2)]
        sq_ready = [[sem(f"sq_ready{n}_l{i}") for n in range(4)] for i in range(DEPTH)]
        out_rows, out_stored = sem("out_rows"), sem("out_stored")
        mean2_ready = sem("mean2_ready")
        sq_first = sem("sq_first")
        names = """
            rot_ready rot_free spread_ready spread_free xl_late xl_ffn_ready h_late half_late sq_summed
            silu_ready silu_scaled rstd_ready xn_ready xh_ready xl_ready post_scaled h_ready pad_set
            rot_cos rot_done conv_step conv_done gla_soft gla_dve gla_exp gla_ops ml_soft ml_dve ml_em
            sc_ready sc_free ex_ready ex_free k0_ready k0_free e0_ready e0_free sb_soft sb_keep sb_keep0
            sb_p sb_p0 ml_w o_ready o_free den_ready den_abs den_dve osq_ready hlog_ready hrstd_ready
            mo_ready y_step yh_ready yl_ready gates_ready branch_free half_ready merge_step mh_ready
            ml_ready ah_ready al_ready""".split()
        (rot_ready, rot_free, spread_ready, spread_free, xl_late, xl_ffn_ready, h_late, half_late,
         sq_summed, silu_ready, silu_scaled, rstd_ready, xn_ready, xh_ready, xl_ready, post_scaled, h_ready,
         pad_set, rot_cos, rot_done, conv_step, conv_done, gla_soft, gla_dve, gla_exp, gla_ops, ml_soft,
         ml_dve, ml_em, sc_ready, sc_free, ex_ready, ex_free, k0_ready, k0_free, e0_ready, e0_free, sb_soft,
         sb_keep, sb_keep0, sb_p, sb_p0, ml_w, o_ready, o_free, den_ready, den_abs, den_dve, osq_ready,
         hlog_ready, hrstd_ready, mo_ready, y_step, yh_ready, yl_ready, gates_ready, branch_free,
         half_ready, merge_step, mh_ready, ml_ready, ah_ready, al_ready) = (per_layer(n) for n in names)

        G_MIX = [l * GROUPS for l in range(DEPTH)]
        G_LOGIT = [g + len(MIX) for g in G_MIX]
        G_BRANCH = [g + NLOGIT for g in G_LOGIT]
        G_OUT = [g + NBRANCH for g in G_BRANCH]
        G_GU = [g + NOUT for g in G_OUT]
        G_DOWN = [g + NGU for g in G_GU]
        G_END = GROUPS * DEPTH

        def group_k(g):
            l = g % GROUPS - (GROUPS - NDOWN)
            return DOWN_K[l % 3] if l >= 0 else KT

        def wait_tile(eng, t, i=0, step=0):
            kind, n, _ = SIGNAL[t]
            per = SIGNAL[t + step][1] - n
            eng.wait_ge(tile_done if kind == "tile" else half_used, n + i * per)

        def wait_taken(eng, t, i=0, step=0):
            eng.wait_ge(bank_free[t % 2], t // 2 + 1 + i * (step // 2))

        def group_tile(l, name):
            return TILE[l][("group", name)]

        def run_steps(l, parts):
            for name, *which in STEPS:
                if name in parts:
                    parts[name](l, *which)

        def wait_h(eng, l, n, k):
            if n == 3 and k >= H_POOL:
                eng.wait_ge(h_late[l], k - H_POOL + 1)
            else:
                eng.wait_ge(h_ready[l], n // 2 * KT + k + 1)

        def q_start(l):
            return META if l == DEPTH - 1 else 0

        head_rows = [slice(HD * (h % 2), HD * (h % 2) + HD) for h in range(HEADS)]
        quad = [slice(32 * h, 32 * h + 32) for h in range(HEADS)]
        quad_real = [slice(32 * h, 32 * h + META) for h in range(HEADS)]

        PARAM_ROWS = [(r, src.rearrange("l (a p) -> a l p", p=P)) for r, src in (
            (R_MIXPRE, norm_mix_pre), (R_MIXPOST, norm_mix_post), (R_FFNPRE, norm_ffn_pre), (R_FFNPOST, norm_ffn_post),
            (R_BGATE, gla_b_gate), (R_GLAN, gla_norm), (R_MLN, ml_norm), (R_RETN, ret_norm))]
        PARAM_ROWS += [(R_CONV, ml_conv.rearrange("l j (a p) -> (j a) l p", p=P)),
                       (R_BMERGE, b_merge.rearrange("l n (a p) -> (n a) l p", p=P))]

        def load_rows(eng, rows, loaded):
            for r, src in rows:
                eng.dma_start(prows[r:r + src.shape[0], :, :], src).then_inc(loaded, 16)

        block = ctx.enter_context(nc.Block())

        @block.sync
        def _(sp):
            def load(g, src, i=0, step=0, nk=KT):
                if g >= 2:
                    sp.wait_ge(hi_ready, 2 * (g - 1) + i * (2 * step))
                    sp.wait_ge(lo_ready, 2 * (g - 1) + i * (2 * step))
                sp.dma_start(raw[g % 2][:, 0:nk, 0:src.shape[2]], src).then_inc(raw_loaded[g % 2], 16)

            def cols(w, c, n=256):
                return w.rearrange("(k p) n -> p k n", p=P)[:, :, c:c + n]

            sp.dma_start(xt[0:META, 0, :], meta_tokens).then_inc(meta_loaded, 16)
            for n in range(2):
                sp.dma_start(xt[:, 1:3, n * 512:n * 512 + 512],
                             x[0].rearrange("(b p) n -> p b n", p=P)[:, :, n * 512:n * 512 + 512]).then_inc(x_loaded[n], 16)
            load_rows(sp, PARAM_ROWS[4:7], par_loaded)
            for l in range(DEPTH):
                g = G_MIX[l]
                for name, c, kind in MIX:
                    if kind == "small":
                        load(g, cols(w_in[l], C_CODE, 32))
                        sp.dma_start(raw[g % 2][:, :, 32:64], cols(w_in[l], C_MI, 32)).then_inc(small_loaded, 16)
                        sp.dma_start(raw[g % 2][:, :, 64:256], cols(w_in[l], C_MF, 192)).then_inc(small_loaded, 16)
                    else:
                        load(g, cols(w_in[l], c))
                    g += 1
                wm = w_in[l].rearrange("(k p) n -> p k n", p=P)
                wb = w_branch[l].rearrange("n (k p) m -> p (n k) m", p=P)
                wo = w_out[l].rearrange("(k p) m -> p k m", p=P)
                wg = ffn_w_gate[l].rearrange("(k p) m -> p k m", p=P)
                wu = ffn_w_up[l].rearrange("(k p) m -> p k m", p=P)
                wd = ffn_w_down[l].rearrange("(k p) m -> p k m", p=P)
                with sp.Fori(0, NLOGIT // 2) as i:
                    for j in range(2):
                        load(G_LOGIT[l] + j, wm[:, :, ds(i * 512 + (C_MERGE + 256 * j), 256)], i, 2)
                with sp.Fori(0, NBRANCH // 2) as i:
                    for j in range(2):
                        load(G_BRANCH[l] + j, wb[:, :, ds(i * 512 + 256 * j, 256)], i, 2)
                with sp.Fori(0, NOUT // 2) as i:
                    for j in range(2):
                        load(G_OUT[l] + j, wo[:, :, ds(i * 512 + 256 * j, 256)], i, 2)
                with sp.Fori(0, NGU // 2) as i:
                    for j, w in enumerate((wg, wu)):
                        load(G_GU[l] + j, w[:, :, ds(i * 256, 256)], i, 2)
                with sp.Fori(0, 2) as i:
                    for j in range(6):
                        k = 8 * (j % 3)
                        nk = DOWN_K[j % 3]
                        load(G_DOWN[l] + j, wd[:, k:k + nk, ds(i * 512 + 256 * (j // 3), 256)], i, 6, nk)
            for n in range(4):
                half, b = n // 2, n % 2
                sp.wait_ge(out_rows, n + 1)
                sp.dma_start(out[0, b * P:(b + 1) * P, 512 * half:512 * half + 512],
                             otok[:, b, 512 * half:512 * half + 512]).then_inc(out_stored, 16)
            sp.wait_ge(out_stored, 64)

        @block.tensor
        def _(pe):
            mm = nc.tensor.matmul

            def keep_warm(n):
                for _ in range(n):
                    mm(ops[:, 0:T], ones[:, 0:P], ones[:], start=True, stop=True)

            def open_tile(t, i=0, step=0):
                if t >= 2:
                    pe.wait_ge(bank_free[t % 2], t // 2 + i * (step // 2))
                return ring[t % 2]

            def close_tile(last, t):
                last.then_inc(tile_done if SIGNAL[t][0] == "tile" else half_used, SIGNAL[t][2])

            def use_half(g, c, i=0, step=0):
                pe.wait_ge(hi_ready, 2 * g + c + 1 + i * (2 * step))
                pe.wait_ge(lo_ready, 2 * g + c + 1 + i * (2 * step))
                return hi[g % 2], lo[g % 2]

            def product(dst, wh, wl, mh, ml, start, stop):
                mm(dst, wh, mh, start=start, stop=False)
                mm(dst, wh, ml, start=False, stop=False)
                return mm(dst, wl, mh, start=False, stop=stop)

            def features(t, g, c, mh, ml, q0, i=0, step=0, ready=None, mean=None):
                wh, wl = use_half(g, c, i, step)
                ps = open_tile(t, i, 2 * step)
                f = slice(c * P, c * P + P)
                for k in range(KT):
                    if ready:
                        ready(k)
                    last = product(ps[:, 0:T - q0], wh[:, k, f], wl[:, k, f], mh[:, k, q0:], ml[:, k, q0:],
                                   k == 0, k == KT - 1)
                    if mean:
                        mean(k)
                close_tile(last, t)

            def mean_square(l, n, q0):
                def tile(k, ps):
                    pe.wait_ge(sq_ready[l][n], k + 1)
                    return mm(ps[:, 0:T - q0], cut["mean"], sq[:, k, q0:], start=k == 0, stop=k == KT - 1)

                if n == 2:
                    def beside(k):
                        last = tile(k, mean2_bank)
                        if k == KT - 1:
                            last.then_inc(mean2_ready, 1)
                    return beside
                t = TILE[l][f"norm{n}"]
                ps = open_tile(t)
                if n == 0 and l == 0:
                    pe.wait_ge(sq_first, KT - 1)
                    close_tile(mm(ps[:, 0:T], cut["mean"], sq[:, 0, :], start=True, stop=True), t)
                elif n == 0:
                    for k in range(KT):
                        last = tile(k, ps)
                    close_tile(last, t)
                else:
                    pe.wait_ge(sq_summed[l], n // 2 * (KT - 2) + KT - 2)
                    tile(0, ps)
                    close_tile(tile(KT - 1, ps), t)

            def group(l, name):
                g, t, kind = G_MIX[l] + MIX_NO[name], group_tile(l, name), KIND[name]

                def x_ready(k):
                    pe.wait_ge(xh_ready[l], k + 1)
                    pe.wait_ge(*((xl_ready[l], k + 1) if k < X_POOL else (xl_late[l], k + 1 - X_POOL)))

                if kind != "v":
                    for j in range(TILES_OF[kind]):
                        features(t + j, g, j, xh, xl, 0, ready=x_ready if name == "small" else None)
                    return
                use_half(g, 0)
                wh, wl = use_half(g, 1)
                for b, tok in enumerate((0, KB1, KB2)):
                    ps = open_tile(t + b)
                    for k in range(KT):
                        last = product(ps[:, 0:256], xh[:, k, tok:tok + P], xl[:, k, tok:tok + P], wh[:, k, :], wl[:, k, :],
                                       k == 0, k == KT - 1)
                    close_tile(last, t + b)

            def gate(l):
                t = TILE[l][("gate",)]
                wait_taken(pe, group_tile(l, "small"))
                pe.wait_ge(bias_loaded, 48)
                close_tile(mm(open_tile(t)[:, 0:T], wgate[:, l, :], M["small"][0:16, :], start=True, stop=True), t)

            def rot(l, i):
                name = ("rq", "rk")[i // 2]
                pe.wait_ge(const_loaded, 48)
                wait_taken(pe, group_tile(l, name) + i % 2)
                if i >= 2:
                    pe.wait_ge(rot_free[l], i - 1)
                mm(rot_banks[i % 2][:, 0:T], cut["perm"], M[name][:, i % 2, :], start=True, stop=True).then_inc(rot_ready[l], 1)

            def logit(l, j):
                features(TILE[l][("logit", j)], G_LOGIT[l] + j // 2, j % 2, xh, xl, q_start(l))

            def open_scores(l, mix, h):
                j = 4 * mix + h
                if j >= 2:
                    pe.wait_ge(sc_free[l], j - 1)
                return sc[j % 2]

            def open_scores0(l, mix):
                if mix:
                    pe.wait_ge(k0_free[l], mix)
                return k0

            def plain_scores(dst, dst0, qs, ks, h, both):
                i, rows = h // 2, head_rows[h]
                if dst is not None:
                    mm(dst[:, 0:256], ks[rows, i, KB1:KB2], qs[rows, i, KB1:], start=True, stop=both)
                    return mm(dst[:, 256:SCW], ks[rows, i, KB2:], qs[rows, i, KB2:], start=True, stop=both)
                return mm(dst0[quad[h], 0:T], ks[rows, i, 0:32], qs[rows, i, :], start=True, stop=both)

            def scores0(l, mix, qs, ks):
                d = open_scores0(l, mix)
                for h in range(HEADS):
                    last = plain_scores(None, d, qs, ks, h, True)
                last.then_inc(k0_ready[l], 1)

            def scores(l, mix, h, qs, ks):
                plain_scores(open_scores(l, mix, h), None, qs, ks, h, True).then_inc(sc_ready[l], 1)

            def sb_exponent(l, h):
                qs, ks, i, rows = M["sbq"], M["sbk"], h // 2, head_rows[h]
                keep = M["pt"]
                pe.wait_ge(rot_free[l], 4)
                pe.wait_ge(sb_keep0[l], 1)
                pe.wait_ge(sb_keep[l], h + 1)
                mm(e0[quad[h], 0:T], ks[rows, i, 0:32], qs[rows, i, :], start=True, stop=False)
                mm(e0[quad[h], 0:T], cut["negtri0"][quad[h], :], M["pt0"][quad[h], :], start=False, stop=False)
                mm(e0[quad[h], KB1:T], cut["negones"][:, 0:32], keep[:, h, 0:256], start=False, stop=False)
                last0 = mm(e0[quad[h], KB2:T], cut["negones"][:, 0:32], keep[:, h, 256:SCW], start=False, stop=True)
                if h == HEADS - 1:
                    last0.then_inc(e0_ready[l], 1)
                if h:
                    pe.wait_ge(ex_free[l], h)
                mm(ex[:, 0:256], ks[rows, i, KB1:KB2], qs[rows, i, KB1:], start=True, stop=False)
                mm(ex[:, 0:256], cut["negtri"], keep[:, h, 0:256], start=False, stop=False)
                mm(ex[:, 128:256], cut["negones"], keep[:, h, 256:SCW], start=False, stop=True)
                mm(ex[:, 256:SCW], ks[rows, i, KB2:], qs[rows, i, KB2:], start=True, stop=False)
                mm(ex[:, 256:SCW], cut["negtri"], keep[:, h, 256:SCW], start=False, stop=True).then_inc(ex_ready[l], 1)

            def gla_scores0(l):
                d = open_scores0(l, GLA)
                pe.wait_ge(gla_ops[l], 6)
                for h in range(HEADS):
                    mm(d[quad[h], 0:META], M["k00"][quad[h], :], M["q0"][quad[h], :], start=True, stop=True)
                    last = mm(d[quad[h], META:T], M["kr0"][quad[h], 0:32], M["qa"][quad[h], :], start=True, stop=True)
                last.then_inc(k0_ready[l], 1)

            def gla_scores(l, h):
                d = open_scores(l, GLA, h)
                mm(d[:, 0:128], M["kr0"][quad[h], KB1:KB2], M["qa"][quad[h], 0:P], start=True, stop=True)
                mm(d[:, 128:256], M["kr1"][quad[h], 0:P], M["qb"][quad[h], :], start=True, stop=True)
                mm(d[:, 256:SCW], M["kr1"][quad[h], P:], M["qb"][quad[h], :], start=True, stop=True).then_inc(sc_ready[l], 1)

            def ml_exponent0(l):
                pe.wait_ge(ml_dve[l], 10)
                pe.wait_ge(e0_free[l], 1)
                for h in range(HEADS):
                    last = mm(e0[quad[h], 0:T], gl[:, 0:32], gr_rows[:, h, :], start=True, stop=True)
                last.then_inc(e0_ready[l], 1)

            def ml_exponent(l, h):
                pe.wait_ge(ex_free[l], HEADS + h)
                mm(ex[:, 0:256], gl[:, KB1:KB2], gr_rows[:, h, KB1:], start=True, stop=True)
                mm(ex[:, 256:SCW], gl[:, KB2:], gr_rows[:, h, KB2:], start=True, stop=True).then_inc(ex_ready[l], 1)

            def wait_p(l, mix, h):
                if mix == SB:
                    pe.wait_ge(sb_p0[l], 1)
                    pe.wait_ge(sb_p[l], h + 1)
                else:
                    pe.wait_ge(k0_free[l], mix + 1)
                    pe.wait_ge(sc_free[l], 4 * mix + h + 1)

            def ml_den(l):
                pe.wait_ge(e0_free[l], 2)
                den = c3("denind", 4)
                wait_p(l, ML, 0)
                mm(e0[0:4, 0:T], cut["denind0"], M["pt0"][:], start=True, stop=False)
                for h in range(HEADS):
                    wait_p(l, ML, h)
                    mm(e0[0:4, KB1:T], den[:, h, :], M["pt"][:, h, 0:256], start=False, stop=False)
                    last = mm(e0[0:4, KB2:T], den[:, h, :], M["pt"][:, h, 256:SCW], start=False, stop=h == 3)
                last.then_inc(den_ready[l], 1)

            def values(l, mix, pair):
                n = 2 * mix + pair
                if n:
                    pe.wait_ge(o_free[l], n)
                name = [k for k, m in V_OF.items() if m == mix][0]
                for b in range(3):
                    wait_taken(pe, group_tile(l, name) + b)
                for h in (2 * pair, 2 * pair + 1):
                    wait_p(l, mix, h)
                    o = ops[head_rows[h], :]
                    c = slice(h * HD, h * HD + HD)
                    mm(o[:, 0:T], M["v0"][quad_real[h], mix, :], M["pt0"][quad_real[h], :], start=True, stop=False)
                    mm(o[:, KB1:T], M["v"][:, 0, mix, c], M["pt"][:, h, 0:256], start=False, stop=False)
                    last = mm(o[:, KB2:T], M["v"][:, 1, mix, c], M["pt"][:, h, 256:SCW], start=False, stop=True)
                last.then_inc(o_ready[l], 1)

            mq, mk = M["mqk"][:, 0:2, :], M["mqk"][:, 2:4, :]

            def sb_scores0(l):
                for name in ("sbq", "sbk"):
                    for j in range(2):
                        wait_taken(pe, group_tile(l, name) + j)
                scores0(l, SB, M["sbq"], M["sbk"])

            def ml_scores0(l):
                pe.wait_ge(conv_done[l], 4)
                scores0(l, ML, mq, mk)

            def ret_scores0(l):
                pe.wait_ge(rot_done[l], 4)
                scores0(l, RET, M["rq"], M["rk"])

            def headsum(l):
                t = TILE[l][("headsum",)]
                ps = open_tile(t)
                for p in range(6):
                    pe.wait_ge(osq_ready[l], 6)
                    last = mm(ps[0:12, 0:T], c3("headsum", 6)[:, p, :], osq[:, p, :], start=p == 0, stop=p == 5)
                close_tile(last, t)

            def headbc(l, p):
                pe.wait_ge(hrstd_ready[l], 1)
                pe.wait_ge(sc_free[l], 4 * HEADS)
                if p >= 2:
                    pe.wait_ge(spread_free[l], p - 1)
                mm(spread_banks[p % 2][:, 0:T], c3("headbc", 6)[0:12, p, :], M["rows"][0:12, 0, :], start=True, stop=True).then_inc(spread_ready[l], 1)

            parts = {
                "group": group, "gate": gate, "rot": rot, "logit": logit, "headsum": headsum, "headbc": headbc,
                "sb_scores0": sb_scores0, "sb_scores": lambda l, h: scores(l, SB, h, M["sbq"], M["sbk"]),
                "sb_exponent": sb_exponent, "gla_scores0": gla_scores0, "gla_scores": gla_scores,
                "ml_exponent0": ml_exponent0, "ml_exponent": ml_exponent, "ml_scores0": ml_scores0,
                "ml_scores": lambda l, h: scores(l, ML, h, mq, mk), "ml_den": ml_den,
                "ret_scores0": ret_scores0, "ret_scores": lambda l, h: scores(l, RET, h, M["rq"], M["rk"]),
                "values": values,
            }

            def branch(l):
                q0 = q_start(l)
                pe.wait_ge(spread_free[l], 6)
                pe.wait_ge(yh_ready[l], 8)
                pe.wait_ge(yl_ready[l], 8)
                for m in range(KT):
                    wh, wl = use_half(G_BRANCH[l] + m // 2, m % 2)
                    if m >= 2:
                        pe.wait_ge(branch_free[l], m - 1)
                    c = m % 2 * P
                    for n in (2, 3, 0, 1):
                        if (m, n) == (0, 0):
                            for b in range(2):
                                wait_taken(pe, TILE[l][("logit", 2 * NLOGIT - 1)] - b)
                        for k in range(2):
                            last = product(branch_banks[m % 2][:, n, 0:T - q0], wh[:, 2 * n + k, c:c + P], wl[:, 2 * n + k, c:c + P],
                                           yh[:, 2 * n + k, q0:], yl[:, 2 * n + k, q0:], k == 0, k == 1)
                    last.then_inc(half_used, 1)

            def output(l):
                q0, g, t = q_start(l), G_OUT[l], TILE[l]["out"]

                def merged_ready(k):
                    pe.wait_ge(mh_ready[l], k + 1)
                    pe.wait_ge(ml_ready[l], k + 1)

                pe.wait_ge(branch_free[l], KT - 1)
                with pe.Fori(0, NOUT // 2) as i:
                    for j in range(2):
                        for c in range(2):
                            features(t + 2 * j + c, g + j, c, xh, xl, q0, i, 2, merged_ready if j + c == 0 else None)

            def gate_up(l):
                q0, g, t = q_start(l), G_GU[l], TILE[l]["gu"]
                mean = mean_square(l, 2, q0)

                def x_ready(k):
                    pe.wait_ge(xh_ready[l], KT + k + 1)
                    pe.wait_ge(xl_ffn_ready[l], k + 1)

                for j in range(2):
                    for c in range(2):
                        first = (j, c) == (0, 0)
                        features(t + 2 * j + c, g + j, c, xh, xl, q0, ready=x_ready if first else None, mean=mean if first else None)
                with pe.Fori(0, NGU // 2 - 1) as i:
                    for j in range(2, 4):
                        for c in range(2):
                            features(t + 2 * j + c, g + j, c, xh, xl, q0, i, 2)

            def down(l):
                q0, g, t = q_start(l), G_DOWN[l], TILE[l]["down"]
                with pe.Fori(0, 2) as i:
                    for j in range(6):
                        n = DOWN_K[j % 3]
                        for c in range(2):
                            wh, wl = use_half(g + j, c, i, 6)
                            tt = t + 2 * (j // 3) + c
                            ps = open_tile(tt, i, 4) if j % 3 == 0 else ring[tt % 2]
                            if j < 3 and c == 0:
                                pe.wait_ge(ah_ready[l], 8 * j + n)
                                pe.wait_ge(al_ready[l], 8 * j + n)
                            for k in range(n):
                                kk = 8 * (j % 3) + k
                                last = product(ps[:, 0:T - q0], wh[:, k, c * P:c * P + P], wl[:, k, c * P:c * P + P],
                                               ah[:, kk, q0:], al[:, kk, q0:], kk == 0, kk == FT - 1)
                            if j % 3 == 2:
                                close_tile(last, tt)
                            else:
                                last.then_inc(half_used, 1)

            pe.wait_ge(misc_set, 2)
            keep_warm(WARM_START)
            pe.wait_ge(first_loaded, 16)
            pe.wait_ge(meta_loaded, 16)
            for k in range(KT):
                pe.wait_ge(x_loaded[k // 4], 16)
                ps = open_tile(k)
                f = slice(k * P, k * P + P)
                nc.tensor.transpose(ps[:, 0:META], xt[0:META, 0, f], cut["ident"][0:META, 0:META])
                nc.tensor.transpose(ps[:, KB1:KB2], xt[:, 1, f], cut["ident"])
                close_tile(nc.tensor.transpose(ps[:, KB2:T], xt[:, 2, f], cut["ident"]), k)
            pe.wait_ge(par_loaded, 16 * 7)
            pe.wait_ge(par_late, 16 * (len(PARAM_ROWS) - 7))
            for l in range(DEPTH):
                t = KT + l
                close_tile(nc.tensor.transpose(open_tile(t)[:, 0:NPAR], prows[:, l, :], cut["ident"][0:NPAR, 0:NPAR]), t)
            for l in range(DEPTH):
                mean_square(l, 0, 0)
                keep_warm(WARM_PRE)
                run_steps(l, parts)
                branch(l)
                output(l)
                mean_square(l, 1, q_start(l))
                pe.wait_ge(branch_free[l], KT)
                keep_warm(WARM_POST)
                gate_up(l)
                down(l)
                mean_square(l, 3, q_start(l))
                keep_warm(WARM_POST - 1)
            for n, ps in enumerate((sc[0], sc[1], ex, k0)):
                half, b = n // 2, n % 2
                for c in range(4):
                    wait_h(pe, DEPTH - 1, 3, 4 * half + c)
                    last = nc.tensor.transpose(ps[:, c * P:c * P + P], hT[:, 4 * half + c, META + b * P:META + b * P + P], cut["ident"])
                close_tile(last, TILE_OUT + n)

        @block.scalar
        def _(act):
            fn = nc.scalar.activation

            def round_half(n, i=0, step=0):
                if n >= 2 * G_END:
                    return
                g, c, k = n // 2, n % 2 * P, group_k(n // 2)
                act.wait_ge(raw_loaded[g % 2], 16 * (g // 2 + 1) + i * (4 * step))
                if g in G_MIX:
                    act.wait_ge(small_loaded, 32 * (G_MIX.index(g) + 1))
                if n >= 4:
                    act.wait_ge(half_used, n - 3 + i * step)
                fn(hi[g % 2][:, 0:k, c:c + P], raw[g % 2][:, 0:k, c:c + P], ACT.Copy).then_inc(hi_ready, 1)

            def taken(ins, t):
                ins.then_inc(bank_free[t % 2], 1)

            def square_h(l, n, k, q0):
                if n == 2:
                    wait_h(act, l, 1, k)
                elif l:
                    wait_h(act, l - 1, 3, k)
                else:
                    wait_taken(act, k)
                fn(sq[:, k, q0:], hT[:, k, q0:], ACT.Square).then_inc(sq_ready[l][n], 1)

            def root(l, n, q0):
                if n == 2:
                    act.wait_ge(mean2_ready, l + 1)
                    fn(rstd[:, q0:], mean2_bank[:, 0:T - q0], ACT.Ln, bias=cut["eps"]).then_inc(rstd_ready[l], 1)
                    act.wait_ge(rstd_ready[l], 3)
                else:
                    t = TILE[l][f"norm{n}"]
                    wait_tile(act, t)
                    taken(fn(rstd[:, q0:], ring[t % 2][:, 0:T - q0], ACT.Ln, bias=cut["eps"]), t)
                    wait_taken(act, t)
                fn(rstd[:, q0:], rstd[:, q0:], ACT.Exp, scale=-0.5).then_inc(rstd_ready[l], 1)

            def round_x(l):
                for k in range(KT):
                    act.wait_ge(xn_ready[l], k + 1)
                    fn(xh[:, k, :], sq[:, k, :], ACT.Copy).then_inc(xh_ready[l], 1)

            def round_ffn_x(l, q0):
                for k in range(KT):
                    wait_h(act, l, 1, k)
                    fn(xh[:, k, q0:], hT[:, k, q0:], ACT.Copy, scale=par[:, l, R_FFNPRE + k:R_FFNPRE + k + 1]).then_inc(xh_ready[l], 1)
                    square_h(l, 2, k, q0)

            def group(l, name):
                kind, t = KIND[name], group_tile(l, name)
                half = 2 * (G_MIX[l] + MIX_NO[name]) + ROUND_AHEAD
                if kind == "v":
                    round_half(half)
                    round_half(half + 1)
                    return
                for j in range(TILES_OF[kind]):
                    wait_tile(act, t + j)
                    ps = ring[(t + j) % 2][:, 0:T]
                    if name == "small":
                        ins = fn(M["small"][:], ps, ACT.Identity, bias=ifbias[:, l:l + 1])
                    elif name in ("mqk0", "mqk1"):
                        ins = fn(M["conv_in"][:, 2 * int(name[3]) + j, 3:], ps, ACT.Copy)
                    elif name == "gqk":
                        ins = fn((M["gq"], M["gk"])[j][:], ps, ACT.Copy, scale=(HD // 2) ** -0.5 if j == 0 else 1.0)
                    elif name in ("gr", "rg"):
                        ins = fn(M[name][:, j, :], ps, ACT.Silu)
                    elif name == "sbq":
                        ins = fn(M["sbq"][:, j, :], ps, ACT.Copy, scale=HD ** -0.5)
                    else:
                        ins = fn(M[name][:, j, :], ps, ACT.Copy)
                    taken(ins, t + j)
                    round_half(half + j)
                if kind == "small":
                    round_half(half + 1)

            def logit(l, j):
                q0, t = q_start(l), TILE[l][("logit", j)]
                wait_tile(act, t)
                taken(fn(gates[:, j, q0:], ring[t % 2][:, 0:T - q0], ACT.Sigmoid if j >= SIGMOID_FROM else ACT.Identity,
                         bias=par[:, l, R_BMERGE + j:R_BMERGE + j + 1]), t)
                round_half(2 * G_LOGIT[l] + j + ROUND_AHEAD)

            def mo_sigmoid(l):
                for j in range(2):
                    wait_taken(act, group_tile(l, "mo") + j)
                fn(M["mo"][:], M["mo"][:], ACT.Sigmoid).then_inc(mo_ready[l], 1)

            def gate_sigmoid(l, n):
                for j in (4 * n + 2, 4 * n + 3):
                    wait_taken(act, TILE[l][("logit", j)])
                v = gates[:, 4 * n:4 * n + 4, q_start(l):]
                fn(v, v, ACT.Sigmoid).then_inc(gates_ready[l], 1)

            def gate(l):
                t = TILE[l][("gate",)]
                wait_tile(act, t)
                taken(fn(M["gwork"][:], ring[t % 2][:, 0:T], ACT.Identity, bias=par[:, l, R_BGATE:R_BGATE + 1]), t)

            def conv_silu(l):
                for t in range(4):
                    act.wait_ge(conv_step[l], 12 + t + 1)
                    fn(M["mqk"][:, t, :], M["mqk"][:, t, :], ACT.Silu).then_inc(conv_done[l], 1)

            def softplus_part(dst, src, done, n, first_wait=None):
                if first_wait:
                    act.wait_ge(*first_wait)
                fn(dst, src, ACT.Abs).then_inc(done, 1)
                act.wait_ge(done, n + 1)
                fn(dst, dst, ACT.Exp, scale=-1.0).then_inc(done, 1)
                act.wait_ge(done, n + 2)
                fn(dst, dst, ACT.Ln, bias=1.0).then_inc(done, 1)

            def gla_soft_(l):
                softplus_part(M["gwork2"][:], M["gwork"][:], gla_soft[l], 0,
                              (bank_free[TILE[l][("gate",)] % 2], TILE[l][("gate",)] // 2 + 1))

            def ml_soft_(l):
                t = group_tile(l, "small")
                softplus_part(M["rows"][64:68, 0, :], M["small"][64:68, :], ml_soft[l], 0, (bank_free[t % 2], t // 2 + 1))

            def gla_exp_(l):
                act.wait_ge(gla_dve[l], 6)
                s = 1.0 / GLA_NORMALIZER
                cum, ref = M["cum"], glaref
                for dst, src, scale, bias in ((M["qa"], cum[:, KB1:], s, ref[:, 0:1]), (M["qb"], cum[:, KB2:], s, ref[:, 1:2]),
                                              (M["q0"], cum[:, 0:META], s, 0.0), (M["kr0"], cum[:, 0:KB2], -s, ref[:, 2:3]),
                                              (M["kr1"], cum[:, KB1:], -s, ref[:, 3:4]), (M["k00"], cum[:, 0:32], -s, 0.0)):
                    fn(dst[:], src, ACT.Exp, scale=scale, bias=bias).then_inc(gla_exp[l], 1)

            def ml_em_(l):
                act.wait_ge(ml_dve[l], 11)
                fn(M["rows"][0:4, 1, :], M["rows"][32:36, 0, :], ACT.Exp, scale=-1.0).then_inc(ml_em[l], 1)

            def take_out(l, n):
                act.wait_ge(o_ready[l], n + 1)
                fn(M["osb"][:, n, :], ops[:, 0:T], ACT.Copy).then_inc(o_free[l], 1)

            def sb_soft0(l):
                softplus_part(M["cum"][:], k0[:, 0:T], sb_soft[l], 0, (k0_ready[l], 1))

            def sb_soft_(l, h):
                softplus_part(M["sb2"][:, h % 2, :], sc[h % 2][:, 0:SCW], sb_soft[l], 3 * (h + 1), (sc_ready[l], h + 1))

            def sb_p_(l, h):
                act.wait_ge(ex_free[l], h + 1)
                fn(M["pt"][:, h, :], M["sa"][:, h % 2, :], ACT.Exp).then_inc(sb_p[l], 1)

            def sb_p0_(l):
                act.wait_ge(e0_free[l], 1)
                fn(M["pt0"][:], M["cum"][:], ACT.Exp).then_inc(sb_p0[l], 1)

            def ml_w0(l):
                act.wait_ge(e0_free[l], 2)
                fn(M["gwork2"][:], M["gwork"][:], ACT.Exp).then_inc(ml_w[l], 1)

            def ml_w_(l, h):
                act.wait_ge(ex_free[l], HEADS + h + 1)
                if h >= 2:
                    act.wait_ge(sc_free[l], 4 * ML + h - 1)
                fn(M["sb2"][:, h % 2, :], M["sa"][:, h % 2, :], ACT.Exp).then_inc(ml_w[l], 1)

            def den_abs_(l):
                act.wait_ge(den_ready[l], 1)
                act.wait_ge(ml_em[l], 1)
                fn(M["rows"][0:4, 0, :], e0[0:4, 0:T], ACT.Abs).then_inc(den_abs[l], 1)

            def head_square(l, p):
                n = NORM_ORDER[p]
                act.wait_ge(o_free[l], n + 1)
                fn(osq[:, p, :], M["osb"][:, n, :], ACT.Square).then_inc(osq_ready[l], 1)

            def head_rstd(l):
                r = M["rows"][0:12, 0, :]
                wait_taken(act, TILE[l][("headsum",)])
                fn(r, r, ACT.Ln).then_inc(hlog_ready[l], 1)
                act.wait_ge(hlog_ready[l], 1)
                fn(r, r, ACT.Exp, scale=-0.5).then_inc(hrstd_ready[l], 1)

            def round_y(l, n):
                fn(yh[:, n, :], M["osb"][:, n, :], ACT.Copy).then_inc(yh_ready[l], 1)

            def y_plain(l):
                for n in range(2):
                    act.wait_ge(o_free[l], n + 1)
                    round_y(l, n)

            def y_rest(l, p):
                act.wait_ge(y_step[l], p + 1)
                round_y(l, NORM_ORDER[p])

            def load_tables(l, n):
                if l == 0:
                    c = [CONST_FIRST + (CONST_W - CONST_FIRST) * i // 3 for i in (n, n + 1)]
                    act.dma_start(const[:, c[0]:c[1]], consts[:, c[0]:c[1]]).then_inc(const_loaded, 16)

            def tables(name):
                return lambda l: nc.scalar.preload_act_table_set(name)

            parts = {
                "group": group, "logit": logit, "gate_sigmoid": gate_sigmoid, "gate": gate, "conv_silu": conv_silu,
                "gla_soft": gla_soft_, "ml_soft": ml_soft_, "gla_exp": gla_exp_, "ml_em": ml_em_, "take_out": take_out,
                "sb_soft0": sb_soft0, "sb_soft": sb_soft_, "sb_p": sb_p_, "sb_p0": sb_p0_, "ml_w0": ml_w0, "ml_w": ml_w_,
                "den_abs": den_abs_, "head_square": head_square, "head_rstd": head_rstd, "mo_sigmoid": mo_sigmoid, "y_plain": y_plain, "y_rest": y_rest,
                "load_tables": load_tables, "exp_tables": tables("natural_log_exp_and_others"), "silu_tables": tables("silu_and_others"),
                "sigmoid_tables": tables("sigmoid_and_others"),
            }

            def branch(l):
                q0 = q_start(l)

                def round_merged(m):
                    act.wait_ge(*((merge_step[l], m + 1) if m < KT - 1 else (half_late[l], 2)))
                    fn(xh[:, m, q0:], acc[:, m % 2, q0:], ACT.Copy).then_inc(mh_ready[l], 1)

                for m in range(KT - 1):
                    if m:
                        round_merged(m - 1)
                    round_half(2 * G_BRANCH[l] + m + ROUND_AHEAD)
                round_merged(KT - 2)
                round_merged(KT - 1)

            def take_sublayer(l, n, t, m, q0, i=0, step=0):
                wait_tile(act, t, i, step)
                k = ds(i * step + m, 1) if step else slice(m, m + 1)
                ps = ring[t % 2][:, 0:T - q0]
                fn(sq[:, k, q0:], ps, ACT.Square).then_inc(sq_ready[l][n], 1)
                taken(fn(sub[:, k, q0:], ps, ACT.Copy), t)

            def output(l):
                q0, t = q_start(l), TILE[l]["out"]
                with act.Fori(0, KT // 4) as i:
                    for m in range(4):
                        round_half(2 * G_OUT[l] + m - 1 + ROUND_AHEAD, i, 4)
                        take_sublayer(l, 1, t + m, m, q0, i, 4)

            def gate_up(l):
                q0, n, t = q_start(l), 2 * G_GU[l] + ROUND_AHEAD, TILE[l]["gu"]
                with act.Fori(0, NGU // 2) as i:
                    for c in range(2):
                        wait_taken(act, t + c, i, 4)
                        v = silu_g[:, c, q0:]
                        fn(v, v, ACT.Silu).then_inc(silu_ready[l], 1)
                        round_half(n + c, i, 4)
                    for c in range(2):
                        wait_taken(act, t + 2 + c, i, 4)
                        fn(ah[:, ds(i * 2 + c, 1), q0:], prod[:, c, q0:], ACT.Copy).then_inc(ah_ready[l], 1)
                        round_half(n + 2 + c, i, 4)

            def down(l):
                q0, g, t = q_start(l), G_DOWN[l], TILE[l]["down"]
                for j in range(NDOWN):
                    for c in range(2):
                        if j % 3 == 2:
                            m = 2 * (j // 3) + c
                            take_sublayer(l, 3, t + m, m, q0)
                        if 2 * j + c < 2 * NDOWN - 1:
                            round_half(2 * (g + j) + c + ROUND_AHEAD)

            act.dma_start(const[:, 0:CONST_FIRST], consts[:, 0:CONST_FIRST]).then_inc(first_loaded, 16)
            load_rows(act, PARAM_ROWS[0:4], par_loaded)
            exp_tables = tables("natural_log_exp_and_others")
            exp_tables(0)
            act.wait_ge(first_loaded, 16)
            for l in range(DEPTH):
                q0 = q_start(l)
                for k in range(KT):
                    square_h(l, 0, k, 0)
                for n in ([2 * G_MIX[l] - 1 + ROUND_AHEAD] if l else [0, 1]):
                    round_half(n)
                root(l, 0, 0)
                round_x(l)
                if l == 0:
                    for n in range(2, ROUND_AHEAD):
                        round_half(n)
                    act.wait_ge(bias_loaded, 48)
                run_steps(l, parts)
                branch(l)
                exp_tables(l)
                output(l)
                round_half(2 * G_GU[l] - 1 + ROUND_AHEAD)
                root(l, 1, q0)
                round_ffn_x(l, q0)
                root(l, 2, q0)
                tables("silu_and_others")(l)
                gate_up(l)
                exp_tables(l)
                down(l)
                root(l, 3, q0)
            for n, ps in enumerate((sc[0], sc[1], ex, k0)):
                half, b = n // 2, n % 2
                wait_tile(act, TILE_OUT + n)
                fn(otok[:, b, 512 * half:512 * half + 512], ps, ACT.Copy).then_inc(out_rows, 1)

        @block.vector
        def _(dve):
            tt, ts, stt = nc.vector.tensor_tensor, nc.vector.tensor_scalar, nc.vector.scalar_tensor_tensor
            scan = nc.vector.tensor_tensor_scan

            def rest_of_half(n, i=0, step=0):
                if n >= 2 * G_END:
                    return
                g, c, k = n // 2, n % 2 * P, group_k(n // 2)
                dve.wait_ge(hi_ready, n + 1 + i * step)
                tt(lo[g % 2][:, 0:k, c:c + P], raw[g % 2][:, 0:k, c:c + P], hi[g % 2][:, 0:k, c:c + P].bitcast(F32), ALU.subtract).then_inc(lo_ready, 1)

            def taken(ins, t):
                ins.then_inc(bank_free[t % 2], 1)

            def pre_norm(l):
                dve.wait_ge(rstd_ready[l], RSTD_COUNT[0])
                for k in range(KT):
                    stt(sq[:, k, :], hT[:, k, :], par[:, l, R_MIXPRE + k:R_MIXPRE + k + 1], rstd[:], ALU.mult, ALU.mult).then_inc(xn_ready[l], 1)
                for k in range(X_POOL, KT):
                    dve.wait_ge(xh_ready[l], k + 1)
                    tt(xl[:, k, :], sq[:, k, :], xh[:, k, :].bitcast(F32), ALU.subtract).then_inc(xl_late[l], 1)

            def post_norm(l, n, q0, row, behind=None):
                dve.wait_ge(rstd_ready[l], RSTD_COUNT[n])
                for k in range(KT):
                    stt(sub[:, k, q0:], sub[:, k, q0:], par[:, l, row + k:row + k + 1], rstd[:, q0:], ALU.mult, ALU.mult).then_inc(post_scaled[l], 1)
                    if behind and k >= 3:
                        behind(k - 3)
                if behind:
                    for k in range(KT - 3, KT):
                        behind(k)
                if n == 3:
                    for k in range(H_POOL, KT):
                        dve.wait_ge(post_scaled[l], KT + k + 1)
                        tt(hT[:, k, q0:], hT[:, k, q0:], sub[:, k, q0:], ALU.add).then_inc(h_late[l], 1)

            def rest_of_ffn_x(l, q0):
                def tile(k):
                    dve.wait_ge(xh_ready[l], KT + k + 1)
                    stt(xl[:, k, q0:], hT[:, k, q0:], par[:, l, R_FFNPRE + k:R_FFNPRE + k + 1], xh[:, k, q0:].bitcast(F32),
                        ALU.mult, ALU.subtract).then_inc(xl_ffn_ready[l], 1)
                return tile

            def group(l, name):
                g, t, kind = G_MIX[l] + MIX_NO[name], group_tile(l, name), KIND[name]
                if name == "small":
                    nc.vector.memset(M["conv_in"][:, :, 0:3], 0.0).then_inc(pad_set[l], 1)
                rest_of_half(2 * g + REST_AHEAD)
                if kind != "v":
                    rest_of_half(2 * g + REST_AHEAD + 1)
                    return
                mix = V_OF[name]
                wait_tile(dve, t)
                for h in range(HEADS):
                    ins = nc.vector.tensor_copy(M["v0"][quad_real[h], mix, :], ring[t % 2][0:META, h * HD:h * HD + HD])
                taken(ins, t)
                for b in range(2):
                    wait_tile(dve, t + 1 + b)
                    taken(nc.vector.tensor_copy(M["v"][:, b, mix, :], ring[(t + 1 + b) % 2][:, 0:256]), t + 1 + b)

            def rest(l, name):
                rest_of_half(2 * (G_MIX[l] + MIX_NO[name]) + REST_AHEAD + 1)

            def logit(l, j):
                rest_of_half(2 * G_LOGIT[l] + j + REST_AHEAD)

            def rot(l, i):
                name = ("rq", "rk")[i // 2]
                v = M[name][:, i % 2, :]
                turned = M["sa"][:, i % 2, 0:T]
                dve.wait_ge(const_loaded, 48)
                dve.wait_ge(rot_ready[l], i + 1)
                tt(turned, rot_banks[i % 2][:, 0:T], cut["sin"], ALU.mult).then_inc(rot_free[l], 1)
                tt(v, v, cut["cos"], ALU.mult).then_inc(rot_cos[l], 1)
                dve.wait_ge(rot_free[l], i + 1)
                dve.wait_ge(rot_cos[l], i + 1)
                tt(v, v, turned, ALU.add).then_inc(rot_done[l], 1)

            def conv(l, j):
                if j == 0:
                    for name in ("mqk0", "mqk1"):
                        for c in range(2):
                            wait_taken(dve, group_tile(l, name) + c)
                    dve.wait_ge(pad_set[l], 1)
                for t in range(4):
                    tap = par[:, l, R_CONV + 4 * j + t:R_CONV + 4 * j + t + 1]
                    src = M["conv_in"][:, t, j:j + T]
                    if j == 0:
                        ts(M["mqk"][:, t, :], src, tap, None, ALU.mult).then_inc(conv_step[l], 1)
                    else:
                        dve.wait_ge(conv_step[l], 4 * (j - 1) + t + 1)
                        stt(M["mqk"][:, t, :], src, tap, M["mqk"][:, t, :], ALU.mult, ALU.add).then_inc(conv_step[l], 1)

            def gla_log(l):
                dve.wait_ge(gla_soft[l], 3)
                stt(M["gwork"][:], M["gwork"][:], 0.0, M["gwork2"][:], ALU.min, ALU.subtract).then_inc(gla_dve[l], 1)
                dve.wait_ge(gla_dve[l], 1)
                dve.wait_ge(sb_p0[l], 1)
                scan(M["cum"][:], ones[:], M["gwork"][:], 0.0, ALU.mult, ALU.add).then_inc(gla_dve[l], 1)
                dve.wait_ge(gla_dve[l], 2)
                for c, (at_, s) in enumerate(((KB1 - 1, -1), (KB2 - 1, -1), (KB1 - 1, 1), (KB2 - 1, 1))):
                    ts(glaref[:, c:c + 1], M["cum"][:, at_:at_ + 1], s / GLA_NORMALIZER, None, ALU.mult).then_inc(gla_dve[l], 1)

            def ml_rows(l):
                rows, small = M["rows"], M["small"]
                dve.wait_ge(ml_soft[l], 3)
                stt(rows[64:68, 1, :], small[64:68, :], 0.0, rows[64:68, 0, :], ALU.min, ALU.subtract).then_inc(ml_dve[l], 1)
                dve.wait_ge(ml_dve[l], 1)
                scan(rows[64:68, 2, :], ones[64:68, :], rows[64:68, 1, :], 0.0, ALU.mult, ALU.add).then_inc(ml_dve[l], 1)
                dve.wait_ge(ml_dve[l], 2)
                nc.vector.tensor_copy(rows[32:36, 0, :], rows[64:68, 2, :]).then_inc(ml_dve[l], 1)
                dve.wait_ge(ml_dve[l], 3)
                tt(rows[32:36, 1, :], small[32:36, :], rows[32:36, 0, :], ALU.subtract).then_inc(ml_dve[l], 1)
                dve.wait_ge(ml_dve[l], 4)
                scan(rows[32:36, 2, :], rows[32:36, 1, :], rows[32:36, 1, :], 0.0, ALU.max, ALU.max).then_inc(ml_dve[l], 1)
                dve.wait_ge(ml_dve[l], 5)
                nc.vector.tensor_copy(gl[0:4, :], rows[32:36, 1, :]).then_inc(ml_dve[l], 1)
                for h in range(HEADS):
                    ts(gr_rows[32:36, h, :], rows[32:36, 2, :], cut["negind"][32:36, h:h + 1], None, ALU.mult).then_inc(ml_dve[l], 1)
                tt(rows[32:36, 0, :], rows[32:36, 0, :], rows[32:36, 2, :], ALU.add).then_inc(ml_dve[l], 1)

            def gla_decay(l):
                for n, (dst, src, c) in enumerate(((M["qa"], M["gq"], KB1), (M["qb"], M["gq"], KB2), (M["q0"], M["gq"], 0),
                                                   (M["kr0"], M["gk"], 0), (M["kr1"], M["gk"], KB1), (M["k00"], M["gk"], 0))):
                    dve.wait_ge(gla_exp[l], n + 1)
                    tt(dst[:], dst[:], src[:, c:c + dst.shape[1]], ALU.mult).then_inc(gla_ops[l], 1)

            def wait_spent(l, mix, pair):
                dve.wait_ge(o_ready[l], 2 * (mix - 1) + pair + 1)

            def sb_keep_head(l, h):
                dve.wait_ge(sb_soft[l], 3 * (h + 2))
                stt(M["pt"][:, h, :], sc[h % 2][:, 0:SCW], 0.0, M["sb2"][:, h % 2, :], ALU.max, ALU.add).then_inc(sc_free[l], 1)
                dve.wait_ge(sc_free[l], h + 1)
                tt(M["pt"][:, h, :], M["pt"][:, h, :], cut["mask_lt"], ALU.mult).then_inc(sb_keep[l], 1)

            pt, pt0, sa = M["pt"], M["pt0"], M["sa"]

            def sb_keep0_(l):
                dve.wait_ge(sb_soft[l], 3)
                stt(pt0[:], k0[:, 0:T], 0.0, M["cum"][:], ALU.max, ALU.add).then_inc(k0_free[l], 1)
                dve.wait_ge(k0_free[l], 1)
                tt(pt0[:], pt0[:], cut["mask_lt0"], ALU.mult).then_inc(sb_keep0[l], 1)

            def sb_mask(l, h):
                dve.wait_ge(ex_ready[l], h + 1)
                if h >= 2:
                    dve.wait_ge(sb_p[l], h - 1)
                stt(sa[:, h % 2, :], ex[:, 0:SCW], 0.0, cut["neg_lt"], ALU.min, ALU.add).then_inc(ex_free[l], 1)

            def sb_mask0(l):
                dve.wait_ge(e0_ready[l], 1)
                stt(M["cum"][:], e0[:, 0:T], 0.0, cut["neg_lt0"], ALU.min, ALU.add).then_inc(e0_free[l], 1)

            def gla_p0(l):
                dve.wait_ge(k0_ready[l], GLA + 1)
                wait_spent(l, GLA, 1)
                tt(pt0[:], k0[:, 0:T], cut["mask_le0"], ALU.mult).then_inc(k0_free[l], 1)

            def gla_p(l, h):
                j = 4 * GLA + h
                dve.wait_ge(sc_ready[l], j + 1)
                wait_spent(l, GLA, h // 2)
                tt(pt[:, h, :], sc[j % 2][:, 0:SCW], cut["mask_le"], ALU.mult).then_inc(sc_free[l], 1)

            def ml_mask0(l):
                dve.wait_ge(e0_ready[l], 2)
                stt(M["gwork"][:], e0[:, 0:T], 0.0, cut["neg_le0"], ALU.min, ALU.add).then_inc(e0_free[l], 1)

            def ml_mask(l, h):
                dve.wait_ge(ex_ready[l], HEADS + h + 1)
                dve.wait_ge(sb_p[l], 4)
                if h >= 2:
                    dve.wait_ge(ml_w[l], h)
                stt(sa[:, h % 2, :], ex[:, 0:SCW], 0.0, cut["neg_le"], ALU.min, ALU.add).then_inc(ex_free[l], 1)

            def ml_p0(l):
                dve.wait_ge(k0_ready[l], ML + 1)
                dve.wait_ge(ml_w[l], 1)
                wait_spent(l, ML, 1)
                stt(pt0[:], k0[:, 0:T], ML_SCALE, M["gwork2"][:], ALU.mult, ALU.mult).then_inc(k0_free[l], 1)

            def ml_p(l, h):
                j = 4 * ML + h
                dve.wait_ge(sc_ready[l], j + 1)
                dve.wait_ge(ml_w[l], h + 2)
                wait_spent(l, ML, h // 2)
                stt(pt[:, h, :], sc[j % 2][:, 0:SCW], ML_SCALE, M["sb2"][:, h % 2, :], ALU.mult, ALU.mult).then_inc(sc_free[l], 1)

            def den_square(l):
                dve.wait_ge(den_abs[l], 1)
                tt(M["rows"][0:4, 2, :], M["rows"][0:4, 0, :], M["rows"][0:4, 1, :], ALU.max).then_inc(den_dve[l], 1)
                dve.wait_ge(den_dve[l], 1)
                tt(dm2[0:4, :], M["rows"][0:4, 2, :], M["rows"][0:4, 2, :], ALU.mult).then_inc(den_dve[l], 1)

            def ret_p0(l):
                wait_spent(l, RET, 1)
                dve.wait_ge(k0_ready[l], RET + 1)
                tt(pt0[:], k0[:, 0:T], cut["decay0"], ALU.mult).then_inc(k0_free[l], 1)

            def ret_p(l, h):
                j = 4 * RET + h
                dve.wait_ge(sc_ready[l], j + 1)
                wait_spent(l, RET, h // 2)
                tt(pt[:, h, :], sc[j % 2][:, 0:SCW], c3("decay", 4)[:, h, :], ALU.mult).then_inc(sc_free[l], 1)

            def head_var(l):
                t = TILE[l][("headsum",)]
                wait_tile(dve, t)
                dve.wait_ge(den_dve[l], 2)
                taken(stt(M["rows"][0:12, 0, :], dm2[:], EPS, ring[t % 2][0:12, 0:T], ALU.mult, ALU.add), t)

            def rest_of_y(l, i, n):
                dve.wait_ge(yh_ready[l], i + 1)
                tt(yl[:, n, :], M["osb"][:, n, :], yh[:, n, :].bitcast(F32), ALU.subtract).then_inc(yl_ready[l], 1)

            def y_plain(l):
                rest_of_y(l, 0, 0)
                rest_of_y(l, 1, 1)

            def y_rest(l, p):
                osb, n = M["osb"], NORM_ORDER[p]
                row, gate = {GLA: (R_GLAN, "gr"), ML: (R_MLN, "mo"), RET: (R_RETN, "rg")}[n // 2]
                dve.wait_ge(spread_ready[l], p + 1)
                stt(osb[:, n, :], osb[:, n, :], par[:, l, row + n % 2:row + n % 2 + 1], spread_banks[p % 2][:, 0:T],
                    ALU.mult, ALU.mult).then_inc(spread_free[l], 1)
                dve.wait_ge(spread_free[l], p + 1)
                if gate == "mo":
                    dve.wait_ge(mo_ready[l], 1)
                tt(osb[:, n, :], osb[:, n, :], M[gate][:, n % 2, :], ALU.mult).then_inc(y_step[l], 1)
                rest_of_y(l, p + 2, n)

            parts = {
                "group": group, "rest": rest, "logit": logit, "rot": rot, "conv": conv, "gla_log": gla_log, "gla_decay": gla_decay,
                "ml_rows": ml_rows, "sb_keep0": sb_keep0_, "sb_keep": sb_keep_head, "sb_mask": sb_mask, "sb_mask0": sb_mask0,
                "gla_p0": gla_p0, "gla_p": gla_p, "ml_mask0": ml_mask0, "ml_mask": ml_mask, "ml_p0": ml_p0, "ml_p": ml_p,
                "den_square": den_square, "ret_p0": ret_p0, "ret_p": ret_p, "head_var": head_var,
                "y_plain": y_plain, "y_rest": y_rest,
            }

            def branch(l):
                q0 = q_start(l)
                dve.wait_ge(gates_ready[l], SIGMOID_FROM // 4)
                for b in range(2):
                    wait_taken(dve, TILE[l][("logit", 2 * NLOGIT - 1 - b)])

                def rest_of_merged(m):
                    dve.wait_ge(mh_ready[l], m + 1)
                    tt(xl[:, m, q0:], acc[:, m % 2, q0:], xh[:, m, q0:].bitcast(F32), ALU.subtract).then_inc(ml_ready[l], 1)

                by_branch = gates[:].rearrange("p (n m) t -> p n m t", n=4)
                for m in range(KT):
                    dve.wait_ge(half_used, 2 * G_BRANCH[l] + m + 1)
                    if m >= 2:
                        dve.wait_ge(merge_step[l], m - 1)
                    tt(term[:, m % 2, :, q0:], branch_banks[m % 2][:, :, 0:T - q0], by_branch[:, :, m, q0:], ALU.mult).then_inc(branch_free[l], 1)
                    if m == KT - 1:
                        last = term[:, m % 2, :, q0:]
                        dve.wait_ge(branch_free[l], KT)
                        tt(last[:, 0:2, :], last[:, 0:2, :], last[:, 2:4, :], ALU.add).then_inc(half_late[l], 1)
                        rest_of_merged(m - 2)
                        dve.wait_ge(half_late[l], 1)
                        dve.wait_ge(ml_ready[l], KT - 2)
                        tt(acc[:, m % 2, q0:], last[:, 0, :], last[:, 1, :], ALU.add).then_inc(half_late[l], 1)
                    else:
                        rest_of_half(2 * G_BRANCH[l] + m + REST_AHEAD)
                    if m and m != KT - 2:
                        rest_of_merged(m - 1)
                rest_of_merged(KT - 1)
                rest_of_half(2 * G_BRANCH[l] + KT - 1 + REST_AHEAD)

            def output(l):
                with dve.Fori(0, KT // 4) as i:
                    for m in range(4):
                        rest_of_half(2 * G_OUT[l] + m + REST_AHEAD, i, 4)

            def gate_up(l):
                q0, n, t = q_start(l), 2 * G_GU[l] + REST_AHEAD, TILE[l]["gu"]
                dve.wait_ge(rstd_ready[l], RSTD_COUNT[2])
                with dve.Fori(0, NGU // 2) as i:
                    for c in range(2):
                        wait_tile(dve, t + c, i, 4)
                        dve.wait_ge(bank_free[(t + c) % 2], (t + c) // 2 + i * 2)
                        taken(tt(silu_g[:, c, q0:], ring[(t + c) % 2][:, 0:T - q0], rstd[:, q0:], ALU.mult), t + c)
                        rest_of_half(n + c, i, 4)
                    for c in range(2):
                        wait_tile(dve, t + 2 + c, i, 4)
                        dve.wait_ge(silu_scaled[l], c + 1 + i * 2)
                        taken(tt(prod[:, c, q0:], ring[(t + c) % 2][:, 0:T - q0], silu_g[:, c, q0:], ALU.mult), t + 2 + c)
                        rest_of_half(n + 2 + c, i, 4)
                        dve.wait_ge(ah_ready[l], c + 1 + i * 2)
                        tt(al[:, ds(i * 2 + c, 1), q0:], prod[:, c:c + 1, q0:], ah[:, ds(i * 2 + c, 1), q0:].bitcast(F32), ALU.subtract).then_inc(al_ready[l], 1)

            def down(l):
                for j in range(2 * NDOWN):
                    rest_of_half(2 * G_DOWN[l] + j + REST_AHEAD)

            nc.vector.memset(ifbias[:], 0.0).then_inc(misc_set, 1)
            nc.vector.memset(ones[:], 1.0).then_inc(misc_set, 1)
            nc.vector.memset(dm2[:], 1.0).then_inc(misc_set, 1)
            nc.vector.memset(gl[:], 0.0).then_inc(misc_set, 1)
            nc.vector.memset(gr_rows[:], 0.0).then_inc(misc_set, 1)
            dve.wait_ge(misc_set, 5)
            nc.vector.memset(gl[32:36, :], 1.0).then_inc(misc_set, 1)
            dve.wait_ge(first_loaded, 16)
            for h in range(HEADS):
                ts(gr_rows[0:4, h, :], ones[0:4, :], cut["ident"][0:4, h:h + 1], None, ALU.mult).then_inc(misc_set, 1)
            def sum_first(k):
                dve.wait_ge(sq_ready[0][0], k + 1)
                if k > 1:
                    dve.wait_ge(sq_first, k - 1)
                tt(sq[:, 0, :], sq[:, 0, :], sq[:, k, :], ALU.add).then_inc(sq_first, 1)

            for k in range(KT):
                wait_tile(dve, k)
                taken(nc.vector.tensor_copy(hT[:, k, :], ring[k % 2][:, 0:T]), k)
                if k >= 3:
                    sum_first(k - 2)
            for k in range(KT - 2, KT):
                sum_first(k)
            for l in range(DEPTH):
                t = KT + l
                wait_tile(dve, t)
                taken(nc.vector.tensor_copy(par[:, l, :], ring[t % 2][:, 0:NPAR]), t)
            for l in range(DEPTH):
                wait_taken(dve, KT + l)
            rest_of_half(0)
            rest_of_half(1)
            for l in range(DEPTH):
                q0 = q_start(l)
                pre_norm(l)
                if l == 0:
                    for n in range(2, REST_AHEAD):
                        rest_of_half(n)
                run_steps(l, parts)
                branch(l)
                output(l)
                post_norm(l, 1, q0, R_MIXPOST, rest_of_ffn_x(l, q0))
                gate_up(l)
                down(l)
                post_norm(l, 3, q0, R_FFNPOST)

        @block.gpsimd
        def _(pool):
            tt = nc.gpsimd.tensor_tensor

            def rest_of_x(l):
                for k in range(X_POOL):
                    pool.wait_ge(xh_ready[l], k + 1)
                    tt(xl[:, k, :], sq[:, k, :], xh[:, k, :].bitcast(F32), ALU.subtract).then_inc(xl_ready[l], 1)

            def sum_squares(l, n, q0):
                for k in range(1, KT - 1):
                    pool.wait_ge(sq_ready[l][n], k + 1)
                    if k > 1:
                        pool.wait_ge(sq_summed[l], n // 2 * (KT - 2) + k - 1)
                    elif n == 3:
                        pool.wait_ge(sq_summed[l], KT - 2)
                    tt(sq[:, 0, q0:], sq[:, 0, q0:], sq[:, k, q0:], ALU.add).then_inc(sq_summed[l], 1)

            def scale_silu(l, q0):
                with pool.Fori(0, NGU // 2) as i:
                    for c in range(2):
                        pool.wait_ge(silu_ready[l], c + 1 + i * 2)
                        v = silu_g[:, c, q0:]
                        tt(v, v, rstd[:, q0:], ALU.mult).then_inc(silu_scaled[l], 1)

            def merge(l):
                q0 = q_start(l)
                for m in range(KT - 1):
                    pool.wait_ge(branch_free[l], m + 1)
                    if m:
                        pool.wait_ge(merge_step[l], m)
                    tt(half[:, :, q0:], term[:, m % 2, 0:2, q0:], term[:, m % 2, 2:4, q0:], ALU.add).then_inc(half_ready[l], 1)
                    pool.wait_ge(half_ready[l], m + 1)
                    if m >= 2:
                        pool.wait_ge(ml_ready[l], m - 1)
                    tt(acc[:, m % 2, q0:], half[:, 0, q0:], half[:, 1, q0:], ALU.add).then_inc(merge_step[l], 1)

            def add_sublayer(l, n, q0):
                for k in range(H_POOL if n == 3 else KT):
                    pool.wait_ge(post_scaled[l], n // 2 * KT + k + 1)
                    tt(hT[:, k, q0:], hT[:, k, q0:], sub[:, k, q0:], ALU.add).then_inc(h_ready[l], 1)

            load_rows(pool, PARAM_ROWS[7:], par_late)
            pool.dma_start(wgate[:], gla_w_gate_up.rearrange("l r m -> r l m")).then_inc(bias_loaded, 16)
            pool.wait_ge(misc_set, 1)
            pool.dma_start(ifbias[32:36, :], ml_b_i.rearrange("l h -> h l"), allow_slow_non_contiguous=True).then_inc(bias_loaded, 16)
            pool.dma_start(ifbias[64:68, :], ml_b_f.rearrange("l h -> h l"), allow_slow_non_contiguous=True).then_inc(bias_loaded, 16)
            for l in range(DEPTH):
                q0 = q_start(l)
                rest_of_x(l)
                merge(l)
                sum_squares(l, 1, q0)
                add_sublayer(l, 1, q0)
                scale_silu(l, q0)
                sum_squares(l, 3, q0)
                add_sublayer(l, 3, q0)


_INS = ["x", "meta_tokens", "norm_mix_pre", "norm_mix_post", "norm_ffn_pre", "norm_ffn_post", "w_in", "gla_w_gate_up",
        "gla_b_gate", "gla_norm", "ml_conv", "ml_b_i", "ml_b_f", "ml_norm", "ret_norm", "w_branch", "b_merge", "w_out",
        "ffn_w_gate", "ffn_w_up", "ffn_w_down"]


def kernel(**inputs):
    import concourse.bacc as bacc
    from concourse.bass_utils import run_bass_kernel_spmd

    nc = bacc.Bacc("TRN2", target_bir_lowering=False, num_devices=1)
    arrays = {f"in_{n}": np.ascontiguousarray(inputs[n]) for n in _INS}
    arrays["in_consts"] = constants()
    args = [nc.dram_tensor(n, a.shape, mybir.dt.from_np(a.dtype), kind="ExternalInput").ap() for n, a in arrays.items()]
    out = nc.dram_tensor("out", (1, SEQ, D), F32, kind="ExternalOutput").ap()
    build(nc, *args, out)
    r = run_bass_kernel_spmd(nc, [arrays], core_ids=[0])
    return r.results[0]["out"]
```
